# Optimizing a Trainium2 kernel written in Bass

```python
import jax, jax.numpy as jnp
from jax import lax
import numpy as np

D_MODEL = 1024
BATCH = 1
SEQ = 1024
DEPTH = 1

HEAD_DIM = 64
N_META = 16
BLOCK = 128
PAD = BLOCK - N_META
FOX_HEADS = 8
SWA_HEADS = 8
SWA_KV_HEADS = 2
WINDOW = 128
N_EXPERTS = 32
TOP_K = 4
D_FF = 1024
SWIGLU_LIMIT = 7.0
SWIGLU_ALPHA = 1.702
RMS_EPS = 1e-6
NEG_INF = -1e30
MOE_BLOCK = 128

FOX_W = FOX_HEADS * HEAD_DIM
SWA_QW = SWA_HEADS * HEAD_DIM
SWA_KW = SWA_KV_HEADS * HEAD_DIM
SPLITS = [FOX_W, FOX_W, FOX_W, FOX_HEADS, SWA_QW, SWA_KW, SWA_KW, D_MODEL, D_MODEL]
IN_WIDTH = 3 * FOX_W + FOX_HEADS + SWA_QW + 2 * SWA_KW + 2 * D_MODEL

kernel_name = "hybrid_fox_swa_sink_moe_block"

def _rmsnorm(t, gain):
    tf = t.astype(jnp.float32)
    y = tf * lax.rsqrt(jnp.mean(tf * tf, axis=-1, keepdims=True) + RMS_EPS)
    return (y * gain.astype(jnp.float32)).astype(t.dtype)

def _pad_front(t):
    return jnp.pad(t, ((0, 0), (PAD, 0)) + ((0, 0),) * (t.ndim - 2))

def _fox_attention(q, k, v, log_f):
    B, Lp, H, d = q.shape
    nb = Lp // BLOCK
    F = jnp.cumsum(log_f, axis=1)
    FT = F.transpose(0, 2, 1)
    pos = jnp.arange(Lp)
    key_ok = pos >= PAD
    qb = q.reshape(B, nb, BLOCK, H, d).transpose(1, 0, 2, 3, 4)
    Fb = F.reshape(B, nb, BLOCK, H).transpose(1, 0, 3, 2)
    scale = HEAD_DIM ** -0.5

    def one_block(args):
        qi, Fi, i = args
        s = jnp.einsum('bqhd,bkhd->bhqk', qi, k, preferred_element_type=jnp.float32) * scale
        s = s + Fi[..., :, None] - FT[:, :, None, :]
        qpos = i * BLOCK + jnp.arange(BLOCK)
        mask = (pos[None, :] <= qpos[:, None]) & key_ok[None, :]
        s = jnp.where(mask[None, None], s, NEG_INF)
        p = jax.nn.softmax(s, axis=-1)
        return jnp.einsum('bhqk,bkhd->bqhd', p.astype(v.dtype), v)

    out = lax.map(one_block, (qb, Fb, jnp.arange(nb)))
    return out.transpose(1, 0, 2, 3, 4).reshape(B, Lp, H, d)

def _swa_attention(q, k, v, sinks, slopes):
    B, Lp, H, d = q.shape
    G = k.shape[2]
    R = H // G
    nb = Lp // BLOCK
    qb = q.reshape(B, nb, BLOCK, G, R, d)

    def with_prev(t):
        tb = t.reshape(B, nb, BLOCK, G, d)
        prev = jnp.pad(tb[:, :-1], ((0, 0), (1, 0), (0, 0), (0, 0), (0, 0)))
        return jnp.concatenate([prev, tb], axis=2)

    kk, vv = with_prev(k), with_prev(v)
    s = jnp.einsum('bnqgrd,bnkgd->bngrqk', qb, kk, preferred_element_type=jnp.float32) * (HEAD_DIM ** -0.5)
    blk = jnp.arange(nb)[:, None]
    qpos = blk * BLOCK + jnp.arange(BLOCK)[None, :]
    kpos = blk * BLOCK - BLOCK + jnp.arange(2 * BLOCK)[None, :]
    dist = qpos[:, :, None] - kpos[:, None, :]
    mask = (dist >= 0) & (dist < WINDOW) & (kpos[:, None, :] >= PAD)
    s = s - slopes.reshape(G, R)[None, None, :, :, None, None] * dist.astype(jnp.float32)[None, :, None, None]
    s = jnp.where(mask[None, :, None, None], s, NEG_INF)
    sink = jnp.broadcast_to(sinks.astype(jnp.float32).reshape(G, R)[None, None, :, :, None, None], s.shape[:-1] + (1,))
    p = jax.nn.softmax(jnp.concatenate([s, sink], axis=-1), axis=-1)[..., :-1]
    o = jnp.einsum('bngrqk,bnkgd->bnqgrd', p.astype(v.dtype), vv)
    return o.reshape(B, Lp, H, d)

def _moe(h, w_router, b_router, w_up, b_up, w_down, b_down):
    N, D = h.shape
    logits = jnp.matmul(h, w_router).astype(jnp.float32) + b_router.astype(jnp.float32)
    top_val, top_idx = lax.top_k(logits, TOP_K)
    gates = jax.nn.softmax(top_val, axis=-1)
    n_assign = N * TOP_K
    flat_e = top_idx.reshape(-1)
    flat_tok = jnp.arange(n_assign) // TOP_K
    order = jnp.argsort(flat_e)
    se, stok, sw = flat_e[order], flat_tok[order], gates.reshape(-1)[order]
    counts = jnp.bincount(flat_e, length=N_EXPERTS)
    padded = (counts + MOE_BLOCK - 1) // MOE_BLOCK * MOE_BLOCK
    pend = jnp.cumsum(padded)
    pstart = pend - padded
    start = jnp.cumsum(counts) - counts
    dest = pstart[se] + jnp.arange(n_assign) - start[se]
    n_blocks = -(-n_assign // MOE_BLOCK) + N_EXPERTS
    n_rows = n_blocks * MOE_BLOCK
    row_tok = jnp.zeros((n_rows,), jnp.int32).at[dest].set(stok)
    row_w = jnp.zeros((n_rows,), jnp.float32).at[dest].set(sw)
    block_e = jnp.minimum(jnp.searchsorted(pend, jnp.arange(n_blocks) * MOE_BLOCK, side='right'), N_EXPERTS - 1)
    xs = h[row_tok].reshape(n_blocks, MOE_BLOCK, D)

    def expert_block(args):
        xb, e = args
        gu = jnp.matmul(xb, w_up[e]) + b_up[e]
        g, u = gu[:, :D_FF], gu[:, D_FF:]
        g = jnp.minimum(g, SWIGLU_LIMIT)
        u = jnp.clip(u, -SWIGLU_LIMIT, SWIGLU_LIMIT)
        act = (u + 1.0) * (g * jax.nn.sigmoid(SWIGLU_ALPHA * g))
        return jnp.matmul(act, w_down[e]) + b_down[e]

    ys = lax.map(expert_block, (xs, block_e)).reshape(n_rows, D)
    return jnp.zeros_like(h).at[row_tok].add(ys * row_w[:, None].astype(ys.dtype))

def setup_inputs(seed: int = 0) -> dict:
    key = jax.random.key(seed)
    ks = jax.random.split(key, 20)
    f32 = jnp.float32
    nrm = lambda k, shape, scale: jax.random.normal(k, shape, f32) * scale
    return {
        "x": nrm(ks[0], (BATCH, SEQ, D_MODEL), 1.0),
        "meta_tokens": nrm(ks[1], (N_META, D_MODEL), 1.0),
        "norm1_gain": 1.0 + nrm(ks[2], (DEPTH, D_MODEL), 0.02),
        "w_in": nrm(ks[3], (DEPTH, D_MODEL, IN_WIDTH), D_MODEL ** -0.5),
        "b_forget": jax.random.uniform(ks[4], (DEPTH, FOX_HEADS), f32, 1.0, 4.0),
        "fox_q_gain": 1.0 + nrm(ks[5], (DEPTH, HEAD_DIM), 0.02),
        "fox_k_gain": 1.0 + nrm(ks[6], (DEPTH, HEAD_DIM), 0.02),
        "swa_q_gain": 1.0 + nrm(ks[7], (DEPTH, HEAD_DIM), 0.02),
        "swa_k_gain": 1.0 + nrm(ks[8], (DEPTH, HEAD_DIM), 0.02),
        "swa_sinks": nrm(ks[9], (DEPTH, SWA_HEADS), 0.5),
        "w_fox_out": nrm(ks[10], (DEPTH, FOX_W, D_MODEL), FOX_W ** -0.5),
        "w_swa_out": nrm(ks[11], (DEPTH, SWA_QW, D_MODEL), SWA_QW ** -0.5),
        "w_out": nrm(ks[12], (DEPTH, D_MODEL, D_MODEL), D_MODEL ** -0.5),
        "norm2_gain": 1.0 + nrm(ks[13], (DEPTH, D_MODEL), 0.02),
        "w_router": nrm(ks[14], (DEPTH, D_MODEL, N_EXPERTS), D_MODEL ** -0.5),
        "b_router": nrm(ks[15], (DEPTH, N_EXPERTS), 0.01),
        "w_up": nrm(ks[16], (DEPTH, N_EXPERTS, D_MODEL, 2 * D_FF), D_MODEL ** -0.5),
        "b_up": nrm(ks[17], (DEPTH, N_EXPERTS, 2 * D_FF), 0.01),
        "w_down": nrm(ks[18], (DEPTH, N_EXPERTS, D_FF, D_MODEL), D_FF ** -0.5),
        "b_down": nrm(ks[19], (DEPTH, N_EXPERTS, D_MODEL), 0.01),
    }

def reference(x, meta_tokens, norm1_gain, w_in, b_forget, fox_q_gain, fox_k_gain, swa_q_gain, swa_k_gain, swa_sinks, w_fox_out, w_swa_out, w_out, norm2_gain, w_router, b_router, w_up, b_up, w_down, b_down):
    B = x.shape[0]
    meta = jnp.broadcast_to(meta_tokens[None].astype(x.dtype), (B, N_META, D_MODEL))
    hres = jnp.concatenate([meta, x], axis=1)
    L = hres.shape[1]
    slopes = jnp.exp2(-8.0 * (jnp.arange(SWA_HEADS, dtype=jnp.float32) + 1.0) / SWA_HEADS)
    cuts = np.cumsum(SPLITS)[:-1].tolist()

    def head_rms(t, n_heads, gain):
        return _rmsnorm(t.reshape(B, L, n_heads, HEAD_DIM), gain)

    for l in range(DEPTH):
        h = _rmsnorm(hres, norm1_gain[l])
        proj = jnp.matmul(h, w_in[l])
        fq, fk, fv, flog, sq, sk, sv, ga, gb = jnp.split(proj, cuts, axis=-1)
        fq = head_rms(fq, FOX_HEADS, fox_q_gain[l])
        fk = head_rms(fk, FOX_HEADS, fox_k_gain[l])
        fv = fv.reshape(B, L, FOX_HEADS, HEAD_DIM)
        log_f = jax.nn.log_sigmoid(flog.astype(jnp.float32) + b_forget[l].astype(jnp.float32))
        sq = head_rms(sq, SWA_HEADS, swa_q_gain[l])
        sk = head_rms(sk, SWA_KV_HEADS, swa_k_gain[l])
        sv = sv.reshape(B, L, SWA_KV_HEADS, HEAD_DIM)

        o_a = _fox_attention(_pad_front(fq), _pad_front(fk), _pad_front(fv), _pad_front(log_f))
        o_a = o_a[:, PAD:].reshape(B, L, FOX_W)
        o_b = _swa_attention(_pad_front(sq), _pad_front(sk), _pad_front(sv), swa_sinks[l], slopes)
        o_b = o_b[:, PAD:].reshape(B, L, SWA_QW)

        mix = jax.nn.sigmoid(ga) * jnp.matmul(o_a, w_fox_out[l]) + jax.nn.sigmoid(gb) * jnp.matmul(o_b, w_swa_out[l])
        hres = hres + jnp.matmul(mix, w_out[l])

        h2 = _rmsnorm(hres, norm2_gain[l]).reshape(B * L, D_MODEL)
        hres = hres + _moe(h2, w_router[l], b_router[l], w_up[l], b_up[l], w_down[l], b_down[l]).reshape(B, L, D_MODEL)

    return hres[:, N_META:]


_drawn_inputs = setup_inputs


def setup_inputs(seed=0):
    import zlib

    import numpy as np

    out = dict(_drawn_inputs(seed))
    spreads = {}
    factors = {'fox_q_gain': 3.553,
     'fox_k_gain': 3.625,
     'swa_q_gain': 4.967,
     'swa_k_gain': 4.002,
     'b_router': 2.894,
     'b_up': 8.0,
     'b_down': 8.0,
     'swa_sinks': 64.0}
    for name, (base, spread) in spreads.items():
        noise = np.random.default_rng([zlib.crc32(name.encode()), seed]).standard_normal(out[name].shape)
        drawn = base * np.exp(spread * noise) if base else spread * noise
        out[name] = __import__('jax').numpy.asarray(drawn.astype(out[name].dtype))
    for name, factor in factors.items():
        out[name] = (out[name] * factor).astype(out[name].dtype)
    return out
```

```python
import numpy as np
import concourse.bass as bass
from concourse import mybir
from concourse.alu_op_type import AluOpType as ALU
from contextlib import ExitStack

P = 128
D = 1024
T = 1024
NM = 16
TT = T // P
KT = D // P
HD = 64
FH, SH, KVH = 8, 8, 2
FW, SW, KW = FH * HD, SH * HD, KVH * HD
WINDOW = 128
E = 32
TOPK = 4
FF = 1024
LIMIT, ALPHA, EPS, NEG = 7.0, 1.702, 1e-6, -1e30
C_FQ, C_FK, C_FV, C_FL = 0, FW, 2 * FW, 3 * FW
C_SQ = C_FL + FH
C_SK, C_SV = C_SQ + SW, C_SQ + SW + KW
C_GA = C_SV + KW
C_GB = C_GA + D
NC = 512
HK = 4
RING = 4
LEAD = 3
LO_DVE = 3
AUG = HD + 2
PAIR = 2 * P
MAX_ITEMS = E + T * TOPK // PAIR
NJ = MAX_ITEMS + 2
SCALE = HD ** -0.5


def constants():
    p = np.arange(P)[:, None]
    f = np.arange(P)[None, :]
    ident = (p == f).astype(np.float32)
    causal = np.where(f <= p, 0.0, NEG).astype(np.float32)
    tri_incl = (p <= f).astype(np.float32)
    tri_strict = (p < f).astype(np.float32)
    ones = np.ones((P, P), np.float32)
    tok = (np.arange(TT)[None, :] * P + p).astype(np.float32)
    iota_e = np.broadcast_to(np.arange(E, dtype=np.float32), (P, E))
    cst = np.concatenate([ident, causal, tri_incl, tri_strict, ones, tok, iota_e], 1)

    def neg_dist(key_pos):
        dist = (NM + P + p) - key_pos
        return np.where((dist >= 0) & (dist < WINDOW), -dist, -1e34).astype(np.float32)

    near = neg_dist(NM + np.arange(2 * P)[None, :])
    first = np.concatenate([neg_dist(NM + P + np.arange(P)[None, :]), neg_dist(P + np.arange(NM)[None, :])], 1)
    dist = np.concatenate([near, first], 1)
    slots = np.broadcast_to(np.arange(T, dtype=np.float32), (P, T))
    items = np.broadcast_to(np.arange(NJ, dtype=np.float32), (1, NJ))
    return [np.ascontiguousarray(a, dtype=np.float32) for a in (cst, dist, slots, items)]


CONST_SHAPES = [(P, 5 * P + TT + E), (P, 3 * P + NM), (P, T), (1, NJ)]


def block_kernel(nc, x, meta_tokens, norm1_gain, w_in, b_forget, fox_q_gain, fox_k_gain, swa_q_gain,
                 swa_k_gain, swa_sinks, w_fox_out, w_swa_out, w_out, norm2_gain, w_router, b_router,
                 w_up, b_up, w_down, b_down, c_cst, c_dist, c_slots, c_items, out):
    f32, f32r, i32, u32 = mybir.dt.float32, mybir.dt.float32r, mybir.dt.int32, mybir.dt.uint32
    ACT = mybir.ActivationFunctionType
    AX = mybir.AxisListType

    x2 = x.rearrange("b s d -> (b s) d")
    out2 = out.rearrange("b s d -> (b s) d")
    win = w_in.rearrange("l d n -> (l d) n")
    wfo = w_fox_out.rearrange("l d n -> (l d) n")
    wso = w_swa_out.rearrange("l d n -> (l d) n")
    wout = w_out.rearrange("l d n -> (l d) n")
    wrt = w_router.rearrange("l d n -> (l d) n")
    wup = w_up.rearrange("l e d n -> (l e d) n")
    wdn = w_down.rearrange("l e d n -> (l e d) n")
    bup = b_up.rearrange("l e n -> (l e) n")
    bdn = b_down.rearrange("l e n -> (l e) n")

    def row(a):
        return a.rearrange("l n -> (l n)").partition_broadcast(P)

    fqT_d = nc.dram_tensor("fqT_d", (AUG, FH, T), f32, kind="Internal").ap()
    fkT_d = nc.dram_tensor("fkT_d", (AUG, FH, T + NM), f32, kind="Internal").ap()
    sqT_d = nc.dram_tensor("sqT_d", (P, SH // 2, T), f32, kind="Internal").ap()
    skT_d = nc.dram_tensor("skT_d", (P, KVH, T + NM), f32, kind="Internal").ap()
    v_d = nc.dram_tensor("v_d", (P, TT + 1, FW + KW), f32, kind="Internal").ap()
    gate_d = nc.dram_tensor("gate_d", (P, TT, 2 * D), f32, kind="Internal").ap()
    h2_d = nc.dram_tensor("h2_d", (T, D), f32, kind="Internal").ap()

    ctx = ExitStack()
    with ctx:
        def sb(stack, name, shape, dt=f32):
            return stack.enter_context(nc.sbuf_tensor(name, shape, dt))

        def sem(name):
            return ctx.enter_context(nc.semaphore(name))

        psum = ctx.enter_context(nc.psum_tensor("psum", [P, 8, NC], f32))

        def bank(b):
            return psum[:, b, :]

        raw = [sb(ctx, f"raw{i}", [P, HK, NC]) for i in range(RING)]
        whi = [sb(ctx, f"whi{i}", [P, HK, NC], f32r) for i in range(RING)]
        wlo = [sb(ctx, f"wlo{i}", [P, HK, NC], f32r) for i in range(RING)]
        cst = sb(ctx, "cst", list(CONST_SHAPES[0]))
        ident, causal, tri_incl, tri_strict, ones = (cst[:, i * P:(i + 1) * P] for i in range(5))
        tok_index = cst[:, 5 * P:5 * P + TT]
        iota_e = cst[:, 5 * P + TT:5 * P + TT + E]
        slot_of = sb(ctx, "slot_of", [P, E, TT])
        tok_gate = sb(ctx, "tok_gate", [P, E, TT, 2])
        table = sb(ctx, "table", [1, 6, NJ], i32)

        s_raw = [sem(f"s_raw{i}") for i in range(RING)]
        s_hi = sem("s_hi")
        s_lo = sem("s_lo")
        s_lo_pool = sem("s_lo_pool")
        s_used = sem("s_used")
        s_const = sem("s_const")
        s_mm = sem("s_mm")
        s_tr = sem("s_tr")
        s_tr_act = sem("s_tr_act")
        s_tr_dve = sem("s_tr_dve")

        SMALL = FH + 2 * KW
        subs = []

        def chunk_subs(w, rows, cols):
            first = len(subs)
            for r0 in range(0, rows, HK * P):
                subs.append([(w[r0:r0 + HK * P, c:c + n].rearrange("(k p) n -> p k n", p=P), at, n)
                             for c, n, at in cols])
            return first, len(subs) - first, sum(n for _, n, _ in cols)

        proj = [("small", chunk_subs(win, D, [(C_FL, FH, 0), (C_SK, 2 * KW, FH)]))]
        for name, c in (("fk", C_FK), ("fq", C_FQ), ("fv", C_FV), ("sq", C_SQ)):
            proj.append((name, chunk_subs(win, D, [(c, NC, 0)])))
        for i in range(2 * D // NC):
            proj.append((f"g{i}", chunk_subs(win, D, [(C_GA + i * NC, NC, 0)])))
        N_PROJ = len(subs)
        outs = []
        for half in range(D // NC):
            for name, w in (("fox", wfo), ("swa", wso)):
                outs.append((name, half, chunk_subs(w, FW, [(half * NC, NC, 0)])))
        for half in range(D // NC):
            outs.append(("res", half, chunk_subs(wout, D, [(half * NC, NC, 0)])))
        N0 = len(subs)

        dma_count = [0] * RING
        raw_done = []
        for n, parts in enumerate(subs):
            dma_count[n % RING] += 16 * len(parts)
            raw_done.append(dma_count[n % RING])
        raw_base = list(dma_count)

        def load_sub(sp, n):
            if n >= RING:
                sp.wait_ge(s_lo, n - RING + 1)
                sp.wait_ge(s_lo_pool, n - RING + 1)
            for src, at, w in subs[n]:
                sp.dma_start(raw[n % RING][:, :, at:at + w], src).then_inc(s_raw[n % RING], 16)

        def sub_width(n):
            return sum(w for _, _, w in subs[n])

        def split_hi(act, n):
            act.wait_ge(s_raw[n % RING], raw_done[n])
            if n >= RING:
                act.wait_ge(s_used, n - RING + 1)
            w = sub_width(n)
            act.activation(whi[n % RING][:, :, 0:w], raw[n % RING][:, :, 0:w], ACT.Copy).then_inc(s_hi, 1)

        def split_lo(dve, n):
            dve.wait_ge(s_hi, n + 1)
            w = sub_width(n)
            dve.tensor_tensor(wlo[n % RING][:, 0:LO_DVE, 0:w], raw[n % RING][:, 0:LO_DVE, 0:w],
                              whi[n % RING][:, 0:LO_DVE, 0:w].bitcast(f32), ALU.subtract).then_inc(s_lo, 1)

        def split_lo_pool(pool, n):
            pool.wait_ge(s_hi, n + 1)
            w = sub_width(n)
            pool.tensor_tensor(wlo[n % RING][:, LO_DVE:HK, 0:w], raw[n % RING][:, LO_DVE:HK, 0:w],
                               whi[n % RING][:, LO_DVE:HK, 0:w].bitcast(f32), ALU.subtract).then_inc(s_lo_pool, 1)

        SUBS = 12
        splits_after = {k: [N_PROJ + RING + k - 1] if 1 <= k <= 4 else [] for k in range(6)}

        CHUNK_HALF = [(m // 2, m % 2) for m in range(8)] + [(4, 0), (5, 0), (4, 1), (5, 1)]

        def expert_source(e, m):
            chunk, half = CHUNK_HALF[m]
            w, c = (wup, (chunk % 2) * FF + (chunk // 2) * NC) if chunk < 4 else (wdn, (chunk - 4) * NC)
            rows = bass.ds(e * D + half * HK * P, HK * P)
            return w[rows, c:c + NC].rearrange("(k p) n -> p k n", p=P)

        def slot(m):
            return (N0 + m) % RING

        def raw_ready(m, j=0):
            return raw_base[slot(m)] + 16 * (m // RING + 1) + j * (16 * (SUBS // RING))

        def load_expert_sub(sp, n, e, m):
            sp.wait_ge(s_lo, n - RING + 1)
            sp.wait_ge(s_lo_pool, n - RING + 1)
            sp.dma_start(raw[slot(m)][:, :, :], expert_source(e, m)).then_inc(s_raw[slot(m)], 16)

        def expert_hi(act, n, m, j=0):
            act.wait_ge(s_raw[slot(m)], raw_ready(m, j))
            act.wait_ge(s_used, n - RING + 1)
            act.activation(whi[slot(m)][:, :, :], raw[slot(m)][:, :, :], ACT.Copy).then_inc(s_hi, 1)

        def expert_lo(dve, n, m):
            dve.wait_ge(s_hi, n + 1)
            dve.tensor_tensor(wlo[slot(m)][:, 0:LO_DVE, :], raw[slot(m)][:, 0:LO_DVE, :],
                              whi[slot(m)][:, 0:LO_DVE, :].bitcast(f32), ALU.subtract).then_inc(s_lo, 1)

        def expert_lo_pool(pool, n, m):
            pool.wait_ge(s_hi, n + 1)
            pool.tensor_tensor(wlo[slot(m)][:, LO_DVE:HK, :], raw[slot(m)][:, LO_DVE:HK, :],
                               whi[slot(m)][:, LO_DVE:HK, :].bitcast(f32), ALU.subtract).then_inc(s_lo_pool, 1)

        def three_passes(pe, dst, x_hi, x_lo, w_hi, w_lo, first, last):
            pe.matmul(dst, x_hi, w_hi, start=first, stop=False)
            pe.matmul(dst, x_hi, w_lo, start=False, stop=False)
            return pe.matmul(dst, x_lo, w_hi, start=False, stop=last)

        META = TT
        rows_of = [P] * TT + [NM]
        units = []
        for name, (n0, ns, w) in proj:
            for t in range(TT + 1 if name in ("small", "fk", "fv") else TT):
                units.append((name, t, n0, w))
        AUG_LAG = 2
        SMALLS = TT + 1

        def n_jobs(name):
            return {"fk": 2, "fq": 2, "sq": 1, "small": 1}.get(name, 0)

        plan = []
        for r in range(SMALLS):
            plan.append(("act_T", r))
            if r >= 1:
                plan.append(("mm", r - 1))
            if r >= 1 + AUG_LAG:
                plan.append(("head_T", r - 1 - AUG_LAG))
        plan.append(("mm", SMALLS - 1))
        plan += [("head_T", u) for u in range(SMALLS - 1 - AUG_LAG, SMALLS)]
        plan.append(("log_f", 0))
        pending = []
        for u in range(SMALLS, len(units)):
            plan.append(("mm", u))
            if u == SMALLS + 1:
                plan.append(("F", 0))
            pending.append(u)
            if len(pending) > AUG_LAG:
                plan.append(("head_T", pending.pop(0)))
        plan += [("head_T", u) for u in pending]
        plan = [s for s in plan if s[0] != "head_T" or n_jobs(units[s[1]][0])]
        staged = {}
        for s in plan:
            if s[0] == "head_T" or (s[0] == "mm" and (units[s[1]][0] == "small" or not n_jobs(units[s[1]][0]))):
                staged[s] = len(staged)
        job0 = {}
        n_tr = 0
        for s in plan:
            if s[0] in ("act_T", "head_T"):
                job0[s] = n_tr
                n_tr += 2 if s[0] == "act_T" else n_jobs(units[s[1]][0])
        TR1 = n_tr
        dve_jobs = [job0[s] + g for s in plan if s[0] == "act_T" for g in range(2)]
        NORMED = ("fk", "fq", "sq")
        by_dve = [u for u in range(len(units)) if units[u][0] in NORMED + ("small",)]
        by_act = [u for u in range(len(units)) if units[u][0] not in NORMED + ("small",)]
        normed = [u for u in range(len(units)) if n_jobs(units[u][0])]
        last_of_chunk = {u for u in range(len(units)) if u + 1 == len(units) or units[u + 1][0] != units[u][0]}
        first_of_chunk = {u for u in range(len(units)) if u == 0 or units[u - 1][0] != units[u][0]}

        s_x = [sem("s_x0"), sem("s_x1")]
        s_ss = sem("s_ss")
        s_ms = sem("s_ms")
        s_rt = sem("s_rt")
        s_ri = sem("s_ri")
        s_h = sem("s_h")
        s_free_dve = sem("s_free_dve")
        s_free_act = sem("s_free_act")
        s_qsq = sem("s_qsq")
        s_qms = sem("s_qms")
        s_qrt = sem("s_qrt")
        s_qri = sem("s_qri")
        s_qt = sem("s_qt")
        s_aug = sem("s_aug")
        s_stage = sem("s_stage")
        s_out = [sem(f"s_out{i}") for i in range(3)]
        s_z = sem("s_z")
        s_lf = sem("s_lf")
        s_F = sem("s_F")
        s_Fsb = sem("s_Fsb")
        s_gain = sem("s_gain")

        with ExitStack() as st:
            hT_hi = sb(st, "hT_hi", [P, KT, T + NM], f32r)
            hT_lo = sb(st, "hT_lo", [P, KT, T + NM], f32r)
            xin = [sb(st, f"xin{i}", [P, D]) for i in range(2)]
            g1 = sb(st, "g1", [P, D])
            squares = sb(st, "squares", [P, NC])
            scaled = sb(st, "scaled", [P, NC])
            aug = [sb(st, f"aug{i}", [P, FH, AUG]) for i in range(3)]
            stage = [sb(st, f"stage{i}", [P, D]) for i in range(3)]
            gains = sb(st, "gains", [P, 4, HD])
            bf = sb(st, "bf", [P, FH])
            ss = sb(st, "ss", [P, 4 * SMALLS])
            qss = sb(st, "qss", [P, 4, FH])
            z = sb(st, "z", [P, 4, SMALLS, FH])
            Fs = sb(st, "Fs", [P, 2, SMALLS, FH])

            gain_of = {"fq": 0, "fk": 1, "sq": 2, "small": 3}
            n_stage = [0]

            def heads_of(name):
                return KVH if name == "small" else FH

            def unit_cols(name):
                return (FH, FH + KW) if name == "small" else (0, NC)

            with nc.Block() as block:
                @block.sync
                def _(sp):
                    for n in range(N_PROJ):
                        load_sub(sp, n)

                @block.gpsimd
                def _(pool):
                    pool.dma_start(xin[0][:, :], x2[0:P, :]).then_inc(s_x[0], 16)
                    pool.dma_start(xin[1][:, :], x2[P:2 * P, :]).then_inc(s_x[1], 16)
                    pool.dma_start(g1[:, :], row(norm1_gain)).then_inc(s_const, 16)
                    pool.dma_start(cst[:, :], c_cst).then_inc(s_const, 16)
                    for i, g in enumerate((fox_q_gain, fox_k_gain, swa_q_gain, swa_k_gain)):
                        pool.dma_start(gains[:, i, :], row(g)).then_inc(s_const, 16)
                    pool.dma_start(bf[:, :], row(b_forget)).then_inc(s_const, 16)
                    for n in range(2):
                        split_lo_pool(pool, n)
                    for s in plan:
                        if s[0] == "act_T" and s[1] + 2 < SMALLS:
                            t = s[1] + 2
                            pool.wait_ge(s_tr, job0[("act_T", s[1])] + 2)
                            src = x2[t * P:(t + 1) * P, :] if t < META else meta_tokens
                            pool.dma_start(xin[t % 2][0:rows_of[t], :], src).then_inc(s_x[t % 2], 16)
                        if s[0] == "mm" and s[1] in first_of_chunk:
                            n0 = units[s[1]][2]
                            for n in range(n0 + 2, min(n0 + RING, N_PROJ)):
                                split_lo_pool(pool, n)

                @block.scalar
                def _(act):
                    def norm_front(t):
                        n = rows_of[t]
                        act.wait_ge(s_x[t % 2], 16 * (t // 2 + 1))
                        if t >= 1:
                            act.wait_ge(s_ss, t)
                        act.activation(psum[0:n, 6:8, :].rearrange("p b n -> p (b n)"), xin[t % 2][0:n, :], ACT.Square,
                                       accum_out=ss[0:n, t:t + 1]).then_inc(s_ss, 1)
                        act.wait_ge(s_ms, t + 1)
                        act.activation(ss[0:n, 2 * SMALLS + t:2 * SMALLS + t + 1],
                                       ss[0:n, SMALLS + t:SMALLS + t + 1], ACT.Sqrt).then_inc(s_rt, 1)

                    def to_dram(parts):
                        k = n_stage[0]
                        act.wait_ge(s_stage, k + 1)
                        (dst, src), = parts
                        act.dma_start(dst, src).then_inc(s_out[k % 3], 16)
                        n_stage[0] += 1

                    def stage_free():
                        k = n_stage[0]
                        if k >= 3:
                            act.wait_ge(s_out[k % 3], 16 * (k // 3))
                        return stage[k % 3]

                    act.wait_ge(s_const, 16 * 7)
                    for i in (0, 2):
                        act.activation(gains[:, i, :], gains[:, i, :], ACT.Copy, scale=SCALE).then_inc(s_gain, 1)
                    norm_front(0)
                    for n in range(2):
                        split_hi(act, n)
                    n_unit = 0
                    for s, i in plan:
                        if s == "act_T":
                            if i + 1 < SMALLS:
                                norm_front(i + 1)
                            n = rows_of[i]
                            for g in range(2):
                                j = job0[(s, i)] + g
                                act.wait_ge(s_tr, j + 1)
                                act.activation(hT_hi[:, g * 4:g * 4 + 4, i * P:i * P + n],
                                               bank(4 + j % 2).rearrange("p (k n) -> p k n", k=4)[:, :, 0:n],
                                               ACT.Copy).then_inc(s_tr_act, 1)
                        elif s == "mm":
                            name, t, n0, w = units[i]
                            n = rows_of[t]
                            if i in first_of_chunk:
                                for m in range(n0 + 2, min(n0 + RING, N_PROJ)):
                                    split_hi(act, m)
                            act.wait_ge(s_mm, i + 1)
                            src = bank(i % 4)[0:n, 0:w]
                            if name in gain_of:
                                k = normed.index(i)
                                c0, c1 = unit_cols(name)
                                if k >= 1:
                                    act.wait_ge(s_qms, k)
                                act.activation(squares[0:n, 0:c1 - c0], src[:, c0:c1], ACT.Square).then_inc(s_qsq, 1)
                                if name == "small":
                                    dst = stage_free()
                                    act.activation(dst[0:n, 0:KW], src[:, FH + KW:w], ACT.Copy).then_inc(s_stage, 1)
                                    to_dram([(v_d[0:n, t, FW:FW + KW], dst[0:n, 0:KW])])
                                act.wait_ge(s_qms, k + 1)
                                nh = heads_of(name)
                                act.activation(qss[0:n, 2, 0:nh], qss[0:n, 1, 0:nh], ACT.Sqrt).then_inc(s_qrt, 1)
                            else:
                                dst = stage_free()
                                func = ACT.Copy if name == "fv" else ACT.Sigmoid
                                act.activation(dst[0:n, 0:NC], src, func).then_inc(s_stage, 1)
                                act.wait_ge(s_stage, n_stage[0] + 1)
                                act.sem_inc(s_free_act, 1)
                                if name == "fv":
                                    to_dram([(v_d[0:n, t, 0:FW], dst[0:n, 0:NC])])
                                else:
                                    c = int(name[1:]) * NC
                                    to_dram([(gate_d[:, t, c:c + NC], dst[:, 0:NC])])
                        elif s == "log_f":
                            act.wait_ge(s_z, SMALLS + 2)
                            act.activation(z[:, 1], z[:, 1], ACT.Exp, scale=-1.0).then_inc(s_lf, 1)
                            act.wait_ge(s_z, SMALLS + 3)
                            act.activation(z[:, 1], z[:, 1], ACT.Ln).then_inc(s_lf, 1)
                        elif s == "head_T":
                            name, t, n0, w = units[i]
                            n = rows_of[t]
                            j = job0[(s, i)]
                            dst = stage_free()
                            for g in range(n_jobs(name)):
                                act.wait_ge(s_tr, j + g + 1)
                                src = bank(4 + (j + g) % 2).rearrange("p (k n) -> p k n", k=4)
                                if name in ("fk", "fq"):
                                    view = dst[0:AUG, 0:FH * n].rearrange("p (h n) -> p h n", n=n)
                                    ins = act.activation(view[:, g * 4:g * 4 + 4, :], src[0:AUG, :, 0:n], ACT.Copy)
                                elif name == "sq":
                                    view = dst[:, 0:4 * n].rearrange("p (h n) -> p h n", n=n)
                                    ins = act.activation(view, src[:, :, 0:n], ACT.Copy)
                                else:
                                    view = dst[:, 0:KVH * n].rearrange("p (h n) -> p h n", n=n)
                                    ins = act.activation(view, src[:, 0:KVH, 0:n], ACT.Copy)
                                ins.then_inc(s_tr_act, 1)
                            act.wait_ge(s_tr_act, j + n_jobs(name))
                            act.sem_inc(s_stage, 1)
                            dram = {"fk": fkT_d, "fq": fqT_d, "sq": sqT_d, "small": skT_d}[name]
                            to_dram([(dram[:, :, t * P:t * P + n], view)])

                @block.vector
                def _(dve):
                    def norm_front(t):
                        n = rows_of[t]
                        dve.wait_ge(s_ss, t + 1)
                        dve.tensor_scalar(ss[0:n, SMALLS + t:SMALLS + t + 1], ss[0:n, t:t + 1], 1.0 / D, EPS,
                                          ALU.mult, ALU.add).then_inc(s_ms, 1)
                        dve.wait_ge(s_rt, t + 1)
                        dve.reciprocal(ss[0:n, 3 * SMALLS + t:3 * SMALLS + t + 1],
                                       ss[0:n, 2 * SMALLS + t:2 * SMALLS + t + 1]).then_inc(s_ri, 1)
                        dve.wait_ge(s_ri, t + 1)
                        dve.scalar_tensor_tensor(xin[t % 2][0:n, :], xin[t % 2][0:n, :],
                                                 ss[0:n, 3 * SMALLS + t:3 * SMALLS + t + 1], g1[0:n, :],
                                                 ALU.mult, ALU.mult).then_inc(s_h, 1)

                    dve.memset(z[:, 0], 0.0).then_inc(s_z, 1)
                    dve.wait_ge(s_z, 1)
                    dve.wait_ge(s_const, 16 * 7)
                    dve.wait_ge(s_gain, 2)
                    norm_front(0)
                    for n in range(2):
                        split_lo(dve, n)
                    for s, i in plan:
                        if s == "act_T":
                            if i + 1 < SMALLS:
                                norm_front(i + 1)
                            n = rows_of[i]
                            for g in range(2):
                                j = job0[(s, i)] + g
                                dve.wait_ge(s_tr_act, j + 1)
                                dve.tensor_tensor(hT_lo[:, g * 4:g * 4 + 4, i * P:i * P + n],
                                                  bank(4 + j % 2).rearrange("p (k n) -> p k n", k=4)[:, :, 0:n],
                                                  hT_hi[:, g * 4:g * 4 + 4, i * P:i * P + n].bitcast(f32),
                                                  ALU.subtract).then_inc(s_tr_dve, 1)
                        elif s == "mm":
                            name, t, n0, w = units[i]
                            n = rows_of[t]
                            if i in first_of_chunk:
                                for m in range(n0 + 2, min(n0 + RING, N_PROJ)):
                                    split_lo(dve, m)
                            if name not in gain_of:
                                continue
                            k = normed.index(i)
                            nh = heads_of(name)
                            c0, c1 = unit_cols(name)
                            dve.wait_ge(s_qsq, k + 1)
                            dve.tensor_reduce(qss[0:n, 0, 0:nh],
                                              squares[0:n, 0:c1 - c0].rearrange("p (h d) -> p h d", d=HD),
                                              AX.X, ALU.add).then_inc(s_qri, 1)
                            dve.wait_ge(s_qri, 3 * k + 1)
                            dve.tensor_scalar(qss[0:n, 1, 0:nh], qss[0:n, 0, 0:nh], 1.0 / HD, EPS,
                                              ALU.mult, ALU.add).then_inc(s_qms, 1)
                            if name == "small":
                                dve.wait_ge(s_stage, staged[(s, i)] + 1)
                                dve.tensor_tensor(z[0:n, 0, t, :], bank(i % 4)[0:n, 0:FH], bf[0:n, :],
                                                  ALU.add).then_inc(s_z, 1)
                            dve.wait_ge(s_qrt, k + 1)
                            dve.reciprocal(qss[0:n, 3, 0:nh], qss[0:n, 2, 0:nh]).then_inc(s_qri, 1)
                            dve.wait_ge(s_qri, 3 * k + 2)
                            dve.tensor_tensor(scaled[0:n, 0:c1 - c0].rearrange("p (h d) -> p h d", d=HD),
                                              bank(i % 4)[0:n, c0:c1].rearrange("p (h d) -> p h d", d=HD),
                                              qss[0:n, 3, 0:nh].unsqueeze(2).to_broadcast([n, nh, HD]),
                                              ALU.mult).then_inc(s_free_dve, 1)
                            dve.wait_ge(s_free_dve, k + 1)
                            if k >= 3:
                                old = normed[k - 3]
                                dve.wait_ge(s_tr, job0[("head_T", old)] + n_jobs(units[old][0]))
                            g = gains[0:n, gain_of[name], :]
                            src = scaled[0:n, 0:c1 - c0].rearrange("p (h d) -> p h d", d=HD)
                            a = aug[k % 3]
                            if name == "small":
                                dup = a[0:n, :, :].rearrange("p h d -> p (h d)")[:, 0:2 * KW] \
                                    .rearrange("p (g c d) -> p g c d", g=KVH, c=2)
                                for c in range(2):
                                    ins = dve.tensor_tensor(dup[:, :, c, :], src, g.unsqueeze(1).to_broadcast([n, KVH, HD]),
                                                            ALU.mult)
                                    if c == 0:
                                        ins.then_inc(s_qri, 1)
                                ins.then_inc(s_aug, 1)
                            elif name == "sq":
                                ins = dve.tensor_tensor(
                                    a[0:n, :, :].rearrange("p h d -> p (h d)")[:, 0:NC].rearrange("p (h d) -> p h d", d=HD),
                                    src, g.unsqueeze(1).to_broadcast([n, FH, HD]), ALU.mult)
                                ins.then_inc(s_aug, 1)
                                dve.sem_inc(s_qri, 1)
                            else:
                                dve.tensor_tensor(a[0:n, :, 0:HD], src, g.unsqueeze(1).to_broadcast([n, FH, HD]),
                                                  ALU.mult).then_inc(s_qri, 1)
                                one, f = (HD, HD + 1) if name == "fk" else (HD + 1, HD)
                                dve.memset(a[0:n, :, one:one + 1], 1.0).then_inc(s_qt, 1)
                                dve.tensor_copy(a[0:n, :, f:f + 1],
                                                Fs[0:n, 1 if name == "fk" else 0, t, :].unsqueeze(2)).then_inc(s_qt, 1)
                                kk = k - SMALLS
                                dve.wait_ge(s_qt, 2 * kk + 2)
                                dve.wait_ge(s_qri, 3 * k + 3)
                                dve.sem_inc(s_aug, 1)
                        elif s == "log_f":
                            dve.wait_ge(s_z, SMALLS + 1)
                            dve.scalar_tensor_tensor(z[:, 1], z[:, 0], -1.0, z[:, 0], ALU.mult, ALU.max).then_inc(s_z, 1)
                            dve.wait_ge(s_lf, 1)
                            dve.tensor_scalar(z[:, 1], z[:, 1], 1.0, None, ALU.add).then_inc(s_z, 1)
                            dve.wait_ge(s_lf, 2)
                            dve.scalar_tensor_tensor(z[:, 2], z[:, 0], 0.0, z[:, 1], ALU.min, ALU.subtract).then_inc(s_z, 1)
                            dve.wait_ge(s_F, 1)
                            fps = bank(6)[:, 0:SMALLS * FH].rearrange("p (t h) -> p t h", h=FH)
                            dve.tensor_copy(Fs[:, 0, 0:TT, :], fps[:, 0:TT, :]).then_inc(s_Fsb, 1)
                            dve.tensor_copy(Fs[0:NM, 0, META, :], fps[0:NM, META, :]).then_inc(s_Fsb, 1)
                            dve.tensor_scalar(Fs[:, 1, 0:TT, :], fps[:, 0:TT, :], -1.0, None, ALU.mult).then_inc(s_Fsb, 1)
                            dve.tensor_scalar(Fs[0:NM, 1, META, :], fps[0:NM, META, :], -1.0, None,
                                              ALU.mult).then_inc(s_Fsb, 1)
                            dve.wait_ge(s_Fsb, 4)

                @block.tensor
                def _(pe):
                    def job_free(j):
                        if j >= 2:
                            pe.wait_ge(s_tr_act, j - 1)
                            if j - 2 in dve_jobs:
                                pe.wait_ge(s_tr_dve, dve_jobs.index(j - 2) + 1)

                    pe.wait_ge(s_const, 16 * 7)
                    for s, i in plan:
                        if s == "act_T":
                            n = rows_of[i]
                            pe.wait_ge(s_h, i + 1)
                            for g in range(2):
                                j = job0[(s, i)] + g
                                job_free(j)
                                for k in range(4):
                                    c = (g * 4 + k) * P
                                    ins = pe.transpose(bank(4 + j % 2)[:, k * P:k * P + n],
                                                       xin[i % 2][0:n, c:c + P], ident[0:n, 0:n])
                                ins.then_inc(s_tr, 1)
                        elif s == "mm":
                            name, t, n0, w = units[i]
                            n = rows_of[t]
                            if i in first_of_chunk:
                                pe.wait_ge(s_lo, n0 + 2)
                                pe.wait_ge(s_lo_pool, n0 + 2)
                            if i < SMALLS:
                                pe.wait_ge(s_tr_dve, 2 * (t + 1))
                            if i >= 4:
                                if (i - 4) in by_dve:
                                    pe.wait_ge(s_free_dve, by_dve.index(i - 4) + 1)
                                    if units[i - 4][0] == "small":
                                        pe.wait_ge(s_z, i - 4 + 2)
                                        pe.wait_ge(s_stage, staged[("mm", i - 4)] + 1)
                                else:
                                    pe.wait_ge(s_free_act, by_act.index(i - 4) + 1)
                            dst = bank(i % 4)[0:n, 0:w]
                            for k in range(KT):
                                slot = (n0 + k // HK) % RING
                                ins = three_passes(pe, dst, hT_hi[:, k, t * P:t * P + n], hT_lo[:, k, t * P:t * P + n],
                                                   whi[slot][:, k % HK, 0:w], wlo[slot][:, k % HK, 0:w],
                                                   k == 0, k == KT - 1)
                                if i in last_of_chunk and k == HK - 1:
                                    ins.then_inc(s_used, 1)
                            ins.then_inc(s_mm, 1)
                            if i in last_of_chunk:
                                pe.wait_ge(s_mm, i + 1)
                                pe.sem_inc(s_used, 1)
                        elif s == "F":
                            pe.wait_ge(s_z, SMALLS + 4)
                            lf = z[:, 2]
                            for t in range(TT):
                                dst = bank(6)[:, t * FH:(t + 1) * FH]
                                pe.matmul(dst, ones[0:NM, :], lf[0:NM, META, :], start=True, stop=False)
                                for j in range(t):
                                    pe.matmul(dst, ones, lf[:, j, :], start=False, stop=False)
                                pe.matmul(dst, tri_incl, lf[:, t, :], start=False, stop=True)
                            pe.matmul(bank(6)[0:NM, META * FH:(META + 1) * FH], tri_incl[0:NM, 0:NM],
                                      lf[0:NM, META, :], start=True, stop=True).then_inc(s_F, 1)
                        elif s == "head_T":
                            name, t, n0, w = units[i]
                            n = rows_of[t]
                            k = normed.index(i)
                            pe.wait_ge(s_aug, k + 1)
                            a = aug[k % 3]
                            flat = a[0:n, :, :].rearrange("p h d -> p (h d)")
                            for g in range(n_jobs(name)):
                                j = job0[(s, i)] + g
                                job_free(j)
                                dst = bank(4 + j % 2)
                                if name in ("fk", "fq"):
                                    for h in range(4):
                                        ins = pe.transpose(dst[0:AUG, h * P:h * P + n], a[0:n, g * 4 + h, :], ident[0:n, 0:n])
                                else:
                                    for h in range(4 if name == "sq" else KVH):
                                        ins = pe.transpose(dst[:, h * P:h * P + n], flat[:, h * P:(h + 1) * P],
                                                           ident[0:n, 0:n])
                                ins.then_inc(s_tr, 1)
            N_STAGE = n_stage[0]

        def stage_count(i):
            return 16 * ((N_STAGE - i + 2) // 3)

        if block_kernel.stop == 1:
            with nc.Block() as block:
                @block.sync
                def _(sp):
                    for i in range(3):
                        sp.wait_ge(s_out[i], stage_count(i))
            return

        rest = ctx.enter_context(ExitStack())
        token_major = sb(rest, "token_major", [P, TT, D])

        ORDER = [7, 0, 6, 1, 5, 2, 4, 3]
        att = [(h, i) for h in range(FH + SH) for i in ORDER]
        META_AT = T

        def key_blocks(h, i):
            if h < FH:
                return [(b * P, P, b) for b in range(i + 1)] + [(META_AT, NM, META)]
            if i == 0:
                return [(0, P, 0), (META_AT, NM, META)]
            return [((i - 1) * P, P, i - 1), (i * P, P, i)]

        att_jobs = []
        jobs_of = []
        for u, (h, i) in enumerate(att):
            blocks = list(enumerate(key_blocks(h, i)))
            jobs_of.append([])
            for g in range(0, len(blocks), 4):
                jobs_of[u].append(len(att_jobs))
                att_jobs.append((u, blocks[g:g + 4]))

        PT_RING = 4
        s_kq = [sem("s_kq0"), sem("s_kq1")]
        s_kv = sem("s_kv")
        s_S = sem("s_S")
        s_msk = sem("s_msk")
        s_mx = sem("s_mx")
        s_nm = sem("s_nm")
        s_exp = sem("s_exp")
        s_esk = sem("s_esk")
        s_pt = sem("s_pt")
        s_pt_act = sem("s_pt_act")
        s_pt_dve = sem("s_pt_dve")
        s_pv = sem("s_pv")
        s_den = sem("s_den")
        s_O = sem("s_O")

        with ExitStack() as st:
            kT = [sb(st, f"kT{i}", [P, T + NM]) for i in range(2)]
            qT = [sb(st, f"qT{i}", [P, T]) for i in range(2)]
            skT = sb(st, "skT", [P, KVH, T + NM])
            V = sb(st, "V", [P, TT + 1, FW + KW])
            probs = [sb(st, f"probs{i}", [P, T + NM]) for i in range(2)]
            biased = [sb(st, f"biased{i}", [P, 2 * P]) for i in range(2)]
            probsT = [sb(st, f"probsT{i}", [P, 4, P]) for i in range(PT_RING)]
            dist = sb(st, "dist", list(CONST_SHAPES[1]))
            sinks = sb(st, "sinks", [P, SH])
            row_max = sb(st, "row_max", [P, 2])
            neg_max = sb(st, "neg_max", [P, 2])
            row_sum = sb(st, "row_sum", [P, FH + SH, TT])
            sink_exp = sb(st, "sink_exp", [P, SH, TT])
            recip = sb(st, "recip", [P, 2, TT])

            score_buf = [psum[:, 0:3, :].rearrange("p b n -> p (b n)"), psum[:, 3:5, :].rearrange("p b n -> p (b n)")]

            def width(u):
                return sum(n for _, n, _ in key_blocks(*att[u]))

            def kq_slot(h):
                return h if h < FH else FH + (h - FH) // 2

            def job_done(eng, j):
                eng.wait_ge(s_pt_act if j % 2 == 0 else s_pt_dve, j // 2 + 1)

            with nc.Block() as block:
                @block.sync
                def _(sp):
                    for i in range(3):
                        sp.wait_ge(s_out[i], stage_count(i))
                    for k in range(FH + SH // 2):
                        if k >= 2:
                            last_head = k - 2 if k - 2 < FH else FH + 2 * (k - 2 - FH) + 1
                            sp.wait_ge(s_S, TT * (last_head + 1))
                        if k < FH:
                            sp.dma_start(kT[k % 2][0:AUG, :], fkT_d[:, k, :]).then_inc(s_kq[k % 2], 16)
                            sp.dma_start(qT[k % 2][0:AUG, :], fqT_d[:, k, :]).then_inc(s_kq[k % 2], 16)
                        else:
                            sp.dma_start(qT[k % 2][:, :], sqT_d[:, k - FH, :]).then_inc(s_kq[k % 2], 16)
                        if k == 0:
                            sp.dma_start(V[:, 0:TT, :], v_d[:, 0:TT, :]).then_inc(s_kv, 16)
                            sp.dma_start(V[0:NM, META, :], v_d[0:NM, META, :]).then_inc(s_kv, 16)
                            sp.dma_start(skT[:, :, :], skT_d).then_inc(s_kv, 16)
                            sp.dma_start(dist[:, :], c_dist).then_inc(s_kv, 16)
                            sp.dma_start(sinks[:, :], row(swa_sinks)).then_inc(s_kv, 16)
                        if k == 1:
                            for n in range(N_PROJ, N_PROJ + RING):
                                load_sub(sp, n)

                @block.gpsimd
                def _(pool):
                    for n in range(N_PROJ, N_PROJ + RING):
                        split_lo_pool(pool, n)

                @block.scalar
                def _(act):
                    def exponential(u):
                        h, i = att[u]
                        n = width(u)
                        act.wait_ge(s_nm, u + 1)
                        if u >= 2:
                            act.wait_ge(s_pt, jobs_of[u - 2][-1] + 1)
                        src = score_buf[u % 2][:, 0:n] if h < FH else biased[u % 2][:, 0:n]
                        act.activation(probs[u % 2][:, 0:n], src, ACT.Exp, bias=neg_max[:, u % 2:u % 2 + 1],
                                       accum_out=row_sum[:, h, i:i + 1]).then_inc(s_exp, 1)
                        if h >= FH:
                            act.activation(sink_exp[:, h - FH, i:i + 1], sinks[:, h - FH:h - FH + 1], ACT.Exp,
                                           bias=neg_max[:, u % 2:u % 2 + 1]).then_inc(s_esk, 1)

                    act.wait_ge(s_kv, 16 * 5)
                    exponential(0)
                    for u in range(len(att)):
                        if u % 8 == 2 and u // 8 < RING:
                            split_hi(act, N_PROJ + u // 8)
                        for j in jobs_of[u]:
                            if j % 2 == 0:
                                act.wait_ge(s_pt, j + 1)
                                if j >= PT_RING:
                                    act.wait_ge(s_pv, j - PT_RING + 1)
                                act.activation(probsT[j % PT_RING][:, :, :], bank(5).rearrange("p (b q) -> p b q", b=4),
                                               ACT.Copy).then_inc(s_pt_act, 1)
                        if u + 1 < len(att):
                            exponential(u + 1)

                @block.vector
                def _(dve):
                    def softmax_front(u):
                        h, i = att[u]
                        n = width(u)
                        S = score_buf[u % 2]
                        dve.wait_ge(s_S, u + 1)
                        if h < FH:
                            own = S[:, i * P:(i + 1) * P]
                            dve.tensor_tensor(own, own, causal, ALU.add).then_inc(s_msk, 1)
                            src = S[:, 0:n]
                        else:
                            slope = 2.0 ** (-8.0 * (h - FH + 1) / SH)
                            bias = dist[:, 0:2 * P] if i else dist[:, 2 * P:3 * P + NM]
                            if u >= 2:
                                dve.wait_ge(s_exp, u - 1)
                            dve.scalar_tensor_tensor(biased[u % 2][:, 0:n], bias, slope, S[:, 0:n],
                                                     ALU.mult, ALU.add).then_inc(s_msk, 1)
                            src = biased[u % 2][:, 0:n]
                        dve.wait_ge(s_msk, u + 1)
                        dve.tensor_reduce(row_max[:, u % 2:u % 2 + 1], src, AX.X, ALU.max).then_inc(s_mx, 1)
                        dve.wait_ge(s_mx, u + 1)
                        if u >= 2:
                            dve.wait_ge(s_exp, u - 1)
                            if h >= FH and u - 2 >= FH * TT:
                                dve.wait_ge(s_esk, u - 2 - FH * TT + 1)
                        if h < FH:
                            dve.tensor_scalar(neg_max[:, u % 2:u % 2 + 1], row_max[:, u % 2:u % 2 + 1], -1.0, None,
                                              ALU.mult).then_inc(s_nm, 1)
                        else:
                            dve.tensor_scalar(neg_max[:, u % 2:u % 2 + 1], row_max[:, u % 2:u % 2 + 1],
                                              sinks[:, h - FH:h - FH + 1], -1.0, ALU.max, ALU.mult).then_inc(s_nm, 1)

                    den = 0
                    dve.wait_ge(s_kv, 16 * 5)
                    softmax_front(0)
                    for u in range(len(att)):
                        h, i = att[u]
                        if u % 8 == 2 and u // 8 < RING:
                            split_lo(dve, N_PROJ + u // 8)
                        if u + 1 < len(att):
                            softmax_front(u + 1)
                        for j in jobs_of[u]:
                            if j % 2 == 1:
                                dve.wait_ge(s_pt, j + 1)
                                if j >= PT_RING:
                                    dve.wait_ge(s_pv, j - PT_RING + 1)
                                dve.tensor_copy(probsT[j % PT_RING][:, :, :],
                                                bank(6).rearrange("p (b q) -> p b q", b=4)).then_inc(s_pt_dve, 1)
                        if i == ORDER[-1]:
                            total = row_sum[:, h, :]
                            dve.wait_ge(s_exp, u + 1)
                            if h >= FH:
                                dve.wait_ge(s_esk, u - FH * TT + 1)
                                dve.tensor_tensor(recip[:, 0, :], total, sink_exp[:, h - FH, :], ALU.add).then_inc(s_den, 1)
                                den += 1
                                dve.wait_ge(s_den, den)
                                total = recip[:, 0, :]
                            dve.reciprocal(recip[:, 1, :], total).then_inc(s_den, 1)
                            den += 1
                            dve.wait_ge(s_den, den)
                            dve.wait_ge(s_pv, jobs_of[u][-1] + 1)
                            dve.tensor_tensor(token_major[:, :, h * HD:(h + 1) * HD],
                                              bank(7).rearrange("p (t d) -> p t d", d=HD),
                                              recip[:, 1, :].unsqueeze(2).to_broadcast([P, TT, HD]),
                                              ALU.mult).then_inc(s_O, 1)

                @block.tensor
                def _(pe):
                    def scores(u):
                        h, i = att[u]
                        k = kq_slot(h)
                        if i == ORDER[0]:
                            loads = sum(2 if m < FH else 1 for m in range(k % 2, k + 1, 2))
                            pe.wait_ge(s_kq[k % 2], 16 * loads)
                        if u >= 2:
                            pe.wait_ge(s_exp if att[u - 2][0] < FH else s_msk, u - 1)
                        S = score_buf[u % 2]
                        if h < FH:
                            rows, keys = slice(0, AUG), kT[k % 2]
                        else:
                            r0 = HD * (h % 2)
                            rows, keys = slice(r0, r0 + HD), skT[:, (h - FH) // (SH // KVH), :]
                        q = qT[k % 2][rows, i * P:(i + 1) * P]
                        runs = []
                        at = 0
                        for c, n, _ in key_blocks(h, i):
                            if runs and runs[-1][0] + runs[-1][2] == c and at % NC and n == P:
                                runs[-1][2] += n
                            else:
                                runs.append([c, at, n])
                            at += n
                        for c, at, n in runs:
                            ins = pe.matmul(S[:, at:at + n], q, keys[rows, c:c + n], start=True, stop=True)
                        ins.then_inc(s_S, 1)

                    def values(j):
                        u, blocks = att_jobs[j]
                        h, i = att[u]
                        if i == ORDER[0] and j == jobs_of[u][0] and h >= 1:
                            pe.wait_ge(s_O, h)
                        job_done(pe, j)
                        v0 = h * HD if h < FH else FW + HD * ((h - FH) // (SH // KVH))
                        n_blocks = len(key_blocks(h, i))
                        for m, (b, (c, n, tile)) in enumerate(blocks):
                            ins = pe.matmul(bank(7)[:, i * HD:(i + 1) * HD], probsT[j % PT_RING][0:n, m, :],
                                            V[0:n, tile, v0:v0 + HD], start=(b == 0), stop=(b == n_blocks - 1))
                        ins.then_inc(s_pv, 1)

                    pe.wait_ge(s_kv, 16 * 5)
                    scores(0)
                    waiting = []
                    for u in range(len(att)):
                        if u + 1 < len(att):
                            scores(u + 1)
                        pe.wait_ge(s_exp, u + 1)
                        for j in jobs_of[u]:
                            if j >= 2:
                                job_done(pe, j - 2)
                            at = 0
                            for m, (b, (c, n, tile)) in enumerate(att_jobs[j][1]):
                                ins = pe.transpose(bank(5 + j % 2)[0:n, m * P:(m + 1) * P],
                                                   probs[u % 2][:, b * P:b * P + n], ident)
                            ins.then_inc(s_pt, 1)
                            waiting.append(j)
                            if len(waiting) > 1:
                                values(waiting.pop(0))
                    for j in waiting:
                        values(j)

        if block_kernel.stop == 2:
            with nc.Block() as block:
                @block.sync
                def _(sp):
                    sp.dma_start(out2.rearrange("(t p) n -> p t n", p=P), token_major[:, :, :]).then_inc(s_kv, 16)
                    sp.wait_ge(s_kv, 16 * 6)
            return

        s_g = [sem(f"s_g{i}") for i in range(4)]
        s_T = sem("s_T")
        s_T_act = sem("s_T_act")
        s_T_dve = sem("s_T_dve")
        s_mm3 = sem("s_mm3")
        s_o3 = sem("s_o3")
        s_mix = sem("s_mix")
        s_res = sem("s_res")
        ounits = []
        for kind, half, (n0, ns, w) in outs:
            for t in range(TT):
                ounits.append((kind, half, t, n0))
        N_MIX = 4 * TT
        xT_jobs = 2 * TT

        with ExitStack() as st:
            T_hi = sb(st, "T_hi", [P, KT, T], f32r)
            T_lo = sb(st, "T_lo", [P, KT, T], f32r)
            side = [sb(st, f"side{i}", [P, NC]) for i in range(4)]

            def taken(eng, tile, first_job, last):
                eng.wait_ge(s_T_dve, first_job + 2 * tile + 2)

            with nc.Block() as block:
                @block.sync
                def _(sp):
                    for n in range(N_PROJ + RING, N0):
                        load_sub(sp, n)
                    for m in range(RING):
                        load_expert_sub(sp, N0 + m, 0, m)

                @block.gpsimd
                def _(pool):
                    for u, (kind, half, t, n0) in enumerate(ounits):
                        if u >= 4:
                            pool.wait_ge(s_o3, u - 3)
                        c = half * NC + (D if kind == "swa" else 0)
                        src = x2[t * P:(t + 1) * P, half * NC:(half + 1) * NC] if kind == "res" \
                            else gate_d[:, t, c:c + NC]
                        pool.dma_start(side[u % 4][:, :], src).then_inc(s_g[u % 4], 16)
                        if t == 2:
                            k = u // TT
                            for n in splits_after[k]:
                                split_lo_pool(pool, n)

                @block.scalar
                def _(act):
                    def take(first_job, tiles):
                        for t in tiles:
                            for g in range(2):
                                j = first_job + 2 * t + g
                                act.wait_ge(s_T, j + 1)
                                if first_job:
                                    act.wait_ge(s_mm3, N_MIX)
                                act.activation(T_hi[:, g * 4:g * 4 + 4, t * P:(t + 1) * P],
                                               bank(4 + j % 2).rearrange("p (k n) -> p k n", k=4),
                                               ACT.Copy).then_inc(s_T_act, 1)

                    take(0, range(TT))
                    for k in range(4):
                        for n in splits_after[k]:
                            split_hi(act, n)
                    take(xT_jobs, range(TT))
                    for k in range(4, 6):
                        for n in splits_after[k]:
                            split_hi(act, n)

                @block.vector
                def _(dve):
                    def take(first_job, tiles):
                        for t in tiles:
                            for g in range(2):
                                j = first_job + 2 * t + g
                                dve.wait_ge(s_T_act, j + 1)
                                dve.tensor_tensor(T_lo[:, g * 4:g * 4 + 4, t * P:(t + 1) * P],
                                                  bank(4 + j % 2).rearrange("p (k n) -> p k n", k=4),
                                                  T_hi[:, g * 4:g * 4 + 4, t * P:(t + 1) * P].bitcast(f32),
                                                  ALU.subtract).then_inc(s_T_dve, 1)

                    take(0, range(TT))
                    for u, (kind, half, t, n0) in enumerate(ounits):
                        if u == N_MIX:
                            take(xT_jobs, range(TT))
                        if t == 2:
                            for n in splits_after[u // TT]:
                                split_lo(dve, n)
                        dve.wait_ge(s_mm3, u + 1)
                        dve.wait_ge(s_g[u % 4], 16 * (u // 4 + 1))
                        dst = token_major[:, t, half * NC:(half + 1) * NC]
                        if kind == "fox":
                            if half == 0 and t == 0:
                                dve.wait_ge(s_T, 2 * TT)
                            dve.tensor_tensor(dst, bank(u % 4), side[u % 4][:, :], ALU.mult).then_inc(s_o3, 1)
                        elif kind == "swa":
                            dve.tensor_tensor(side[u % 4][:, :], bank(u % 4), side[u % 4][:, :], ALU.mult).then_inc(s_mix, 1)
                            dve.wait_ge(s_mix, 2 * (half * TT + t) + 1)
                            dve.tensor_tensor(dst, dst, side[u % 4][:, :], ALU.add).then_inc(s_mix, 1)
                            dve.wait_ge(s_mix, 2 * (half * TT + t) + 2)
                            dve.sem_inc(s_o3, 1)
                        else:
                            dve.tensor_tensor(dst, bank(u % 4), side[u % 4][:, :], ALU.add).then_inc(s_o3, 1)

                @block.tensor
                def _(pe):
                    def transposes(first_job, t):
                        for g in range(2):
                            j = first_job + 2 * t + g
                            if j >= 2:
                                pe.wait_ge(s_T_act, j - 1)
                                pe.wait_ge(s_T_dve, j - 1)
                            for k in range(4):
                                c = (g * 4 + k) * P
                                ins = pe.transpose(bank(4 + j % 2)[:, k * P:(k + 1) * P],
                                                   token_major[:, t, c:c + P], ident)
                            ins.then_inc(s_T, 1)

                    for t in range(TT):
                        transposes(0, t)
                    for u, (kind, half, t, n0) in enumerate(ounits):
                        if u == N_MIX:
                            pe.wait_ge(s_o3, N_MIX)
                            for i in range(TT):
                                transposes(xT_jobs, i)
                        nk = KT if kind == "res" else FW // P
                        k0 = FW // P if kind == "swa" else 0
                        if t == 0:
                            pe.wait_ge(s_lo, n0 + nk // HK)
                            pe.wait_ge(s_lo_pool, n0 + nk // HK)
                            taken(pe, TT - 1, xT_jobs if kind == "res" else 0, None)
                        if u >= 4:
                            pe.wait_ge(s_o3, u - 3)
                        for k in range(nk):
                            slot = (n0 + k // HK) % RING
                            xs = (slice(None), k0 + k, slice(t * P, (t + 1) * P))
                            ins = three_passes(pe, bank(u % 4), T_hi[xs], T_lo[xs], whi[slot][:, k % HK, :],
                                               wlo[slot][:, k % HK, :], k == 0, k == nk - 1)
                            if nk == KT and k == HK - 1 and t == TT - 1:
                                ins.then_inc(s_used, 1)
                        ins.then_inc(s_mm3, 1)
                        if t == TT - 1:
                            pe.wait_ge(s_mm3, u + 1)
                            pe.sem_inc(s_used, 1)

        if block_kernel.stop == 3:
            with nc.Block() as block:
                @block.sync
                def _(sp):
                    sp.dma_start(out2.rearrange("(t p) n -> p t n", p=P), token_major[:, :, :]).then_inc(s_kv, 16)
                    sp.wait_ge(s_kv, 16 * 6)
            return

        s_c4 = sem("s_c4")
        s_out_res = sem("s_out_res")
        s_h2w = sem("s_h2w")
        s_ss4 = sem("s_ss4")
        s_ms4 = sem("s_ms4")
        s_rt4 = sem("s_rt4")
        s_h4 = sem("s_h4")
        s_wr = sem("s_wr")
        s_lg = sem("s_lg")
        s_lgs = sem("s_lgs")
        s_rk = sem("s_rk")
        s_dve4 = sem("s_dve4")
        s_ex4 = sem("s_ex4")
        s_mask = sem("s_mask")
        with ExitStack() as st:
            g2 = sb(st, "g2", [P, D])
            wr = sb(st, "wr", [P, KT, E])
            wr_hi = sb(st, "wr_hi", [P, KT, E], f32r)
            wr_lo = sb(st, "wr_lo", [P, KT, E], f32r)
            br = sb(st, "br", [P, E])
            h2T_hi = [sb(st, f"h2T_hi{i}", [P, KT, P], f32r) for i in range(2)]
            h2T_lo = [sb(st, f"h2T_lo{i}", [P, KT, P], f32r) for i in range(2)]
            ss = sb(st, "ss4", [P, 4, TT])
            logits = sb(st, "logits", [P, TT, E])
            top = sb(st, "top", [P, TT, 8])
            top_idx = sb(st, "top_idx", [P, TT, 8], u32)
            top_f = sb(st, "top_f", [P, TT, 8])
            gate4 = sb(st, "gate4", [P, TT, TOPK])
            gsum = sb(st, "gsum", [P, 2, TT])
            mask = sb(st, "mask", [P, TT, E])
            gates = sb(st, "gates", [P, TT, E])
            eq = sb(st, "eq", [P, TT, E])
            rank = sb(st, "rank", [P, TT, E])
            other = sb(st, "other", [P, TT, E])
            count = sb(st, "count", [P, E])
            it = sb(st, "it", [1, 6, E])
            grid = sb(st, "grid", [1, NJ, E])
            cols = sb(st, "cols", [1, 6, NJ])
            item_iota = sb(st, "item_iota", [1, NJ])

            with nc.Block() as block:
                @block.sync
                def _(sp):
                    sp.dma_start(g2[:, :], row(norm2_gain)).then_inc(s_c4, 16)
                    sp.dma_start(wr[:, :, :], wrt.rearrange("(k p) n -> p k n", p=P)).then_inc(s_c4, 16)
                    sp.dma_start(br[:, :], row(b_router)).then_inc(s_c4, 16)
                    sp.dma_start(item_iota[:, :], c_items).then_inc(s_c4, 16)
                    for t in range(TT):
                        sp.dma_start(out2[t * P:(t + 1) * P, :], token_major[:, t, :]).then_inc(s_out_res, 16)
                    for t in range(TT):
                        sp.wait_ge(s_h4, t + 1)
                        sp.dma_start(h2_d[t * P:(t + 1) * P, :], token_major[:, t, :]).then_inc(s_h2w, 16)
                    sp.wait_ge(s_h2w, 16 * TT)

                @block.gpsimd
                def _(pool):
                    for m in range(LEAD):
                        expert_lo_pool(pool, N0 + m, m)

                @block.scalar
                def _(act):
                    def norm_front(t):
                        if t >= 1:
                            act.wait_ge(s_ss4, t)
                        act.activation(psum[:, 6:8, :].rearrange("p b n -> p (b n)"), token_major[:, t, :], ACT.Square,
                                       accum_out=ss[:, 0, t:t + 1]).then_inc(s_ss4, 1)
                        act.wait_ge(s_ms4, t + 1)
                        act.activation(ss[:, 2, t:t + 1], ss[:, 1, t:t + 1], ACT.Sqrt).then_inc(s_rt4, 1)

                    act.wait_ge(s_c4, 16 * 4)
                    norm_front(0)
                    act.activation(wr_hi[:, :, :], wr[:, :, :], ACT.Copy).then_inc(s_wr, 1)
                    for t in range(TT):
                        if t + 1 < TT:
                            norm_front(t + 1)
                        for g in range(2):
                            j = 2 * xT_jobs + 2 * t + g
                            act.wait_ge(s_T, j + 1)
                            if t >= 2:
                                act.wait_ge(s_lg, t - 1)
                            act.activation(h2T_hi[t % 2][:, g * 4:g * 4 + 4, :],
                                           bank(4 + j % 2).rearrange("p (k n) -> p k n", k=4),
                                           ACT.Copy).then_inc(s_T_act, 1)
                    for m in range(LEAD):
                        expert_hi(act, N0 + m, m)
                    act.wait_ge(s_mask, 2)
                    act.activation(gate4[:, :, :], gate4[:, :, :], ACT.Exp).then_inc(s_ex4, 1)

                @block.vector
                def _(dve):
                    steps = [0]

                    def step(ins):
                        ins.then_inc(s_dve4, 1)
                        steps[0] += 1
                        dve.wait_ge(s_dve4, steps[0])

                    def norm_front(t):
                        dve.wait_ge(s_ss4, t + 1)
                        dve.tensor_scalar(ss[:, 1, t:t + 1], ss[:, 0, t:t + 1], 1.0 / D, EPS,
                                          ALU.mult, ALU.add).then_inc(s_ms4, 1)
                        dve.wait_ge(s_rt4, t + 1)
                        step(dve.reciprocal(ss[:, 3, t:t + 1], ss[:, 2, t:t + 1]))
                        if t == 0:
                            dve.wait_ge(s_out_res, 16 * TT)
                        dve.scalar_tensor_tensor(token_major[:, t, :], token_major[:, t, :], ss[:, 3, t:t + 1],
                                                 g2[:, :], ALU.mult, ALU.mult).then_inc(s_h4, 1)

                    dve.wait_ge(s_c4, 16 * 4)
                    norm_front(0)
                    dve.wait_ge(s_wr, 1)
                    dve.tensor_tensor(wr_lo[:, :, :], wr[:, :, :], wr_hi[:, :, :].bitcast(f32),
                                      ALU.subtract).then_inc(s_wr, 1)
                    for t in range(TT):
                        if t + 1 < TT:
                            norm_front(t + 1)
                        for g in range(2):
                            j = 2 * xT_jobs + 2 * t + g
                            dve.wait_ge(s_T_act, j + 1)
                            dve.tensor_tensor(h2T_lo[t % 2][:, g * 4:g * 4 + 4, :],
                                              bank(4 + j % 2).rearrange("p (k n) -> p k n", k=4),
                                              h2T_hi[t % 2][:, g * 4:g * 4 + 4, :].bitcast(f32),
                                              ALU.subtract).then_inc(s_T_dve, 1)
                        dve.wait_ge(s_lg, t + 1)
                        dve.tensor_tensor(logits[:, t, :], bank(t % 2)[:, 0:E], br[:, :], ALU.add).then_inc(s_lgs, 1)
                        dve.wait_ge(s_lgs, t + 1)
                        step(dve.max(top[:, t, :], logits[:, t, :]))
                        step(dve.max_index(top_idx[:, t, :], top[:, t, :], logits[:, t, :]))
                    for m in range(LEAD):
                        expert_lo(dve, N0 + m, m)
                    step(dve.tensor_copy(top_f[:, :, :], top_idx[:, :, :]))
                    step(dve.tensor_tensor(gate4[:, :, :], top[:, :, 0:TOPK],
                                           top[:, :, 0:1].to_broadcast([P, TT, TOPK]), ALU.subtract))
                    dve.sem_inc(s_mask, 1)
                    bE = [P, TT, E]
                    iota_b = iota_e.unsqueeze(1).to_broadcast(bE)
                    for k in range(TOPK):
                        idx_b = top_f[:, :, k:k + 1].to_broadcast(bE)
                        if k == 0:
                            step(dve.tensor_tensor(mask[:, :, :], iota_b, idx_b, ALU.is_equal))
                        else:
                            step(dve.tensor_tensor(eq[:, :, :], iota_b, idx_b, ALU.is_equal))
                            step(dve.tensor_tensor(mask[:, :, :], mask[:, :, :], eq[:, :, :], ALU.add))
                    dve.sem_inc(s_mask, 1)
                    dve.wait_ge(s_ex4, 1)
                    step(dve.tensor_reduce(gsum[:, 0, :], gate4[:, :, :], AX.X, ALU.add))
                    step(dve.reciprocal(gsum[:, 1, :], gsum[:, 0, :]))
                    step(dve.tensor_tensor(gate4[:, :, :], gate4[:, :, :],
                                           gsum[:, 1, :].unsqueeze(2).to_broadcast([P, TT, TOPK]), ALU.mult))
                    for k in range(TOPK):
                        step(dve.tensor_tensor(eq[:, :, :], iota_b, top_f[:, :, k:k + 1].to_broadcast(bE), ALU.is_equal))
                        dst = gates if k == 0 else eq
                        step(dve.tensor_tensor(dst[:, :, :], eq[:, :, :], gate4[:, :, k:k + 1].to_broadcast(bE), ALU.mult))
                        if k:
                            step(dve.tensor_tensor(gates[:, :, :], gates[:, :, :], eq[:, :, :], ALU.add))
                    dve.wait_ge(s_rk, 1)
                    step(dve.tensor_copy(rank[:, :, :], bank(2)[:, 0:TT * E].rearrange("p (t e) -> p t e", e=E)))
                    step(dve.tensor_copy(count[:, :], bank(3)[:, 0:E]))
                    step(dve.tensor_tensor(other[:, :, :], count[:, :].unsqueeze(1).to_broadcast(bE),
                                           tok_index.unsqueeze(2).to_broadcast(bE), ALU.add))
                    step(dve.tensor_tensor(other[:, :, :], other[:, :, :], rank[:, :, :], ALU.subtract))
                    step(dve.tensor_tensor(eq[:, :, :], rank[:, :, :], other[:, :, :], ALU.subtract))
                    step(dve.tensor_tensor(eq[:, :, :], eq[:, :, :], mask[:, :, :], ALU.mult))
                    step(dve.tensor_tensor(slot_of[:, :, :].rearrange("p e t -> p t e"), eq[:, :, :], other[:, :, :],
                                           ALU.add))
                    step(dve.tensor_copy(tok_gate[:, :, :, 1].rearrange("p e t -> p t e"), gates[:, :, :]))
                    step(dve.tensor_copy(tok_gate[:, :, :, 0].rearrange("p e t -> p t e"),
                                         tok_index.unsqueeze(2).to_broadcast(bE)))
                    cnt = count[0:1, :]
                    step(dve.tensor_scalar(it[:, 0, :], cnt, float(PAIR), 1.0, ALU.is_gt, ALU.add))
                    for k in range(2, T // PAIR):
                        step(dve.tensor_scalar(it[:, 1, :], cnt, float(k * PAIR), None, ALU.is_gt))
                        step(dve.tensor_tensor(it[:, 0, :], it[:, 0, :], it[:, 1, :], ALU.add))
                    step(dve.tensor_copy(it[:, 2, :], it[:, 0, :]))
                    a, b, d = 2, 3, 1
                    while d < E:
                        step(dve.tensor_copy(it[:, b, 0:d], it[:, a, 0:d]))
                        step(dve.tensor_tensor(it[:, b, d:E], it[:, a, d:E], it[:, a, 0:E - d], ALU.add))
                        a, b, d = b, a, 2 * d
                    bJ = [1, NJ, E]
                    j_b = item_iota[:, :].unsqueeze(2).to_broadcast(bJ)

                    def per_expert(v):
                        return v.unsqueeze(1).to_broadcast(bJ)

                    step(dve.tensor_tensor(grid[:, :, :], per_expert(it[:, a, :]), j_b, ALU.is_le))
                    step(dve.tensor_reduce(cols[:, 0, :], grid[:, :, :], AX.X, ALU.add))
                    step(dve.tensor_tensor(grid[:, :, :], grid[:, :, :], per_expert(it[:, 0, :]), ALU.mult))
                    step(dve.tensor_reduce(cols[:, 1, :], grid[:, :, :], AX.X, ALU.add))
                    step(dve.tensor_tensor(cols[:, 1, :], item_iota[:, :], cols[:, 1, :], ALU.subtract))
                    step(dve.tensor_scalar(cols[:, 1, :], cols[:, 1, :], float(PAIR), float(T - PAIR), ALU.mult, ALU.min))
                    step(dve.tensor_tensor(grid[:, :, :], cols[:, 0, :].unsqueeze(2).to_broadcast(bJ),
                                           per_expert(iota_e[0:1, :]), ALU.is_equal))
                    step(dve.tensor_tensor(grid[:, :, :], grid[:, :, :], per_expert(cnt), ALU.mult))
                    step(dve.tensor_reduce(cols[:, 2, :], grid[:, :, :], AX.X, ALU.add))
                    step(dve.tensor_tensor(cols[:, 2, :], cols[:, 2, :], cols[:, 1, :], ALU.subtract))
                    step(dve.tensor_scalar(cols[:, 2, :], cols[:, 2, :], float(P), None, ALU.is_gt))
                    step(dve.tensor_scalar(cols[:, 0, :], cols[:, 0, :], float(E - 1), None, ALU.min))
                    step(dve.tensor_copy(table[:, 0:3, :], cols[:, 0:3, :]))
                    step(dve.tensor_copy(table[:, 4, 0:1], it[:, a, E - 1:E]))
                    step(dve.memset(cols[:, 3, 0:1], 0.0))
                    step(dve.tensor_copy(cols[:, 3, 1:NJ], cols[:, 2, 0:NJ - 1]))
                    step(dve.tensor_copy(table[:, 5, :], cols[:, 3, :]))
                    a, b, d = 3, 4, 1
                    while d < NJ:
                        step(dve.tensor_copy(cols[:, b, 0:d], cols[:, a, 0:d]))
                        step(dve.tensor_tensor(cols[:, b, d:NJ], cols[:, a, d:NJ], cols[:, a, 0:NJ - d], ALU.add))
                        a, b, d = b, a, 2 * d
                    step(dve.tensor_copy(table[:, 3, :], cols[:, a, :]))

                @block.tensor
                def _(pe):
                    for t in range(TT):
                        pe.wait_ge(s_h4, t + 1)
                        for g in range(2):
                            j = 2 * xT_jobs + 2 * t + g
                            pe.wait_ge(s_T_act, j - 1)
                            pe.wait_ge(s_T_dve, j - 1)
                            for k in range(4):
                                c = (g * 4 + k) * P
                                ins = pe.transpose(bank(4 + j % 2)[:, k * P:(k + 1) * P],
                                                   token_major[:, t, c:c + P], ident)
                            ins.then_inc(s_T, 1)
                        pe.wait_ge(s_T_dve, 2 * xT_jobs + 2 * t + 2)
                        if t == 0:
                            pe.wait_ge(s_wr, 2)
                        if t >= 2:
                            pe.wait_ge(s_lgs, t - 1)
                        for k in range(KT):
                            ins = three_passes(pe, bank(t % 2)[:, 0:E], h2T_hi[t % 2][:, k, :], h2T_lo[t % 2][:, k, :],
                                               wr_hi[:, k, :], wr_lo[:, k, :], k == 0, k == KT - 1)
                        ins.then_inc(s_lg, 1)
                    pe.wait_ge(s_mask, 2)
                    for t in range(TT):
                        dst = bank(2)[:, t * E:(t + 1) * E]
                        for j in range(t):
                            pe.matmul(dst, ones, mask[:, j, :], start=(j == 0), stop=False)
                        pe.matmul(dst, tri_strict, mask[:, t, :], start=(t == 0), stop=True)
                    for j in range(TT):
                        ins = pe.matmul(bank(3)[:, 0:E], ones, mask[:, j, :], start=(j == 0), stop=(j == TT - 1))
                    ins.then_inc(s_rk, 1)

        rest.close()
        if block_kernel.stop == 4:
            with nc.Block() as block:
                @block.sync
                def _(sp):
                    o = out2.rearrange("(p a) n -> p (a n)", p=P)
                    sp.wait_ge(s_h2w, 16 * TT)
                    sp.dma_start(o[:, 0:E * TT], slot_of[:, :, :].rearrange("p e t -> p (e t)")).then_inc(s_kv, 16)
                    sp.dma_start(o[:, 512:512 + 2 * E * TT], tok_gate[:, :, :, :].rearrange("p e t c -> p (e t c)")).then_inc(s_kv, 16)
                    sp.dma_start(o[0:1, 2048:2048 + 3 * NJ], table[:, 0:3, :].rearrange("p e t -> p (e t)").bitcast(f32)).then_inc(s_kv, 16)
                    sp.wait_ge(s_kv, 16 * 8)
            return

        A, B = 0, 1
        START = 1
        m_usedB = sem("m_usedB")
        m_free = [sem("m_freeA"), sem("m_freeB")]
        m_sig = [sem("m_sigA"), sem("m_sigB")]
        m_glu = [sem("m_gluA"), sem("m_gluB")]
        m_act = [sem("m_actA"), sem("m_actB")]
        m_scat = [sem("m_scatA"), sem("m_scatB")]
        m_gat = [sem("m_gatA"), sem("m_gatB")]
        m_sel = [sem("m_selA"), sem("m_selB")]
        m_perm = [sem("m_permA"), sem("m_permB")]
        m_next = [sem("m_nextA"), sem("m_nextB")]
        m_cur = [sem("m_curA"), sem("m_curB")]
        m_tr = [sem("m_trA"), sem("m_trB")]
        m_tr_act = [sem("m_tr_actA"), sem("m_tr_actB")]
        m_tr_dve = [sem("m_tr_dveA"), sem("m_tr_dveB")]
        m_bias_raw = sem("m_bias_raw")
        m_bias_hi = sem("m_bias_hi")
        m_bias_lo = sem("m_bias_lo")
        m_warm = sem("m_warm")
        m_pick = sem("m_pick")
        m_const = sem("m_const")
        m_pass = sem("m_pass")

        ACT0, ACT1, TOKENS = 0, 1, 2

        def job(j, q):
            return 4 * j + (2 + q)

        def job_bank(b, q):
            return bank(7 if b else 4 + q % 2).rearrange("p (k n) -> p k n", k=4)

        with ExitStack() as st:
            slots = sb(st, "slots", [P, T])
            biases = sb(st, "biases", [2 * E, 2 * FF + D], f32r)
            pick = sb(st, "pick", [2 * E, P], f32r)
            warm = sb(st, "warm", [P, 2])
            tokens = [sb(st, f"tokens{b}", [P, D]) for b in (A, B)]
            xT_hi = [sb(st, f"xT_hi{b}", [P, KT, P], f32r) for b in (A, B)]
            xT_lo = [sb(st, f"xT_lo{b}", [P, KT, P], f32r) for b in (A, B)]
            hid = [sb(st, f"hid{b}", [P, FF]) for b in (A, B)]
            hidT_hi = [sb(st, f"hidT_hi{b}", [P, KT, P], f32r) for b in (A, B)]
            hidT_lo = [sb(st, f"hidT_lo{b}", [P, KT, P], f32r) for b in (A, B)]
            gate_part = [sb(st, f"gate_part{b}", [P, NC]) for b in (A, B)]
            sigm = [sb(st, f"sigm{b}", [P, NC]) for b in (A, B)]
            up_part = [sb(st, f"up_part{b}", [P, NC]) for b in (A, B)]
            y = [sb(st, f"y{b}", [P, D]) for b in (A, B)]
            onehot = [sb(st, f"onehot{b}", [P, TT, P]) for b in (A, B)]
            idx_next = [sb(st, f"idx_next{b}", [P, 1], i32) for b in (A, B)]
            gate_next = [sb(st, f"gate_next{b}", [P, 1]) for b in (A, B)]
            idx_cur = [sb(st, f"idx_cur{b}", [P, 1], i32) for b in (A, B)]
            gate_cur = [sb(st, f"gate_cur{b}", [P, 1]) for b in (A, B)]

            def item(eng, j):
                return (eng.value_load(table[0:1, 0, bass.ds(j, 1)], min_val=0, max_val=E - 1),
                        eng.value_load(table[0:1, 1, bass.ds(j, 1)], min_val=0, max_val=T - PAIR),
                        eng.value_load(table[0:1, 2, bass.ds(j, 1)], min_val=0, max_val=1))

            def has_B(eng, j):
                return eng.value_load(table[0:1, 2, bass.ds(j, 1)], min_val=0, max_val=1)

            def expert_of(eng, j):
                return eng.value_load(table[0:1, 0, bass.ds(j, 1)], min_val=0, max_val=E - 1)

            def n_items(eng):
                return eng.value_load(table[0:1, 4, 0:1], min_val=E, max_val=MAX_ITEMS)

            def B_before(eng, j):
                return eng.value_load(table[0:1, 3, bass.ds(j, 1)], min_val=0, max_val=MAX_ITEMS)

            def wait_from_zero(eng, s, value):
                eng.sem_inc(m_pass, 1)
                with eng.If(value > 0):
                    eng.wait_ge(s, value)
                    eng.sem_inc(m_pass, 1)

            def bias_cols(chunk):
                c = (chunk % 2) * FF + (chunk // 2) * NC if chunk < 4 else 2 * FF + (chunk - 4) * NC
                return slice(c, c + NC)

            bias_raw = [(hid[A], 0), (hid[B], FF), (y[A], 2 * FF)]

            def if_B(eng, flag, work, counted):
                with eng.If(flag > 0):
                    work()
                if not counted:
                    return
                with eng.Else():
                    for s, n, before in counted:
                        if not (isinstance(before, int) and before == 0):
                            eng.wait_ge(s, before)
                        eng.sem_inc(s, n)

            with nc.Block() as block:
                @block.sync
                def _(sp):
                    sp.dma_start(slots[:, :], c_slots).then_inc(m_const, 16)
                    for rows in (slice(0, E), slice(E, 2 * E)):
                        for src, dst in ((bup[:, 0:FF], hid[A]), (bup[:, FF:2 * FF], hid[B]), (bdn, y[A])):
                            sp.dma_start(dst[rows, :], src).then_inc(m_bias_raw, 16)
                    n = n_items(sp)
                    with sp.Fori(0, n) as j:
                        e = expert_of(sp, j)
                        for m in range(RING, SUBS):
                            load_expert_sub(sp, N0 + SUBS * j + m, e, m)
                        e1 = expert_of(sp, j + 1)
                        for m in range(RING):
                            load_expert_sub(sp, N0 + SUBS * j + SUBS + m, e1, m)
                    sp.wait_ge(s_raw[slot(LEAD)], raw_ready(LEAD, n))
                    sp.sem_inc(m_const, 1)

                @block.gpsimd
                def _(pool):
                    def gather(b, q):
                        pool.indirect_dma_start(
                            out=tokens[b][:, :], out_offset=None, in_=h2_d,
                            in_offset=bass.IndirectOffsetOnAxis(ap=idx_next[b][:, 0:1], axis=0)).then_inc(m_gat[b], 16)

                    def scatter_add(b):
                        pool.indirect_dma_start(
                            out=out2, out_offset=bass.IndirectOffsetOnAxis(ap=idx_cur[b][:, 0:1], axis=0),
                            in_=y[b][:, :], in_offset=None, compute_op=ALU.add).then_inc(m_scat[b], 16)

                    def second(item):
                        pool.wait_ge(m_scat[A], 16 * item + 16)
                        pool.wait_ge(m_cur[B], 2 * item + 2 + START)
                        pool.wait_ge(m_free[B], 6 * item + 6 + 2)
                        pool.sem_inc(m_pass, 1)
                        scatter_add(B)

                    n = n_items(pool)
                    two0 = has_B(pool, 0)
                    pool.wait_ge(m_next[A], 2)
                    gather(A, 0)

                    def gather_B(q):
                        pool.wait_ge(m_next[B], 2 * q + 2)
                        if not isinstance(q, int):
                            pool.wait_ge(m_tr[B], job(q - 1, ACT0))
                            pool.sem_inc(m_pass, 1)
                        gather(B, q)

                    if_B(pool, two0, lambda: gather_B(0), [])
                    with pool.Fori(0, n) as j:
                        two_last = pool.value_load(table[0:1, 5, bass.ds(j, 1)], min_val=0, max_val=1)
                        two1 = has_B(pool, j + 1)
                        before = B_before(pool, j)
                        for s in range(SUBS):
                            m = s + LEAD
                            expert_lo_pool(pool, N0 + SUBS * j + m, m % SUBS)
                            if s == 5:
                                pool.wait_ge(m_next[A], 2 * j + 4)
                                pool.wait_ge(m_tr[A], job(j, ACT0))
                                pool.sem_inc(m_pass, 1)
                                gather(A, j + 1)
                                if_B(pool, two1, lambda: gather_B(j + 1), [])
                            if s == 0:
                                if_B(pool, two_last, lambda: second(j - 1), [])
                        pool.wait_ge(m_cur[A], 2 * j + 2 + START)
                        pool.wait_ge(m_free[A], 6 * j + 6 + 2)
                        wait_from_zero(pool, m_scat[B], 16 * before)
                        pool.sem_inc(m_pass, 1)
                        scatter_add(A)
                    two_last = pool.value_load(table[0:1, 5, bass.ds(n, 1)], min_val=0, max_val=1)
                    if_B(pool, two_last, lambda: second(n - 1), [])
                    pool.wait_ge(m_scat[A], 16 * n)
                    wait_from_zero(pool, m_scat[B], 16 * B_before(pool, n))
                    pool.sem_inc(m_pass, 1)

                @block.scalar
                def _(act):
                    def take(j, b, q, dst, half):
                        act.wait_ge(m_tr[b], job(j, q) + 1)
                        act.activation(dst[b][:, half * 4:half * 4 + 4, :], job_bank(b, q), ACT.Copy).then_inc(m_tr_act[b], 1)

                    def take_tokens(j, b, half):
                        take(j, b, TOKENS + half, xT_hi, half)

                    def sigmoid(b, j, half):
                        act.wait_ge(m_free[b], 6 * j + 2 * half + 1 + 2)
                        act.wait_ge(m_glu[b], 2 * j + half + START)
                        act.activation(sigm[b][:, :], gate_part[b][:, :], ACT.Sigmoid, scale=ALPHA).then_inc(m_sig[b], 1)

                    for i, (src, c) in enumerate(bias_raw):
                        if i == 0:
                            act.wait_ge(m_bias_raw, 16 * 2 * len(bias_raw))
                        act.activation(biases[:, c:c + FF], src[0:2 * E, :], ACT.Copy).then_inc(m_bias_hi, 1)
                    for b in (A, B):
                        act.sem_inc(m_sig[b], START)
                    act.activation(warm[:, 0:2], ident[:, 0:2], ACT.Copy).then_inc(m_warm, 1)
                    act.wait_ge(m_warm, 1)
                    n = n_items(act)
                    for half in range(2):
                        take_tokens(-1, A, half)
                        if_B(act, has_B(act, 0), lambda: take_tokens(-1, B, half), [(m_tr_act[B], 1, half)])
                    act.activation(warm[:, 0:1], warm[:, 0:1], ACT.Sigmoid)
                    with act.Fori(0, n) as j:
                        act.activation(warm[:, 1:2], warm[:, 1:2], ACT.Sigmoid)
                        two, two1 = has_B(act, j), has_B(act, j + 1)
                        for s in range(SUBS):
                            m = s + LEAD
                            act.wait_ge(m_usedB, SUBS * j + m + 1)
                            expert_hi(act, N0 + SUBS * j + m, m % SUBS, j + m // SUBS)
                            if s in (2, 6):
                                h = s // 4
                                sigmoid(A, j, h)
                                if_B(act, two, lambda: sigmoid(B, j, h), [(m_sig[B], 1, 2 * j + h + START)])
                            if s == 6:
                                take(j, A, ACT0, hidT_hi, 0)
                                if_B(act, two, lambda: take(j, B, ACT0, hidT_hi, 0), [(m_tr_act[B], 1, job(j, ACT0))])
                            if s == 8:
                                take(j, A, ACT1, hidT_hi, 1)
                                if_B(act, two, lambda: take(j, B, ACT1, hidT_hi, 1), [(m_tr_act[B], 1, job(j, ACT1))])
                            if s in (10, 11):
                                h = s - 10
                                take_tokens(j, A, h)
                                if_B(act, two1, lambda: take_tokens(j, B, h), [(m_tr_act[B], 1, job(j, TOKENS + h))])

                @block.vector
                def _(dve):
                    def take(j, b, q, hi, lo, half):
                        dve.wait_ge(m_tr_act[b], job(j, q) + 1)
                        dve.tensor_tensor(lo[b][:, half * 4:half * 4 + 4, :], job_bank(b, q),
                                          hi[b][:, half * 4:half * 4 + 4, :].bitcast(f32),
                                          ALU.subtract).then_inc(m_tr_dve[b], 1)

                    def take_tokens(j, b, half):
                        take(j, b, TOKENS + half, xT_hi, xT_lo, half)

                    def one_hot(b, e, first):
                        dve.tensor_tensor(onehot[b][:, :, :],
                                          slot_of[:, bass.ds(e, 1), :].rearrange("p o t -> p (o t)").unsqueeze(2)
                                          .to_broadcast([P, TT, P]),
                                          slots[:, bass.ds(first + b * P, P)].unsqueeze(1).to_broadcast([P, TT, P]),
                                          ALU.is_equal).then_inc(m_sel[b], 1)

                    def from_psum(b):
                        dve.tensor_copy(idx_next[b][:, :], bank(6)[:, 2 * b:2 * b + 1]).then_inc(m_next[b], 1)
                        dve.tensor_copy(gate_next[b][:, :], bank(6)[:, 2 * b + 1:2 * b + 2]).then_inc(m_next[b], 1)

                    def to_current(b):
                        dve.tensor_copy(idx_cur[b][:, :], idx_next[b][:, :]).then_inc(m_cur[b], 1)
                        dve.tensor_copy(gate_cur[b][:, :], gate_next[b][:, :]).then_inc(m_cur[b], 1)

                    def chunk_done(b, j, s):
                        if b == A:
                            dve.wait_ge(s_used, N0 + SUBS * j + s + 1)
                        else:
                            dve.wait_ge(m_usedB, SUBS * j + s + 1 + RING)

                    def clamp_gate(b, j, s, half):
                        chunk_done(b, j, s)
                        dve.tensor_scalar(gate_part[b][:, :], bank(2 * b), LIMIT, None, ALU.min).then_inc(m_free[b], 1)

                    def glu(b, j, half):
                        dve.wait_ge(m_sig[b], 2 * j + half + 1 + START)
                        dve.tensor_tensor(gate_part[b][:, :], gate_part[b][:, :], sigm[b][:, :], ALU.mult).then_inc(m_glu[b], 1)

                    def up(b, j, s, half):
                        chunk_done(b, j, s)
                        dve.tensor_scalar(up_part[b][:, :], bank(2 * b + 1), LIMIT, -LIMIT, ALU.min, ALU.max).then_inc(m_free[b], 1)
                        dve.wait_ge(m_free[b], 6 * j + 2 * half + 2 + 2)
                        dve.wait_ge(m_glu[b], 2 * j + half + 1 + START)
                        dve.scalar_tensor_tensor(hid[b][:, half * NC:(half + 1) * NC], up_part[b][:, :], 1.0,
                                                 gate_part[b][:, :], ALU.add, ALU.mult).then_inc(m_act[b], 1)

                    def down(b, j, s, half):
                        chunk_done(b, j, s)
                        dve.tensor_scalar(y[b][:, half * NC:(half + 1) * NC], bank(2 * b + half),
                                          gate_cur[b][:, 0:1], None, ALU.mult).then_inc(m_free[b], 1)

                    def pick_biases(e):
                        for g in range(2):
                            r = slice(g * E, (g + 1) * E)
                            dve.tensor_copy(pick[r, :], ident[r, bass.ds(e + g * E, 1)].to_broadcast([E, P])).then_inc(m_pick, 1)

                    dve.wait_ge(m_bias_hi, len(bias_raw))
                    for src, c in bias_raw:
                        dve.tensor_tensor(biases[E:2 * E, c:c + FF], src[E:2 * E, :],
                                          biases[E:2 * E, c:c + FF].bitcast(f32), ALU.subtract).then_inc(m_bias_lo, 1)
                    dve.wait_ge(m_bias_lo, len(bias_raw))
                    pick_biases(0)
                    for sems in (m_glu, m_act, m_cur):
                        for b in (A, B):
                            dve.sem_inc(sems[b], START)
                    n = n_items(dve)
                    for b in (A, B):
                        dve.sem_inc(m_free[b], 2)
                    dve.wait_ge(m_const, 16)
                    two0 = has_B(dve, 0)
                    one_hot(A, 0, 0)
                    if_B(dve, two0, lambda: one_hot(B, 0, 0), [(m_sel[B], 1, 0)])
                    dve.wait_ge(m_perm[A], 1)
                    dve.wait_ge(m_perm[B], 1)
                    from_psum(A)
                    if_B(dve, two0, lambda: from_psum(B), [(m_next[B], 2, 0)])
                    for half in range(2):
                        take_tokens(-1, A, half)
                        if_B(dve, two0, lambda: take_tokens(-1, B, half), [(m_tr_dve[B], 1, half)])
                    with dve.Fori(0, n) as j:
                        two = has_B(dve, j)
                        e1, first1, two1 = item(dve, j + 1)
                        before, before1 = B_before(dve, j), B_before(dve, j + 1)
                        for s in range(SUBS):
                            m = s + LEAD
                            expert_lo(dve, N0 + SUBS * j + m, m % SUBS)
                            if s == 0:
                                dve.wait_ge(m_perm[A], j + 1)
                                dve.wait_ge(m_perm[B], j + 1)
                                one_hot(A, e1, first1)
                                if_B(dve, two1, lambda: one_hot(B, e1, first1), [(m_sel[B], 1, j + 1)])
                            if s in (1, 5):
                                h = s // 4
                                clamp_gate(A, j, s, h)
                                if_B(dve, two, lambda: clamp_gate(B, j, s, h), [(m_free[B], 1, 6 * j + 2 * h + 2)])
                            if s in (2, 6):
                                h = s // 4
                                glu(A, j, h)
                                if_B(dve, two, lambda: glu(B, j, h), [(m_glu[B], 1, 2 * j + h + START)])
                            if s in (3, 7):
                                h = s // 4
                                up(A, j, s, h)
                                if_B(dve, two, lambda: up(B, j, s, h),
                                     [(m_free[B], 1, 6 * j + 2 * h + 3),
                                      (m_act[B], 1, 2 * j + h + START)])
                            if s == 3:
                                dve.wait_ge(m_next[A], 2 * j + 2)
                                dve.wait_ge(m_next[B], 2 * j + 2)
                                wait_from_zero(dve, m_scat[A], 16 * j)
                                wait_from_zero(dve, m_scat[B], 16 * before)
                                to_current(A)
                                if_B(dve, two, lambda: to_current(B), [(m_cur[B], 2, 2 * j + START)])
                            if s == 4:
                                dve.wait_ge(m_perm[A], j + 2)
                                dve.wait_ge(m_perm[B], j + 2)
                                dve.wait_ge(m_cur[A], 2 * j + 2 + START)
                                dve.wait_ge(m_cur[B], 2 * j + 2 + START)
                                dve.wait_ge(m_gat[A], 16 * j + 16)
                                wait_from_zero(dve, m_gat[B], 16 * before1)
                                from_psum(A)
                                if_B(dve, two1, lambda: from_psum(B), [(m_next[B], 2, 2 * j + 2)])
                            if s == 6:
                                take(j, A, ACT0, hidT_hi, hidT_lo, 0)
                                if_B(dve, two, lambda: take(j, B, ACT0, hidT_hi, hidT_lo, 0),
                                     [(m_tr_dve[B], 1, job(j, ACT0))])
                            if s == 8:
                                take(j, A, ACT1, hidT_hi, hidT_lo, 1)
                                if_B(dve, two, lambda: take(j, B, ACT1, hidT_hi, hidT_lo, 1),
                                     [(m_tr_dve[B], 1, job(j, ACT1))])
                            if s in (10, 11):
                                h = s - 10
                                take_tokens(j, A, h)
                                if_B(dve, two1, lambda: take_tokens(j, B, h), [(m_tr_dve[B], 1, job(j, TOKENS + h))])
                                down(A, j, s, h)
                                if_B(dve, two, lambda: down(B, j, s, h),
                                     [(m_free[B], 1, 6 * j + 4 + h + 2)])
                                if s == 10:
                                    dve.wait_ge(s_used, N0 + SUBS * j + s + 1)
                                    pick_biases(e1)

                @block.tensor
                def _(pe):
                    def transposes(j, b, q, src, half):
                        free = job(j, q) - (0 if b else 1)
                        if not (isinstance(free, int) and free <= 0):
                            pe.wait_ge(m_tr_act[b], free)
                            pe.wait_ge(m_tr_dve[b], free)
                        for i in range(4):
                            c = (half * 4 + i) * P
                            ins = pe.transpose(job_bank(b, q)[:, i, :], src[b][:, c:c + P], ident)
                        ins.then_inc(m_tr[b], 1)

                    def token_job(j, b, half, q16):
                        pe.wait_ge(m_gat[b], q16)
                        transposes(j, b, TOKENS + half, tokens, half)

                    def hidden_job(j, b, half):
                        pe.wait_ge(m_act[b], 2 * j + half + 1 + START)
                        transposes(j, b, ACT1 if half else ACT0, hid, half)

                    def permutation(b, e, q2):
                        pe.wait_ge(m_sel[b], q2)
                        for t in range(TT):
                            ins = pe.matmul(bank(6)[:, 2 * b:2 * b + 2], onehot[b][:, t, :],
                                            tok_gate[:, bass.ds(e, 1), t, :].rearrange("p o c -> p (o c)"),
                                            start=(t == 0), stop=(t == TT - 1))
                        ins.then_inc(m_perm[b], 1)

                    def sub_tile(b, j, s):
                        chunk, half = CHUNK_HALF[s]
                        x_hi, x_lo = (xT_hi, xT_lo) if chunk < 4 else (hidT_hi, hidT_lo)
                        if s == 0:
                            pe.wait_ge(m_tr_dve[b], 4 * j + 1)
                        if s == 1:
                            pe.wait_ge(m_tr_dve[b], 4 * j + 2)
                        if s == 8:
                            pe.wait_ge(m_tr_dve[b], job(j, ACT0) + 1)
                        if s == 10:
                            pe.wait_ge(m_tr_dve[b], job(j, ACT1) + 1)
                        if half == 0:
                            pe.wait_ge(m_free[b], 6 * j + chunk + 1)
                            pe.matmul(bank(2 * b + chunk % 2), pick[:, :], biases[:, bias_cols(chunk)], start=True, stop=False)
                        for k in range(HK):
                            kk = half * HK + k
                            ins = three_passes(pe, bank(2 * b + chunk % 2), x_hi[b][:, kk, :], x_lo[b][:, kk, :],
                                               whi[slot(s)][:, k, :], wlo[slot(s)][:, k, :], False, kk == KT - 1)
                        ins.then_inc(s_used if b == A else m_usedB, 1)

                    n = n_items(pe)
                    pe.sem_inc(m_usedB, RING)
                    pe.wait_ge(m_bias_hi, len(bias_raw))
                    pe.wait_ge(m_bias_lo, len(bias_raw))
                    two0 = has_B(pe, 0)
                    permutation(A, 0, 1)
                    if_B(pe, two0, lambda: permutation(B, 0, 1), [(m_perm[B], 1, 0)])
                    for half in range(2):
                        token_job(-1, A, half, 16)
                        if_B(pe, two0, lambda: token_job(-1, B, half, 16), [(m_tr[B], 1, half)])
                    with pe.Fori(0, n) as j:
                        two = has_B(pe, j)
                        pe.wait_ge(m_pick, 2 * j + 2)
                        for s in range(SUBS):
                            pe.wait_ge(s_lo, N0 + SUBS * j + s + 1)
                            pe.wait_ge(s_lo_pool, N0 + SUBS * j + s + 1)
                            sub_tile(A, j, s)
                            if_B(pe, two, lambda: sub_tile(B, j, s), [(m_usedB, 1, SUBS * j + s + RING)])
                            if s == 2:
                                e1, two1, before1 = expert_of(pe, j + 1), has_B(pe, j + 1), B_before(pe, j + 1)
                                pe.wait_ge(m_next[A], 2 * j + 2)
                                pe.wait_ge(m_next[B], 2 * j + 2)
                                permutation(A, e1, j + 2)
                                if_B(pe, two1, lambda: permutation(B, e1, j + 2), [(m_perm[B], 1, j + 1)])
                            if s == 5:
                                hidden_job(j, A, 0)
                                if_B(pe, two, lambda: hidden_job(j, B, 0), [(m_tr[B], 1, job(j, ACT0))])
                            if s == 8:
                                hidden_job(j, A, 1)
                                if_B(pe, two, lambda: hidden_job(j, B, 1), [(m_tr[B], 1, job(j, ACT1))])
                            if s in (9, 10):
                                token_job(j, A, s - 9, 16 * j + 32)
                                if_B(pe, two1, lambda: token_job(j, B, s - 9, 16 * before1 + 16),
                                     [(m_tr[B], 1, job(j, TOKENS + s - 9))])


block_kernel.stop = 0


_INS = ["x", "meta_tokens", "norm1_gain", "w_in", "b_forget", "fox_q_gain", "fox_k_gain", "swa_q_gain",
        "swa_k_gain", "swa_sinks", "w_fox_out", "w_swa_out", "w_out", "norm2_gain", "w_router", "b_router",
        "w_up", "b_up", "w_down", "b_down"]
_OUT = (1, T, D)


def kernel(**inputs):
    import concourse.bacc as bacc
    from concourse.bass_utils import run_bass_kernel_spmd

    nc = bacc.Bacc("TRN2", target_bir_lowering=False, num_devices=1)
    arrays, args = {}, []
    named = [(name, np.ascontiguousarray(inputs[name])) for name in _INS]
    named += [(f"const{i}", c) for i, c in enumerate(constants())]
    for name, a in named:
        arrays[f"{name}_dram"] = a
        args.append(nc.dram_tensor(f"{name}_dram", a.shape, mybir.dt.from_np(a.dtype), kind="ExternalInput").ap())
    result = nc.dram_tensor("out_dram", _OUT, mybir.dt.float32, kind="ExternalOutput").ap()
    block_kernel(nc, *args, result)
    r = run_bass_kernel_spmd(nc, [arrays], core_ids=[0])
    return r.results[0]["out_dram"]
```

```python
import numpy as np
import concourse.bass as bass
from concourse import mybir
from concourse.alu_op_type import AluOpType as ALU
from contextlib import ExitStack

P = 128
D = 1024
T = 1024
NM = 16
TT = T // P
KT = D // P
HD = 64
FH, SH, KVH = 8, 8, 2
FW, SW, KW = FH * HD, SH * HD, KVH * HD
WINDOW = 128
E = 32
TOPK = 4
FF = 1024
LIMIT, ALPHA, EPS, NEG = 7.0, 1.702, 1e-6, -1e30
C_FQ, C_FK, C_FV, C_FL = 0, FW, 2 * FW, 3 * FW
C_SQ = C_FL + FH
C_SK, C_SV = C_SQ + SW, C_SQ + SW + KW
C_GA = C_SV + KW
C_GB = C_GA + D
NC = 512
HK = 4
RING = 4
LEAD = 3
LO_DVE = 2
AUG = HD + 2
PAIR = 2 * P
MAX_ITEMS = E + T * TOPK // PAIR
TAIL = 32
GROUPS = P // TAIL
NJ = MAX_ITEMS + 2
SCALE = HD ** -0.5


def constants():
    p = np.arange(P)[:, None]
    f = np.arange(P)[None, :]
    ident = (p == f).astype(np.float32)
    causal = np.where(f <= p, 0.0, NEG).astype(np.float32)
    tri_incl = (p <= f).astype(np.float32)
    tri_strict = (p < f).astype(np.float32)
    ones = np.ones((P, P), np.float32)
    tok = (np.arange(TT)[None, :] * P + p).astype(np.float32)
    iota_e = np.broadcast_to(np.arange(E, dtype=np.float32), (P, E))
    part = (p // TAIL + np.array([[0, D // P // 2]])).astype(np.float32)
    cst = np.concatenate([ident, causal, tri_incl, tri_strict, ones, tok, iota_e, part], 1)

    def neg_dist(key_pos):
        dist = (NM + P + p) - key_pos
        return np.where((dist >= 0) & (dist < WINDOW), -dist, -1e34).astype(np.float32)

    near = neg_dist(NM + np.arange(2 * P)[None, :])
    first = np.concatenate([neg_dist(NM + P + np.arange(P)[None, :]), neg_dist(P + np.arange(NM)[None, :])], 1)
    dist = np.concatenate([near, first], 1)
    slots = np.broadcast_to(np.arange(T, dtype=np.float32), (P, T))
    return [np.ascontiguousarray(a, dtype=np.float32) for a in (cst, dist, slots)]


CONST_SHAPES = [(P, 5 * P + TT + E + 2), (P, 3 * P + NM), (P, T)]


def block_kernel(nc, x, meta_tokens, norm1_gain, w_in, b_forget, fox_q_gain, fox_k_gain, swa_q_gain,
                 swa_k_gain, swa_sinks, w_fox_out, w_swa_out, w_out, norm2_gain, w_router, b_router,
                 w_up, b_up, w_down, b_down, c_cst, c_dist, c_slots, out):
    f32, f32r, i32, u32 = mybir.dt.float32, mybir.dt.float32r, mybir.dt.int32, mybir.dt.uint32
    ACT = mybir.ActivationFunctionType
    AX = mybir.AxisListType

    x2 = x.rearrange("b s d -> (b s) d")
    out2 = out.rearrange("b s d -> (b s) d")
    win = w_in.rearrange("l d n -> (l d) n")
    wfo = w_fox_out.rearrange("l d n -> (l d) n")
    wso = w_swa_out.rearrange("l d n -> (l d) n")
    wout = w_out.rearrange("l d n -> (l d) n")
    wrt = w_router.rearrange("l d n -> (l d) n")
    wup = w_up.rearrange("l e d n -> (l e d) n")
    wdn = w_down.rearrange("l e d n -> (l e d) n")
    bup = b_up.rearrange("l e n -> (l e) n")
    bdn = b_down.rearrange("l e n -> (l e) n")

    def row(a):
        return a.rearrange("l n -> (l n)").partition_broadcast(P)

    fqT_d = nc.dram_tensor("fqT_d", (AUG, FH, T), f32, kind="Internal").ap()
    fkT_d = nc.dram_tensor("fkT_d", (AUG, FH, T + NM), f32, kind="Internal").ap()
    sqT_d = nc.dram_tensor("sqT_d", (P, SH // 2, T), f32, kind="Internal").ap()
    skT_d = nc.dram_tensor("skT_d", (P, KVH, T + NM), f32, kind="Internal").ap()
    v_d = nc.dram_tensor("v_d", (P, TT + 1, FW + KW), f32, kind="Internal").ap()
    gate_d = nc.dram_tensor("gate_d", (P, TT, 2 * D), f32, kind="Internal").ap()
    h2_d = nc.dram_tensor("h2_d", (T, D), f32, kind="Internal").ap()

    ctx = ExitStack()
    with ctx:
        def sb(stack, name, shape, dt=f32):
            return stack.enter_context(nc.sbuf_tensor(name, shape, dt))

        def sem(name):
            return ctx.enter_context(nc.semaphore(name))

        psum = ctx.enter_context(nc.psum_tensor("psum", [P, 8, NC], f32))

        def bank(b):
            return psum[:, b, :]

        raw = [sb(ctx, f"raw{i}", [P, HK, NC]) for i in range(RING)]
        whi = [sb(ctx, f"whi{i}", [P, HK, NC], f32r) for i in range(RING)]
        wlo = [sb(ctx, f"wlo{i}", [P, HK, NC], f32r) for i in range(RING)]
        cst = sb(ctx, "cst", list(CONST_SHAPES[0]))
        ident, causal, tri_incl, tri_strict, ones = (cst[:, i * P:(i + 1) * P] for i in range(5))
        tok_index = cst[:, 5 * P:5 * P + TT]
        iota_e = cst[:, 5 * P + TT:5 * P + TT + E]
        part_of = cst[:, 5 * P + TT + E:5 * P + TT + E + 2]
        slot_of = sb(ctx, "slot_of", [P, E, TT])
        tok_gate = sb(ctx, "tok_gate", [P, E, TT, 2])
        EXPERT, FIRST, KIND, ANY_BEFORE, ITEMS, LAST_KIND, FULL_BEFORE, TAILS_BEFORE = range(8)
        table = sb(ctx, "table", [1, 8, NJ], i32)

        s_raw = [sem(f"s_raw{i}") for i in range(RING)]
        s_hi = sem("s_hi")
        s_lo = sem("s_lo")
        s_lo_pool = sem("s_lo_pool")
        s_used = sem("s_used")
        s_const = sem("s_const")
        s_mm = sem("s_mm")
        s_tr = sem("s_tr")
        s_tr_act = sem("s_tr_act")
        s_tr_dve = sem("s_tr_dve")

        SMALL = FH + 2 * KW
        subs = []

        def chunk_subs(w, rows, cols):
            first = len(subs)
            for r0 in range(0, rows, HK * P):
                subs.append([(w[r0:r0 + HK * P, c:c + n].rearrange("(k p) n -> p k n", p=P), at, n)
                             for c, n, at in cols])
            return first, len(subs) - first, sum(n for _, n, _ in cols)

        proj = [("small", chunk_subs(win, D, [(C_FL, FH, 0), (C_SK, 2 * KW, FH)]))]
        for name, c in (("fk", C_FK), ("fq", C_FQ), ("fv", C_FV), ("sq", C_SQ)):
            proj.append((name, chunk_subs(win, D, [(c, NC, 0)])))
        for i in range(2 * D // NC):
            proj.append((f"g{i}", chunk_subs(win, D, [(C_GA + i * NC, NC, 0)])))
        N_PROJ = len(subs)
        outs = []
        for half in range(D // NC):
            for name, w in (("fox", wfo), ("swa", wso)):
                outs.append((name, half, chunk_subs(w, FW, [(half * NC, NC, 0)])))
        for half in range(D // NC):
            outs.append(("res", half, chunk_subs(wout, D, [(half * NC, NC, 0)])))
        N0 = len(subs)

        dma_count = [0] * RING
        raw_done = []
        for n, parts in enumerate(subs):
            dma_count[n % RING] += 16 * len(parts)
            raw_done.append(dma_count[n % RING])
        raw_base = list(dma_count)

        def load_sub(sp, n):
            if n >= RING:
                sp.wait_ge(s_lo, n - RING + 1)
                sp.wait_ge(s_lo_pool, n - RING + 1)
            for src, at, w in subs[n]:
                sp.dma_start(raw[n % RING][:, :, at:at + w], src).then_inc(s_raw[n % RING], 16)

        def sub_width(n):
            return sum(w for _, _, w in subs[n])

        def split_hi(act, n):
            act.wait_ge(s_raw[n % RING], raw_done[n])
            if n >= RING:
                act.wait_ge(s_used, n - RING + 1)
            w = sub_width(n)
            act.activation(whi[n % RING][:, :, 0:w], raw[n % RING][:, :, 0:w], ACT.Copy).then_inc(s_hi, 1)

        def split_lo(dve, n):
            dve.wait_ge(s_hi, n + 1)
            w = sub_width(n)
            dve.tensor_tensor(wlo[n % RING][:, 0:LO_DVE, 0:w], raw[n % RING][:, 0:LO_DVE, 0:w],
                              whi[n % RING][:, 0:LO_DVE, 0:w].bitcast(f32), ALU.subtract).then_inc(s_lo, 1)

        def split_lo_pool(pool, n):
            pool.wait_ge(s_hi, n + 1)
            w = sub_width(n)
            pool.tensor_tensor(wlo[n % RING][:, LO_DVE:HK, 0:w], raw[n % RING][:, LO_DVE:HK, 0:w],
                               whi[n % RING][:, LO_DVE:HK, 0:w].bitcast(f32), ALU.subtract).then_inc(s_lo_pool, 1)

        SUBS = 12
        splits_after = {k: [N_PROJ + RING + k - 1] if 1 <= k <= 4 else [] for k in range(6)}

        CHUNK_HALF = [(m // 2, m % 2) for m in range(8)] + [(4, 0), (5, 0), (4, 1), (5, 1)]

        def expert_source(e, m):
            chunk, half = CHUNK_HALF[m]
            w, c = (wup, (chunk % 2) * FF + (chunk // 2) * NC) if chunk < 4 else (wdn, (chunk - 4) * NC)
            rows = bass.ds(e * D + half * HK * P, HK * P)
            return w[rows, c:c + NC].rearrange("(k p) n -> p k n", p=P)

        def slot(m):
            return (N0 + m) % RING

        def raw_ready(m, j=0):
            return raw_base[slot(m)] + 16 * (m // RING + 1) + j * (16 * (SUBS // RING))

        def load_expert_sub(sp, n, e, m):
            sp.wait_ge(s_lo, n - RING + 1)
            sp.wait_ge(s_lo_pool, n - RING + 1)
            sp.dma_start(raw[slot(m)][:, :, :], expert_source(e, m)).then_inc(s_raw[slot(m)], 16)

        def expert_hi(act, n, m, j=0):
            act.wait_ge(s_raw[slot(m)], raw_ready(m, j))
            act.wait_ge(s_used, n - RING + 1)
            act.activation(whi[slot(m)][:, :, :], raw[slot(m)][:, :, :], ACT.Copy).then_inc(s_hi, 1)

        def expert_lo(dve, n, m):
            dve.wait_ge(s_hi, n + 1)
            dve.tensor_tensor(wlo[slot(m)][:, 0:LO_DVE, :], raw[slot(m)][:, 0:LO_DVE, :],
                              whi[slot(m)][:, 0:LO_DVE, :].bitcast(f32), ALU.subtract).then_inc(s_lo, 1)

        def expert_lo_pool(pool, n, m):
            pool.wait_ge(s_hi, n + 1)
            pool.tensor_tensor(wlo[slot(m)][:, LO_DVE:HK, :], raw[slot(m)][:, LO_DVE:HK, :],
                               whi[slot(m)][:, LO_DVE:HK, :].bitcast(f32), ALU.subtract).then_inc(s_lo_pool, 1)

        def three_passes(pe, dst, x_hi, x_lo, w_hi, w_lo, first, last):
            pe.matmul(dst, x_hi, w_hi, start=first, stop=False)
            pe.matmul(dst, x_hi, w_lo, start=False, stop=False)
            return pe.matmul(dst, x_lo, w_hi, start=False, stop=last)

        META = TT
        rows_of = [P] * TT + [NM]
        units = []
        for name, (n0, ns, w) in proj:
            for t in range(TT + 1 if name in ("small", "fk", "fv") else TT):
                units.append((name, t, n0, w))
        AUG_LAG = 2
        SMALLS = TT + 1

        def n_jobs(name):
            return {"fk": 2, "fq": 2, "sq": 1, "small": 1}.get(name, 0)

        plan = []
        for r in range(SMALLS):
            plan.append(("act_T", r))
            if r >= 1:
                plan.append(("mm", r - 1))
            if r >= 1 + AUG_LAG:
                plan.append(("head_T", r - 1 - AUG_LAG))
        plan.append(("mm", SMALLS - 1))
        plan += [("head_T", u) for u in range(SMALLS - 1 - AUG_LAG, SMALLS)]
        plan.append(("log_f", 0))
        pending = []
        for u in range(SMALLS, len(units)):
            plan.append(("mm", u))
            if u == SMALLS + 1:
                plan.append(("F", 0))
            pending.append(u)
            if len(pending) > AUG_LAG:
                plan.append(("head_T", pending.pop(0)))
        plan += [("head_T", u) for u in pending]
        plan = [s for s in plan if s[0] != "head_T" or n_jobs(units[s[1]][0])]
        staged = {}
        for s in plan:
            if s[0] == "head_T" or (s[0] == "mm" and (units[s[1]][0] == "small" or not n_jobs(units[s[1]][0]))):
                staged[s] = len(staged)
        job0 = {}
        n_tr = 0
        for s in plan:
            if s[0] in ("act_T", "head_T"):
                job0[s] = n_tr
                n_tr += 2 if s[0] == "act_T" else n_jobs(units[s[1]][0])
        TR1 = n_tr
        dve_jobs = [job0[s] + g for s in plan if s[0] == "act_T" for g in range(2)]
        NORMED = ("fk", "fq", "sq")
        by_dve = [u for u in range(len(units)) if units[u][0] in NORMED + ("small",)]
        by_act = [u for u in range(len(units)) if units[u][0] not in NORMED + ("small",)]
        normed = [u for u in range(len(units)) if n_jobs(units[u][0])]
        last_of_chunk = {u for u in range(len(units)) if u + 1 == len(units) or units[u + 1][0] != units[u][0]}
        first_of_chunk = {u for u in range(len(units)) if u == 0 or units[u - 1][0] != units[u][0]}

        s_x = [sem("s_x0"), sem("s_x1")]
        s_ss = sem("s_ss")
        s_ms = sem("s_ms")
        s_rt = sem("s_rt")
        s_ri = sem("s_ri")
        s_h = sem("s_h")
        s_free_dve = sem("s_free_dve")
        s_free_act = sem("s_free_act")
        s_qsq = sem("s_qsq")
        s_qms = sem("s_qms")
        s_qrt = sem("s_qrt")
        s_qri = sem("s_qri")
        s_qt = sem("s_qt")
        s_aug = sem("s_aug")
        s_stage = sem("s_stage")
        s_out = [sem(f"s_out{i}") for i in range(3)]
        s_z = sem("s_z")
        s_lf = sem("s_lf")
        s_F = sem("s_F")
        s_Fsb = sem("s_Fsb")
        s_gain = sem("s_gain")

        with ExitStack() as st:
            hT_hi = sb(st, "hT_hi", [P, KT, T + NM], f32r)
            hT_lo = sb(st, "hT_lo", [P, KT, T + NM], f32r)
            xin = [sb(st, f"xin{i}", [P, D]) for i in range(2)]
            g1 = sb(st, "g1", [P, D])
            squares = sb(st, "squares", [P, NC])
            scaled = sb(st, "scaled", [P, NC])
            aug = [sb(st, f"aug{i}", [P, FH, AUG]) for i in range(3)]
            stage = [sb(st, f"stage{i}", [P, D]) for i in range(3)]
            gains = sb(st, "gains", [P, 4, HD])
            bf = sb(st, "bf", [P, FH])
            ss = sb(st, "ss", [P, 4 * SMALLS])
            qss = sb(st, "qss", [P, 4, FH])
            z = sb(st, "z", [P, 4, SMALLS, FH])
            Fs = sb(st, "Fs", [P, 2, SMALLS, FH])

            gain_of = {"fq": 0, "fk": 1, "sq": 2, "small": 3}
            n_stage = [0]

            def heads_of(name):
                return KVH if name == "small" else FH

            def unit_cols(name):
                return (FH, FH + KW) if name == "small" else (0, NC)

            with nc.Block() as block:
                @block.sync
                def _(sp):
                    for n in range(N_PROJ):
                        load_sub(sp, n)

                @block.gpsimd
                def _(pool):
                    pool.dma_start(xin[0][:, :], x2[0:P, :]).then_inc(s_x[0], 16)
                    pool.dma_start(xin[1][:, :], x2[P:2 * P, :]).then_inc(s_x[1], 16)
                    pool.dma_start(g1[:, :], row(norm1_gain)).then_inc(s_const, 16)
                    pool.dma_start(cst[:, :], c_cst).then_inc(s_const, 16)
                    for i, g in enumerate((fox_q_gain, fox_k_gain, swa_q_gain, swa_k_gain)):
                        pool.dma_start(gains[:, i, :], row(g)).then_inc(s_const, 16)
                    pool.dma_start(bf[:, :], row(b_forget)).then_inc(s_const, 16)
                    for n in range(2):
                        split_lo_pool(pool, n)
                    for s in plan:
                        if s[0] == "act_T" and s[1] + 2 < SMALLS:
                            t = s[1] + 2
                            pool.wait_ge(s_tr, job0[("act_T", s[1])] + 2)
                            src = x2[t * P:(t + 1) * P, :] if t < META else meta_tokens
                            pool.dma_start(xin[t % 2][0:rows_of[t], :], src).then_inc(s_x[t % 2], 16)
                        if s[0] == "mm" and s[1] in first_of_chunk:
                            n0 = units[s[1]][2]
                            for n in range(n0 + 2, min(n0 + RING, N_PROJ)):
                                split_lo_pool(pool, n)

                @block.scalar
                def _(act):
                    def norm_front(t):
                        n = rows_of[t]
                        act.wait_ge(s_x[t % 2], 16 * (t // 2 + 1))
                        if t >= 1:
                            act.wait_ge(s_ss, t)
                        act.activation(psum[0:n, 6:8, :].rearrange("p b n -> p (b n)"), xin[t % 2][0:n, :], ACT.Square,
                                       accum_out=ss[0:n, t:t + 1]).then_inc(s_ss, 1)
                        act.wait_ge(s_ms, t + 1)
                        act.activation(ss[0:n, 2 * SMALLS + t:2 * SMALLS + t + 1],
                                       ss[0:n, SMALLS + t:SMALLS + t + 1], ACT.Sqrt).then_inc(s_rt, 1)

                    def to_dram(parts):
                        k = n_stage[0]
                        act.wait_ge(s_stage, k + 1)
                        (dst, src), = parts
                        act.dma_start(dst, src).then_inc(s_out[k % 3], 16)
                        n_stage[0] += 1

                    def stage_free():
                        k = n_stage[0]
                        if k >= 3:
                            act.wait_ge(s_out[k % 3], 16 * (k // 3))
                        return stage[k % 3]

                    act.wait_ge(s_const, 16 * 7)
                    for i in (0, 2):
                        act.activation(gains[:, i, :], gains[:, i, :], ACT.Copy, scale=SCALE).then_inc(s_gain, 1)
                    norm_front(0)
                    for n in range(2):
                        split_hi(act, n)
                    n_unit = 0
                    for s, i in plan:
                        if s == "act_T":
                            if i + 1 < SMALLS:
                                norm_front(i + 1)
                            n = rows_of[i]
                            for g in range(2):
                                j = job0[(s, i)] + g
                                act.wait_ge(s_tr, j + 1)
                                act.activation(hT_hi[:, g * 4:g * 4 + 4, i * P:i * P + n],
                                               bank(4 + j % 2).rearrange("p (k n) -> p k n", k=4)[:, :, 0:n],
                                               ACT.Copy).then_inc(s_tr_act, 1)
                        elif s == "mm":
                            name, t, n0, w = units[i]
                            n = rows_of[t]
                            if i in first_of_chunk:
                                for m in range(n0 + 2, min(n0 + RING, N_PROJ)):
                                    split_hi(act, m)
                            act.wait_ge(s_mm, i + 1)
                            src = bank(i % 4)[0:n, 0:w]
                            if name in gain_of:
                                k = normed.index(i)
                                c0, c1 = unit_cols(name)
                                if k >= 1:
                                    act.wait_ge(s_qms, k)
                                act.activation(squares[0:n, 0:c1 - c0], src[:, c0:c1], ACT.Square).then_inc(s_qsq, 1)
                                if name == "small":
                                    dst = stage_free()
                                    act.activation(dst[0:n, 0:KW], src[:, FH + KW:w], ACT.Copy).then_inc(s_stage, 1)
                                    to_dram([(v_d[0:n, t, FW:FW + KW], dst[0:n, 0:KW])])
                                act.wait_ge(s_qms, k + 1)
                                nh = heads_of(name)
                                act.activation(qss[0:n, 2, 0:nh], qss[0:n, 1, 0:nh], ACT.Sqrt).then_inc(s_qrt, 1)
                            else:
                                dst = stage_free()
                                func = ACT.Copy if name == "fv" else ACT.Sigmoid
                                act.activation(dst[0:n, 0:NC], src, func).then_inc(s_stage, 1)
                                act.wait_ge(s_stage, n_stage[0] + 1)
                                act.sem_inc(s_free_act, 1)
                                if name == "fv":
                                    to_dram([(v_d[0:n, t, 0:FW], dst[0:n, 0:NC])])
                                else:
                                    c = int(name[1:]) * NC
                                    to_dram([(gate_d[:, t, c:c + NC], dst[:, 0:NC])])
                        elif s == "log_f":
                            act.wait_ge(s_z, SMALLS + 2)
                            act.activation(z[:, 1], z[:, 1], ACT.Exp, scale=-1.0).then_inc(s_lf, 1)
                            act.wait_ge(s_z, SMALLS + 3)
                            act.activation(z[:, 1], z[:, 1], ACT.Ln).then_inc(s_lf, 1)
                        elif s == "head_T":
                            name, t, n0, w = units[i]
                            n = rows_of[t]
                            j = job0[(s, i)]
                            dst = stage_free()
                            for g in range(n_jobs(name)):
                                act.wait_ge(s_tr, j + g + 1)
                                src = bank(4 + (j + g) % 2).rearrange("p (k n) -> p k n", k=4)
                                if name in ("fk", "fq"):
                                    view = dst[0:AUG, 0:FH * n].rearrange("p (h n) -> p h n", n=n)
                                    ins = act.activation(view[:, g * 4:g * 4 + 4, :], src[0:AUG, :, 0:n], ACT.Copy)
                                elif name == "sq":
                                    view = dst[:, 0:4 * n].rearrange("p (h n) -> p h n", n=n)
                                    ins = act.activation(view, src[:, :, 0:n], ACT.Copy)
                                else:
                                    view = dst[:, 0:KVH * n].rearrange("p (h n) -> p h n", n=n)
                                    ins = act.activation(view, src[:, 0:KVH, 0:n], ACT.Copy)
                                ins.then_inc(s_tr_act, 1)
                            act.wait_ge(s_tr_act, j + n_jobs(name))
                            act.sem_inc(s_stage, 1)
                            dram = {"fk": fkT_d, "fq": fqT_d, "sq": sqT_d, "small": skT_d}[name]
                            to_dram([(dram[:, :, t * P:t * P + n], view)])

                @block.vector
                def _(dve):
                    def norm_front(t):
                        n = rows_of[t]
                        dve.wait_ge(s_ss, t + 1)
                        dve.tensor_scalar(ss[0:n, SMALLS + t:SMALLS + t + 1], ss[0:n, t:t + 1], 1.0 / D, EPS,
                                          ALU.mult, ALU.add).then_inc(s_ms, 1)
                        dve.wait_ge(s_rt, t + 1)
                        dve.reciprocal(ss[0:n, 3 * SMALLS + t:3 * SMALLS + t + 1],
                                       ss[0:n, 2 * SMALLS + t:2 * SMALLS + t + 1]).then_inc(s_ri, 1)
                        dve.wait_ge(s_ri, t + 1)
                        dve.scalar_tensor_tensor(xin[t % 2][0:n, :], xin[t % 2][0:n, :],
                                                 ss[0:n, 3 * SMALLS + t:3 * SMALLS + t + 1], g1[0:n, :],
                                                 ALU.mult, ALU.mult).then_inc(s_h, 1)

                    dve.memset(z[:, 0], 0.0).then_inc(s_z, 1)
                    dve.wait_ge(s_z, 1)
                    dve.wait_ge(s_const, 16 * 7)
                    dve.wait_ge(s_gain, 2)
                    norm_front(0)
                    for n in range(2):
                        split_lo(dve, n)
                    for s, i in plan:
                        if s == "act_T":
                            if i + 1 < SMALLS:
                                norm_front(i + 1)
                            n = rows_of[i]
                            for g in range(2):
                                j = job0[(s, i)] + g
                                dve.wait_ge(s_tr_act, j + 1)
                                dve.tensor_tensor(hT_lo[:, g * 4:g * 4 + 4, i * P:i * P + n],
                                                  bank(4 + j % 2).rearrange("p (k n) -> p k n", k=4)[:, :, 0:n],
                                                  hT_hi[:, g * 4:g * 4 + 4, i * P:i * P + n].bitcast(f32),
                                                  ALU.subtract).then_inc(s_tr_dve, 1)
                        elif s == "mm":
                            name, t, n0, w = units[i]
                            n = rows_of[t]
                            if i in first_of_chunk:
                                for m in range(n0 + 2, min(n0 + RING, N_PROJ)):
                                    split_lo(dve, m)
                            if name not in gain_of:
                                continue
                            k = normed.index(i)
                            nh = heads_of(name)
                            c0, c1 = unit_cols(name)
                            dve.wait_ge(s_qsq, k + 1)
                            dve.tensor_reduce(qss[0:n, 0, 0:nh],
                                              squares[0:n, 0:c1 - c0].rearrange("p (h d) -> p h d", d=HD),
                                              AX.X, ALU.add).then_inc(s_qri, 1)
                            dve.wait_ge(s_qri, 3 * k + 1)
                            dve.tensor_scalar(qss[0:n, 1, 0:nh], qss[0:n, 0, 0:nh], 1.0 / HD, EPS,
                                              ALU.mult, ALU.add).then_inc(s_qms, 1)
                            if name == "small":
                                dve.wait_ge(s_stage, staged[(s, i)] + 1)
                                dve.tensor_tensor(z[0:n, 0, t, :], bank(i % 4)[0:n, 0:FH], bf[0:n, :],
                                                  ALU.add).then_inc(s_z, 1)
                            dve.wait_ge(s_qrt, k + 1)
                            dve.reciprocal(qss[0:n, 3, 0:nh], qss[0:n, 2, 0:nh]).then_inc(s_qri, 1)
                            dve.wait_ge(s_qri, 3 * k + 2)
                            dve.tensor_tensor(scaled[0:n, 0:c1 - c0].rearrange("p (h d) -> p h d", d=HD),
                                              bank(i % 4)[0:n, c0:c1].rearrange("p (h d) -> p h d", d=HD),
                                              qss[0:n, 3, 0:nh].unsqueeze(2).to_broadcast([n, nh, HD]),
                                              ALU.mult).then_inc(s_free_dve, 1)
                            dve.wait_ge(s_free_dve, k + 1)
                            if k >= 3:
                                old = normed[k - 3]
                                dve.wait_ge(s_tr, job0[("head_T", old)] + n_jobs(units[old][0]))
                            g = gains[0:n, gain_of[name], :]
                            src = scaled[0:n, 0:c1 - c0].rearrange("p (h d) -> p h d", d=HD)
                            a = aug[k % 3]
                            if name == "small":
                                dup = a[0:n, :, :].rearrange("p h d -> p (h d)")[:, 0:2 * KW] \
                                    .rearrange("p (g c d) -> p g c d", g=KVH, c=2)
                                for c in range(2):
                                    ins = dve.tensor_tensor(dup[:, :, c, :], src, g.unsqueeze(1).to_broadcast([n, KVH, HD]),
                                                            ALU.mult)
                                    if c == 0:
                                        ins.then_inc(s_qri, 1)
                                ins.then_inc(s_aug, 1)
                            elif name == "sq":
                                ins = dve.tensor_tensor(
                                    a[0:n, :, :].rearrange("p h d -> p (h d)")[:, 0:NC].rearrange("p (h d) -> p h d", d=HD),
                                    src, g.unsqueeze(1).to_broadcast([n, FH, HD]), ALU.mult)
                                ins.then_inc(s_aug, 1)
                                dve.sem_inc(s_qri, 1)
                            else:
                                dve.tensor_tensor(a[0:n, :, 0:HD], src, g.unsqueeze(1).to_broadcast([n, FH, HD]),
                                                  ALU.mult).then_inc(s_qri, 1)
                                one, f = (HD, HD + 1) if name == "fk" else (HD + 1, HD)
                                dve.memset(a[0:n, :, one:one + 1], 1.0).then_inc(s_qt, 1)
                                dve.tensor_copy(a[0:n, :, f:f + 1],
                                                Fs[0:n, 1 if name == "fk" else 0, t, :].unsqueeze(2)).then_inc(s_qt, 1)
                                kk = k - SMALLS
                                dve.wait_ge(s_qt, 2 * kk + 2)
                                dve.wait_ge(s_qri, 3 * k + 3)
                                dve.sem_inc(s_aug, 1)
                        elif s == "log_f":
                            dve.wait_ge(s_z, SMALLS + 1)
                            dve.scalar_tensor_tensor(z[:, 1], z[:, 0], -1.0, z[:, 0], ALU.mult, ALU.max).then_inc(s_z, 1)
                            dve.wait_ge(s_lf, 1)
                            dve.tensor_scalar(z[:, 1], z[:, 1], 1.0, None, ALU.add).then_inc(s_z, 1)
                            dve.wait_ge(s_lf, 2)
                            dve.scalar_tensor_tensor(z[:, 2], z[:, 0], 0.0, z[:, 1], ALU.min, ALU.subtract).then_inc(s_z, 1)
                            dve.wait_ge(s_F, 1)
                            fps = bank(6)[:, 0:SMALLS * FH].rearrange("p (t h) -> p t h", h=FH)
                            dve.tensor_copy(Fs[:, 0, 0:TT, :], fps[:, 0:TT, :]).then_inc(s_Fsb, 1)
                            dve.tensor_copy(Fs[0:NM, 0, META, :], fps[0:NM, META, :]).then_inc(s_Fsb, 1)
                            dve.tensor_scalar(Fs[:, 1, 0:TT, :], fps[:, 0:TT, :], -1.0, None, ALU.mult).then_inc(s_Fsb, 1)
                            dve.tensor_scalar(Fs[0:NM, 1, META, :], fps[0:NM, META, :], -1.0, None,
                                              ALU.mult).then_inc(s_Fsb, 1)
                            dve.wait_ge(s_Fsb, 4)

                @block.tensor
                def _(pe):
                    def job_free(j):
                        if j >= 2:
                            pe.wait_ge(s_tr_act, j - 1)
                            if j - 2 in dve_jobs:
                                pe.wait_ge(s_tr_dve, dve_jobs.index(j - 2) + 1)

                    pe.wait_ge(s_const, 16 * 7)
                    for s, i in plan:
                        if s == "act_T":
                            n = rows_of[i]
                            pe.wait_ge(s_h, i + 1)
                            for g in range(2):
                                j = job0[(s, i)] + g
                                job_free(j)
                                for k in range(4):
                                    c = (g * 4 + k) * P
                                    ins = pe.transpose(bank(4 + j % 2)[:, k * P:k * P + n],
                                                       xin[i % 2][0:n, c:c + P], ident[0:n, 0:n])
                                ins.then_inc(s_tr, 1)
                        elif s == "mm":
                            name, t, n0, w = units[i]
                            n = rows_of[t]
                            if i in first_of_chunk:
                                pe.wait_ge(s_lo, n0 + 2)
                                pe.wait_ge(s_lo_pool, n0 + 2)
                            if i < SMALLS:
                                pe.wait_ge(s_tr_dve, 2 * (t + 1))
                            if i >= 4:
                                if (i - 4) in by_dve:
                                    pe.wait_ge(s_free_dve, by_dve.index(i - 4) + 1)
                                    if units[i - 4][0] == "small":
                                        pe.wait_ge(s_z, i - 4 + 2)
                                        pe.wait_ge(s_stage, staged[("mm", i - 4)] + 1)
                                else:
                                    pe.wait_ge(s_free_act, by_act.index(i - 4) + 1)
                            dst = bank(i % 4)[0:n, 0:w]
                            for k in range(KT):
                                slot = (n0 + k // HK) % RING
                                ins = three_passes(pe, dst, hT_hi[:, k, t * P:t * P + n], hT_lo[:, k, t * P:t * P + n],
                                                   whi[slot][:, k % HK, 0:w], wlo[slot][:, k % HK, 0:w],
                                                   k == 0, k == KT - 1)
                                if i in last_of_chunk and k == HK - 1:
                                    ins.then_inc(s_used, 1)
                            ins.then_inc(s_mm, 1)
                            if i in last_of_chunk:
                                pe.wait_ge(s_mm, i + 1)
                                pe.sem_inc(s_used, 1)
                        elif s == "F":
                            pe.wait_ge(s_z, SMALLS + 4)
                            lf = z[:, 2]
                            for t in range(TT):
                                dst = bank(6)[:, t * FH:(t + 1) * FH]
                                pe.matmul(dst, ones[0:NM, :], lf[0:NM, META, :], start=True, stop=False)
                                for j in range(t):
                                    pe.matmul(dst, ones, lf[:, j, :], start=False, stop=False)
                                pe.matmul(dst, tri_incl, lf[:, t, :], start=False, stop=True)
                            pe.matmul(bank(6)[0:NM, META * FH:(META + 1) * FH], tri_incl[0:NM, 0:NM],
                                      lf[0:NM, META, :], start=True, stop=True).then_inc(s_F, 1)
                        elif s == "head_T":
                            name, t, n0, w = units[i]
                            n = rows_of[t]
                            k = normed.index(i)
                            pe.wait_ge(s_aug, k + 1)
                            a = aug[k % 3]
                            flat = a[0:n, :, :].rearrange("p h d -> p (h d)")
                            for g in range(n_jobs(name)):
                                j = job0[(s, i)] + g
                                job_free(j)
                                dst = bank(4 + j % 2)
                                if name in ("fk", "fq"):
                                    for h in range(4):
                                        ins = pe.transpose(dst[0:AUG, h * P:h * P + n], a[0:n, g * 4 + h, :], ident[0:n, 0:n])
                                else:
                                    for h in range(4 if name == "sq" else KVH):
                                        ins = pe.transpose(dst[:, h * P:h * P + n], flat[:, h * P:(h + 1) * P],
                                                           ident[0:n, 0:n])
                                ins.then_inc(s_tr, 1)
            N_STAGE = n_stage[0]

        def stage_count(i):
            return 16 * ((N_STAGE - i + 2) // 3)

        rest = ctx.enter_context(ExitStack())
        token_major = sb(rest, "token_major", [P, TT, D])

        ORDER = [7, 0, 6, 1, 5, 2, 4, 3]
        att = [(h, i) for h in range(FH + SH) for i in ORDER]
        META_AT = T

        def key_blocks(h, i):
            if h < FH:
                return [(b * P, P, b) for b in range(i + 1)] + [(META_AT, NM, META)]
            if i == 0:
                return [(0, P, 0), (META_AT, NM, META)]
            return [((i - 1) * P, P, i - 1), (i * P, P, i)]

        att_jobs = []
        jobs_of = []
        for u, (h, i) in enumerate(att):
            blocks = list(enumerate(key_blocks(h, i)))
            jobs_of.append([])
            for g in range(0, len(blocks), 4):
                jobs_of[u].append(len(att_jobs))
                att_jobs.append((u, blocks[g:g + 4]))

        PT_RING = 4
        s_kq = [sem("s_kq0"), sem("s_kq1")]
        s_kv = sem("s_kv")
        s_S = sem("s_S")
        s_msk = sem("s_msk")
        s_mx = sem("s_mx")
        s_nm = sem("s_nm")
        s_exp = sem("s_exp")
        s_esk = sem("s_esk")
        s_pt = sem("s_pt")
        s_pt_act = sem("s_pt_act")
        s_norm = sem("s_norm")
        s_pv = sem("s_pv")
        s_den = sem("s_den")
        s_O = sem("s_O")

        with ExitStack() as st:
            kT = [sb(st, f"kT{i}", [P, T + NM]) for i in range(2)]
            qT = [sb(st, f"qT{i}", [P, T]) for i in range(2)]
            skT = sb(st, "skT", [P, KVH, T + NM])
            V = sb(st, "V", [P, TT + 1, FW + KW])
            probs = [sb(st, f"probs{i}", [P, T + NM]) for i in range(2)]
            biased = [sb(st, f"biased{i}", [P, 2 * P]) for i in range(2)]
            probsT = [sb(st, f"probsT{i}", [P, 4, P]) for i in range(PT_RING)]
            dist = sb(st, "dist", list(CONST_SHAPES[1]))
            sinks = sb(st, "sinks", [P, SH])
            row_max = sb(st, "row_max", [P, 2])
            neg_max = sb(st, "neg_max", [P, 2])
            row_sum = sb(st, "row_sum", [P, FH + SH, TT])
            sink_exp = sb(st, "sink_exp", [P, SH, TT])
            total = sb(st, "total", [P, 2])
            recip = sb(st, "recip", [P, 2])
            GROUP = NC // P
            groups = [sorted(ORDER[g:g + GROUP]) for g in range(0, TT, GROUP)]

            score_buf = [psum[:, 0:3, :].rearrange("p b n -> p (b n)"), psum[:, 3:5, :].rearrange("p b n -> p (b n)")]

            def width(u):
                return sum(n for _, n, _ in key_blocks(*att[u]))

            def kq_slot(h):
                return h if h < FH else FH + (h - FH) // 2

            def job_done(eng, j):
                eng.wait_ge(s_pt_act, j + 1)

            with nc.Block() as block:
                @block.sync
                def _(sp):
                    for i in range(3):
                        sp.wait_ge(s_out[i], stage_count(i))
                    for k in range(FH + SH // 2):
                        if k >= 2:
                            last_head = k - 2 if k - 2 < FH else FH + 2 * (k - 2 - FH) + 1
                            sp.wait_ge(s_S, TT * (last_head + 1))
                        if k < FH:
                            sp.dma_start(kT[k % 2][0:AUG, :], fkT_d[:, k, :]).then_inc(s_kq[k % 2], 16)
                            sp.dma_start(qT[k % 2][0:AUG, :], fqT_d[:, k, :]).then_inc(s_kq[k % 2], 16)
                        else:
                            sp.dma_start(qT[k % 2][:, :], sqT_d[:, k - FH, :]).then_inc(s_kq[k % 2], 16)
                        if k == 0:
                            sp.dma_start(V[:, 0:TT, :], v_d[:, 0:TT, :]).then_inc(s_kv, 16)
                            sp.dma_start(V[0:NM, META, :], v_d[0:NM, META, :]).then_inc(s_kv, 16)
                            sp.dma_start(skT[:, :, :], skT_d).then_inc(s_kv, 16)
                            sp.dma_start(dist[:, :], c_dist).then_inc(s_kv, 16)
                            sp.dma_start(sinks[:, :], row(swa_sinks)).then_inc(s_kv, 16)
                        if k == 1:
                            for n in range(N_PROJ, N_PROJ + RING):
                                load_sub(sp, n)

                @block.gpsimd
                def _(pool):
                    for n in range(N_PROJ, N_PROJ + RING):
                        split_lo_pool(pool, n)

                @block.scalar
                def _(act):
                    def exponential(u):
                        h, i = att[u]
                        n = width(u)
                        act.wait_ge(s_nm, u + 1)
                        if u >= 2:
                            act.wait_ge(s_pt, jobs_of[u - 2][-1] + 1)
                        src = score_buf[u % 2][:, 0:n] if h < FH else biased[u % 2][:, 0:n]
                        act.activation(probs[u % 2][:, 0:n], src, ACT.Exp, bias=neg_max[:, u % 2:u % 2 + 1],
                                       accum_out=row_sum[:, h, i:i + 1]).then_inc(s_exp, 1)
                        if h >= FH:
                            act.activation(sink_exp[:, h - FH, i:i + 1], sinks[:, h - FH:h - FH + 1], ACT.Exp,
                                           bias=neg_max[:, u % 2:u % 2 + 1]).then_inc(s_esk, 1)

                    act.wait_ge(s_kv, 16 * 5)
                    exponential(0)
                    for u in range(len(att)):
                        if u % 8 == 2 and u // 8 < RING:
                            split_hi(act, N_PROJ + u // 8)
                        if u + 1 < len(att):
                            exponential(u + 1)
                        for j in jobs_of[u]:
                            n = len(att_jobs[j][1])
                            act.wait_ge(s_pt, j + 1)
                            if j >= PT_RING:
                                act.wait_ge(s_pv, j - PT_RING + 1)
                            act.activation(probsT[j % PT_RING][:, 0:n, :],
                                           bank(5 + j % 2).rearrange("p (b q) -> p b q", b=4)[:, 0:n, :],
                                           ACT.Copy).then_inc(s_pt_act, 1)

                @block.vector
                def _(dve):
                    def softmax_front(u):
                        h, i = att[u]
                        n = width(u)
                        S = score_buf[u % 2]
                        dve.wait_ge(s_S, u + 1)
                        if h < FH:
                            own = S[:, i * P:(i + 1) * P]
                            dve.tensor_tensor(own, own, causal, ALU.add).then_inc(s_msk, 1)
                            src = S[:, 0:n]
                        else:
                            slope = 2.0 ** (-8.0 * (h - FH + 1) / SH)
                            bias = dist[:, 0:2 * P] if i else dist[:, 2 * P:3 * P + NM]
                            if u >= 2:
                                dve.wait_ge(s_exp, u - 1)
                            dve.scalar_tensor_tensor(biased[u % 2][:, 0:n], bias, slope, S[:, 0:n],
                                                     ALU.mult, ALU.add).then_inc(s_msk, 1)
                            src = biased[u % 2][:, 0:n]
                        dve.wait_ge(s_msk, u + 1)
                        dve.tensor_reduce(row_max[:, u % 2:u % 2 + 1], src, AX.X, ALU.max).then_inc(s_mx, 1)
                        dve.wait_ge(s_mx, u + 1)
                        if u >= 2:
                            dve.wait_ge(s_exp, u - 1)
                            if h >= FH and u - 2 >= FH * TT:
                                dve.wait_ge(s_esk, u - 2 - FH * TT + 1)
                        if h < FH:
                            dve.tensor_scalar(neg_max[:, u % 2:u % 2 + 1], row_max[:, u % 2:u % 2 + 1], -1.0, None,
                                              ALU.mult).then_inc(s_nm, 1)
                        else:
                            dve.tensor_scalar(neg_max[:, u % 2:u % 2 + 1], row_max[:, u % 2:u % 2 + 1],
                                              sinks[:, h - FH:h - FH + 1], -1.0, ALU.max, ALU.mult).then_inc(s_nm, 1)

                    den = 0

                    def normalise(u, den):
                        h, i = att[u]
                        b = u % 2
                        dve.wait_ge(s_exp, u + 1)
                        if u >= 2:
                            dve.wait_ge(s_norm, u - 1)
                        of = row_sum[:, h, i:i + 1]
                        if h >= FH:
                            dve.wait_ge(s_esk, u - FH * TT + 1)
                            dve.tensor_tensor(total[:, b:b + 1], of, sink_exp[:, h - FH, i:i + 1], ALU.add).then_inc(s_den, 1)
                            den += 1
                            dve.wait_ge(s_den, den)
                            of = total[:, b:b + 1]
                        dve.reciprocal(recip[:, b:b + 1], of).then_inc(s_den, 1)
                        den += 1
                        dve.wait_ge(s_den, den)
                        p = probs[b][:, 0:width(u)]
                        dve.tensor_scalar(p, p, recip[:, b:b + 1], None, ALU.mult).then_inc(s_norm, 1)
                        return den

                    def store(u):
                        h, i = att[u]
                        tiles = groups[0] if i in groups[0] else groups[1]
                        rows = slice(HD * (h % 2), HD * (h % 2) + HD)
                        dve.wait_ge(s_pv, jobs_of[u][-1] + 1)
                        at = 0
                        while at < GROUP:
                            n = 1
                            while at + n < GROUP and tiles[at + n] == tiles[at] + n:
                                n += 1
                            ins = dve.tensor_copy(token_major[rows, h // 2, tiles[at] * P:(tiles[at] + n) * P],
                                                  bank(7)[rows, at * P:(at + n) * P])
                            at += n
                        ins.then_inc(s_O, 1)

                    dve.wait_ge(s_kv, 16 * 5)
                    softmax_front(0)
                    softmax_front(1)
                    for u in range(len(att)):
                        h, i = att[u]
                        if u % 8 == 2 and u // 8 < RING:
                            split_lo(dve, N_PROJ + u // 8)
                        den = normalise(u, den)
                        if u + 2 < len(att):
                            softmax_front(u + 2)
                        if u % GROUP == 0 and u and h < FH:
                            store(u - 1)
                        if u % GROUP == 1 and u > 1 and att[u - 1][0] >= FH:
                            store(u - 2)
                    store(len(att) - 1)

                @block.tensor
                def _(pe):
                    def scores(u):
                        h, i = att[u]
                        k = kq_slot(h)
                        if i == ORDER[0]:
                            loads = sum(2 if m < FH else 1 for m in range(k % 2, k + 1, 2))
                            pe.wait_ge(s_kq[k % 2], 16 * loads)
                        if u >= 2:
                            pe.wait_ge(s_exp if att[u - 2][0] < FH else s_msk, u - 1)
                        S = score_buf[u % 2]
                        if h < FH:
                            rows, keys = slice(0, AUG), kT[k % 2]
                        else:
                            r0 = HD * (h % 2)
                            rows, keys = slice(r0, r0 + HD), skT[:, (h - FH) // (SH // KVH), :]
                        q = qT[k % 2][rows, i * P:(i + 1) * P]
                        runs = []
                        at = 0
                        for c, n, _ in key_blocks(h, i):
                            if runs and runs[-1][0] + runs[-1][2] == c and at % NC and n == P:
                                runs[-1][2] += n
                            else:
                                runs.append([c, at, n])
                            at += n
                        for c, at, n in runs:
                            ins = pe.matmul(S[:, at:at + n], q, keys[rows, c:c + n], start=True, stop=True)
                        ins.then_inc(s_S, 1)

                    def value_product(j, m):
                        u, blocks = att_jobs[j]
                        h, i = att[u]
                        if m == 0:
                            if u % GROUP == 0 and u and j == jobs_of[u][0]:
                                pe.wait_ge(s_O, u // GROUP)
                            job_done(pe, j)
                        v0 = h * HD if h < FH else FW + HD * ((h - FH) // (SH // KVH))
                        rows = slice(HD * (h % 2), HD * (h % 2) + HD)
                        at = (groups[0] if i in groups[0] else groups[1]).index(i)
                        b, (c, n, tile) = blocks[m]
                        ins = pe.matmul(bank(7)[rows, at * P:(at + 1) * P], V[0:n, tile, v0:v0 + HD],
                                        probsT[j % PT_RING][0:n, m, :], start=(b == 0),
                                        stop=(b == len(key_blocks(h, i)) - 1))
                        if m == len(blocks) - 1:
                            ins.then_inc(s_pv, 1)

                    pe.wait_ge(s_kv, 16 * 5)
                    scores(0)
                    scores(1)
                    for u in range(len(att)):
                        if u + 2 < len(att):
                            scores(u + 2)
                        pe.wait_ge(s_norm, u + 1)
                        for j in jobs_of[u]:
                            if j >= 2:
                                job_done(pe, j - 2)
                            blocks, products = att_jobs[j][1], len(att_jobs[j - 2][1]) if j >= 2 else 0
                            for m in range(max(len(blocks), products)):
                                if m < len(blocks):
                                    b, (c, n, tile) = blocks[m]
                                    ins = pe.transpose(bank(5 + j % 2)[0:n, m * P:(m + 1) * P],
                                                       probs[u % 2][:, b * P:b * P + n], ident)
                                    if m == len(blocks) - 1:
                                        ins.then_inc(s_pt, 1)
                                if m < products:
                                    value_product(j - 2, m)
                    for j in range(len(att_jobs) - 2, len(att_jobs)):
                        for m in range(len(att_jobs[j][1])):
                            value_product(j, m)

        s_g = [sem(f"s_g{i}") for i in range(4)]
        s_T = sem("s_T")
        s_T_act = sem("s_T_act")
        s_T_dve = sem("s_T_dve")
        s_mm3 = sem("s_mm3")
        s_o3 = sem("s_o3")
        s_mix = sem("s_mix")
        s_out_res = sem("s_out_res")
        ounits = []
        for kind, half, (n0, ns, w) in outs:
            for t in range(TT):
                ounits.append((kind, half, t, n0))
        N_MIX = 4 * TT

        with ExitStack() as st:
            T_hi = sb(st, "T_hi", [P, KT, T], f32r)
            T_lo = sb(st, "T_lo", [P, KT, T], f32r)
            side = [sb(st, f"side{i}", [P, NC]) for i in range(4)]


            with nc.Block() as block:
                @block.sync
                def _(sp):
                    for n in range(N_PROJ + RING, N0):
                        load_sub(sp, n)
                    for m in range(RING):
                        load_expert_sub(sp, N0 + m, 0, m)
                    for t in range(TT):
                        sp.wait_ge(s_o3, N_MIX + TT + t + 1)
                        sp.dma_start(out2[t * P:(t + 1) * P, :], token_major[:, t, :]).then_inc(s_out_res, 16)

                @block.gpsimd
                def _(pool):
                    for u, (kind, half, t, n0) in enumerate(ounits):
                        if u >= 4:
                            pool.wait_ge(s_o3, u - 3)
                        c = half * NC + (D if kind == "swa" else 0)
                        src = x2[t * P:(t + 1) * P, half * NC:(half + 1) * NC] if kind == "res" \
                            else gate_d[:, t, c:c + NC]
                        pool.dma_start(side[u % 4][:, :], src).then_inc(s_g[u % 4], 16)
                        if t == 2:
                            k = u // TT
                            for n in splits_after[k]:
                                split_lo_pool(pool, n)

                @block.scalar
                def _(act):
                    for k in range(KT):
                        act.activation(T_hi[:, k, :], token_major[:, k, :], ACT.Copy).then_inc(s_T_act, 1)
                    for k in range(4):
                        for n in splits_after[k]:
                            split_hi(act, n)
                    act.wait_ge(s_mm3, N_MIX)
                    for j in range(2 * TT):
                        t, g = j // 2, j % 2
                        act.wait_ge(s_T, j + 1)
                        act.activation(T_hi[:, g * 4:g * 4 + 4, t * P:(t + 1) * P],
                                       bank(4 + j % 2).rearrange("p (k n) -> p k n", k=4), ACT.Copy).then_inc(s_T_act, 1)
                    for k in range(4, 6):
                        for n in splits_after[k]:
                            split_hi(act, n)

                @block.vector
                def _(dve):
                    def take_mix():
                        for j in range(2 * TT):
                            t, g = j // 2, j % 2
                            dve.wait_ge(s_T_act, KT + j + 1)
                            dve.tensor_tensor(T_lo[:, g * 4:g * 4 + 4, t * P:(t + 1) * P],
                                              bank(4 + j % 2).rearrange("p (k n) -> p k n", k=4),
                                              T_hi[:, g * 4:g * 4 + 4, t * P:(t + 1) * P].bitcast(f32),
                                              ALU.subtract).then_inc(s_T_dve, 1)

                    for k in range(KT):
                        dve.wait_ge(s_T_act, k + 1)
                        dve.tensor_tensor(T_lo[:, k, :], token_major[:, k, :], T_hi[:, k, :].bitcast(f32),
                                          ALU.subtract).then_inc(s_T_dve, 1)
                    for u, (kind, half, t, n0) in enumerate(ounits):
                        if u == N_MIX:
                            take_mix()
                        if t == 2:
                            for n in splits_after[u // TT]:
                                split_lo(dve, n)
                        dve.wait_ge(s_mm3, u + 1)
                        dve.wait_ge(s_g[u % 4], 16 * (u // 4 + 1))
                        dst = token_major[:, t, half * NC:(half + 1) * NC]
                        if kind == "fox":
                            if half == 0 and t == 0:
                                dve.wait_ge(s_T_dve, KT)
                            dve.tensor_tensor(dst, bank(u % 4), side[u % 4][:, :], ALU.mult).then_inc(s_o3, 1)
                        elif kind == "swa":
                            dve.tensor_tensor(side[u % 4][:, :], bank(u % 4), side[u % 4][:, :], ALU.mult).then_inc(s_mix, 1)
                            dve.wait_ge(s_mix, 2 * (half * TT + t) + 1)
                            dve.tensor_tensor(dst, dst, side[u % 4][:, :], ALU.add).then_inc(s_mix, 1)
                            dve.wait_ge(s_mix, 2 * (half * TT + t) + 2)
                            dve.sem_inc(s_o3, 1)
                        else:
                            dve.tensor_tensor(dst, bank(u % 4), side[u % 4][:, :], ALU.add).then_inc(s_o3, 1)

                @block.tensor
                def _(pe):
                    def transposes(t):
                        for g in range(2):
                            j = 2 * t + g
                            if j >= 2:
                                pe.wait_ge(s_T_act, KT + j - 1)
                                pe.wait_ge(s_T_dve, KT + j - 1)
                            for k in range(4):
                                c = (g * 4 + k) * P
                                ins = pe.transpose(bank(4 + j % 2)[:, k * P:(k + 1) * P],
                                                   token_major[:, t, c:c + P], ident)
                            ins.then_inc(s_T, 1)

                    for u, (kind, half, t, n0) in enumerate(ounits):
                        if u == N_MIX:
                            pe.wait_ge(s_o3, N_MIX)
                            for i in range(TT):
                                transposes(i)
                        nk = KT if kind == "res" else FW // P
                        k0 = FW // P if kind == "swa" else 0
                        if t == 0:
                            pe.wait_ge(s_lo, n0 + nk // HK)
                            pe.wait_ge(s_lo_pool, n0 + nk // HK)
                            pe.wait_ge(s_T_dve, KT + 2 * TT if kind == "res" else k0 + nk)
                        if u >= 4:
                            pe.wait_ge(s_o3, u - 3)
                        for k in range(nk):
                            slot = (n0 + k // HK) % RING
                            xs = (slice(None), k0 + k, slice(t * P, (t + 1) * P))
                            ins = three_passes(pe, bank(u % 4), T_hi[xs], T_lo[xs], whi[slot][:, k % HK, :],
                                               wlo[slot][:, k % HK, :], k == 0, k == nk - 1)
                            if nk == KT and k == HK - 1 and t == TT - 1:
                                ins.then_inc(s_used, 1)
                        ins.then_inc(s_mm3, 1)
                        if t == TT - 1:
                            pe.wait_ge(s_mm3, u + 1)
                            pe.sem_inc(s_used, 1)

        s_c4 = sem("s_c4")
        s_h2w = sem("s_h2w")
        s_ss4 = sem("s_ss4")
        s_ms4 = sem("s_ms4")
        s_rt4 = sem("s_rt4")
        s_h4 = sem("s_h4")
        s_wr = sem("s_wr")
        s_lg = sem("s_lg")
        s_lgs = sem("s_lgs")
        s_rk = sem("s_rk")
        s_dve4 = sem("s_dve4")
        s_ex4 = sem("s_ex4")
        s_mask = sem("s_mask")
        s_cols = sem("s_cols")
        s_rows = sem("s_rows")
        with ExitStack() as st:
            g2 = sb(st, "g2", [P, D])
            wr = sb(st, "wr", [P, KT, E])
            wr_hi = sb(st, "wr_hi", [P, KT, E], f32r)
            wr_lo = sb(st, "wr_lo", [P, KT, E], f32r)
            br = sb(st, "br", [P, E])
            h2T_hi = [sb(st, f"h2T_hi{i}", [P, KT, P], f32r) for i in range(2)]
            h2T_lo = [sb(st, f"h2T_lo{i}", [P, KT, P], f32r) for i in range(2)]
            ss = sb(st, "ss4", [P, 4, TT])
            logits = sb(st, "logits", [P, TT, E])
            top = sb(st, "top", [P, TT, 8])
            top_idx = sb(st, "top_idx", [P, TT, 8], u32)
            top_f = sb(st, "top_f", [P, TT, 8])
            gate4 = sb(st, "gate4", [P, TT, TOPK])
            gsum = sb(st, "gsum", [P, 2, TT])
            mask = sb(st, "mask", [P, TT, E])
            gates = sb(st, "gates", [P, TT, E])
            eq = sb(st, "eq", [P, TT, E])
            rank = sb(st, "rank", [P, TT, E])
            other = sb(st, "other", [P, TT, E])
            count = sb(st, "count", [P, E])
            it = sb(st, "it", [P, 6, E])
            grid = sb(st, "grid", [P, E])
            cols = sb(st, "cols", [P, 6])

            with nc.Block() as block:
                @block.sync
                def _(sp):
                    sp.dma_start(g2[:, :], row(norm2_gain)).then_inc(s_c4, 16)
                    sp.dma_start(wr[:, :, :], wrt.rearrange("(k p) n -> p k n", p=P)).then_inc(s_c4, 16)
                    sp.dma_start(br[:, :], row(b_router)).then_inc(s_c4, 16)
                    for t in range(TT):
                        sp.wait_ge(s_h4, t + 1)
                        sp.dma_start(h2_d[t * P:(t + 1) * P, :], token_major[:, t, :]).then_inc(s_h2w, 16)
                    sp.wait_ge(s_h2w, 16 * TT)

                @block.gpsimd
                def _(pool):
                    for m in range(LEAD):
                        expert_lo_pool(pool, N0 + m, m)

                @block.scalar
                def _(act):
                    def norm_front(t):
                        if t >= 1:
                            act.wait_ge(s_ss4, t)
                        act.activation(psum[:, 6:8, :].rearrange("p b n -> p (b n)"), token_major[:, t, :], ACT.Square,
                                       accum_out=ss[:, 0, t:t + 1]).then_inc(s_ss4, 1)
                        act.wait_ge(s_ms4, t + 1)
                        act.activation(ss[:, 2, t:t + 1], ss[:, 1, t:t + 1], ACT.Sqrt).then_inc(s_rt4, 1)

                    act.wait_ge(s_c4, 16 * 3)
                    norm_front(0)
                    act.activation(wr_hi[:, :, :], wr[:, :, :], ACT.Copy).then_inc(s_wr, 1)
                    for t in range(TT):
                        if t + 1 < TT:
                            norm_front(t + 1)
                        for g in range(2):
                            j = 2 * TT + 2 * t + g
                            act.wait_ge(s_T, j + 1)
                            if t >= 2:
                                act.wait_ge(s_lg, t - 1)
                            act.activation(h2T_hi[t % 2][:, g * 4:g * 4 + 4, :],
                                           bank(4 + j % 2).rearrange("p (k n) -> p k n", k=4),
                                           ACT.Copy).then_inc(s_T_act, 1)
                    for m in range(LEAD):
                        expert_hi(act, N0 + m, m)
                    act.wait_ge(s_mask, 2)
                    act.activation(gate4[:, :, :], gate4[:, :, :], ACT.Exp).then_inc(s_ex4, 1)

                @block.vector
                def _(dve):
                    steps = [0]

                    def step(ins):
                        ins.then_inc(s_dve4, 1)
                        steps[0] += 1
                        dve.wait_ge(s_dve4, steps[0])

                    def norm_front(t):
                        dve.wait_ge(s_ss4, t + 1)
                        dve.tensor_scalar(ss[:, 1, t:t + 1], ss[:, 0, t:t + 1], 1.0 / D, EPS,
                                          ALU.mult, ALU.add).then_inc(s_ms4, 1)
                        dve.wait_ge(s_rt4, t + 1)
                        step(dve.reciprocal(ss[:, 3, t:t + 1], ss[:, 2, t:t + 1]))
                        if t == 0:
                            dve.wait_ge(s_out_res, 16 * TT)
                        dve.scalar_tensor_tensor(token_major[:, t, :], token_major[:, t, :], ss[:, 3, t:t + 1],
                                                 g2[:, :], ALU.mult, ALU.mult).then_inc(s_h4, 1)

                    dve.wait_ge(s_c4, 16 * 3)
                    norm_front(0)
                    dve.wait_ge(s_wr, 1)
                    dve.tensor_tensor(wr_lo[:, :, :], wr[:, :, :], wr_hi[:, :, :].bitcast(f32),
                                      ALU.subtract).then_inc(s_wr, 1)
                    def take_tile(t):
                        if t >= 2:
                            dve.wait_ge(s_lg, t - 1)
                        for g in range(2):
                            j = 2 * TT + 2 * t + g
                            dve.wait_ge(s_T_act, KT + j + 1)
                            dve.tensor_tensor(h2T_lo[t % 2][:, g * 4:g * 4 + 4, :],
                                              bank(4 + j % 2).rearrange("p (k n) -> p k n", k=4),
                                              h2T_hi[t % 2][:, g * 4:g * 4 + 4, :].bitcast(f32),
                                              ALU.subtract).then_inc(s_T_dve, 1)

                    def top_of_tile(t):
                        dve.wait_ge(s_lg, t + 1)
                        dve.tensor_tensor(logits[:, t, :], bank(t % 2)[:, 0:E], br[:, :], ALU.add).then_inc(s_lgs, 1)
                        dve.wait_ge(s_lgs, t + 1)
                        step(dve.max(top[:, t, :], logits[:, t, :]))
                        step(dve.max_index(top_idx[:, t, :], top[:, t, :], logits[:, t, :]))

                    for t in range(TT):
                        if t + 1 < TT:
                            norm_front(t + 1)
                        take_tile(t)
                        if t >= 1:
                            top_of_tile(t - 1)
                    top_of_tile(TT - 1)
                    for m in range(LEAD):
                        expert_lo(dve, N0 + m, m)
                    step(dve.tensor_copy(top_f[:, :, :], top_idx[:, :, :]))
                    step(dve.tensor_tensor(gate4[:, :, :], top[:, :, 0:TOPK],
                                           top[:, :, 0:1].to_broadcast([P, TT, TOPK]), ALU.subtract))
                    dve.sem_inc(s_mask, 1)
                    bE = [P, TT, E]
                    iota_b = iota_e.unsqueeze(1).to_broadcast(bE)
                    for k in range(TOPK):
                        idx_b = top_f[:, :, k:k + 1].to_broadcast(bE)
                        if k == 0:
                            step(dve.tensor_tensor(mask[:, :, :], iota_b, idx_b, ALU.is_equal))
                        else:
                            step(dve.tensor_tensor(eq[:, :, :], iota_b, idx_b, ALU.is_equal))
                            step(dve.tensor_tensor(mask[:, :, :], mask[:, :, :], eq[:, :, :], ALU.add))
                    dve.sem_inc(s_mask, 1)
                    dve.wait_ge(s_ex4, 1)
                    step(dve.tensor_reduce(gsum[:, 0, :], gate4[:, :, :], AX.X, ALU.add))
                    step(dve.reciprocal(gsum[:, 1, :], gsum[:, 0, :]))
                    step(dve.tensor_tensor(gate4[:, :, :], gate4[:, :, :],
                                           gsum[:, 1, :].unsqueeze(2).to_broadcast([P, TT, TOPK]), ALU.mult))
                    for k in range(TOPK):
                        step(dve.tensor_tensor(eq[:, :, :], iota_b, top_f[:, :, k:k + 1].to_broadcast(bE), ALU.is_equal))
                        dst = gates if k == 0 else eq
                        step(dve.tensor_tensor(dst[:, :, :], eq[:, :, :], gate4[:, :, k:k + 1].to_broadcast(bE), ALU.mult))
                        if k:
                            step(dve.tensor_tensor(gates[:, :, :], gates[:, :, :], eq[:, :, :], ALU.add))
                    dve.wait_ge(s_rk, 1)
                    step(dve.tensor_copy(rank[:, :, :], bank(2)[:, 0:TT * E].rearrange("p (t e) -> p t e", e=E)))
                    step(dve.tensor_copy(count[:, :], bank(3)[:, 0:E]))
                    step(dve.tensor_tensor(other[:, :, :], count[:, :].unsqueeze(1).to_broadcast(bE),
                                           tok_index.unsqueeze(2).to_broadcast(bE), ALU.add))
                    step(dve.tensor_tensor(other[:, :, :], other[:, :, :], rank[:, :, :], ALU.subtract))
                    step(dve.tensor_tensor(eq[:, :, :], rank[:, :, :], other[:, :, :], ALU.subtract))
                    step(dve.tensor_tensor(eq[:, :, :], eq[:, :, :], mask[:, :, :], ALU.mult))
                    step(dve.tensor_tensor(slot_of[:, :, :].rearrange("p e t -> p t e"), eq[:, :, :], other[:, :, :],
                                           ALU.add))
                    step(dve.tensor_copy(tok_gate[:, :, :, 1].rearrange("p e t -> p t e"), gates[:, :, :]))
                    step(dve.tensor_copy(tok_gate[:, :, :, 0].rearrange("p e t -> p t e"),
                                         tok_index.unsqueeze(2).to_broadcast(bE)))
                    cnt = count[:, :]
                    step(dve.tensor_scalar(it[:, 0, :], cnt, float(PAIR), 1.0, ALU.is_gt, ALU.add))
                    for k in range(2, T // PAIR):
                        step(dve.tensor_scalar(it[:, 1, :], cnt, float(k * PAIR), None, ALU.is_gt))
                        step(dve.tensor_tensor(it[:, 0, :], it[:, 0, :], it[:, 1, :], ALU.add))
                    step(dve.tensor_copy(it[:, 2, :], it[:, 0, :]))
                    a, b, d = 2, 3, 1
                    while d < E:
                        step(dve.tensor_copy(it[:, b, 0:d], it[:, a, 0:d]))
                        step(dve.tensor_tensor(it[:, b, d:E], it[:, a, d:E], it[:, a, 0:E - d], ALU.add))
                        a, b, d = b, a, 2 * d
                    item_j = tok_index[:, 0:1]
                    step(dve.tensor_scalar(grid[:, :], it[:, a, :], item_j, None, ALU.is_le))
                    step(dve.tensor_reduce(cols[:, 0:1], grid[:, :], AX.X, ALU.add))
                    step(dve.tensor_tensor(grid[:, :], grid[:, :], it[:, 0, :], ALU.mult))
                    step(dve.tensor_reduce(cols[:, 1:2], grid[:, :], AX.X, ALU.add))
                    step(dve.tensor_tensor(cols[:, 1:2], item_j, cols[:, 1:2], ALU.subtract))
                    step(dve.tensor_scalar(cols[:, 1:2], cols[:, 1:2], float(PAIR), float(T - PAIR), ALU.mult, ALU.min))
                    step(dve.tensor_scalar(grid[:, :], iota_e, cols[:, 0:1], None, ALU.is_equal))
                    step(dve.tensor_tensor(grid[:, :], grid[:, :], cnt, ALU.mult))
                    step(dve.tensor_reduce(cols[:, 2:3], grid[:, :], AX.X, ALU.add))
                    step(dve.tensor_tensor(cols[:, 2:3], cols[:, 2:3], cols[:, 1:2], ALU.subtract))
                    step(dve.tensor_scalar(cols[:, 3:4], cols[:, 2:3], float(P), None, ALU.is_gt))
                    step(dve.tensor_scalar(cols[:, 4:5], cols[:, 2:3], float(P + TAIL), None, ALU.is_gt))
                    step(dve.tensor_tensor(cols[:, 2:3], cols[:, 3:4], cols[:, 4:5], ALU.add))
                    step(dve.tensor_tensor(cols[:, 5:6], cols[:, 3:4], cols[:, 4:5], ALU.subtract))
                    step(dve.tensor_scalar(cols[:, 0:1], cols[:, 0:1], float(E - 1), None, ALU.min))
                    dve.sem_inc(s_cols, 1)
                    step(dve.tensor_copy(table[:, ITEMS, 0:1], it[0:1, a, E - 1:E]))
                    dve.wait_ge(s_rows, 1)
                    rows = bank(0)[0:1, 0:8 * NJ].rearrange("p (r j) -> p r j", j=NJ)
                    for part in (slice(0, ITEMS), slice(ITEMS + 1, 8)):
                        step(dve.tensor_copy(table[:, part, :], rows[:, part, :]))

                @block.tensor
                def _(pe):
                    def transposes(t):
                        pe.wait_ge(s_h4, t + 1)
                        for g in range(2):
                            j = 2 * TT + 2 * t + g
                            pe.wait_ge(s_T_act, KT + j - 1)
                            pe.wait_ge(s_T_dve, KT + j - 1)
                            for k in range(4):
                                c = (g * 4 + k) * P
                                ins = pe.transpose(bank(4 + j % 2)[:, k * P:(k + 1) * P],
                                                   token_major[:, t, c:c + P], ident)
                            ins.then_inc(s_T, 1)

                    transposes(0)
                    for t in range(TT):
                        if t + 1 < TT:
                            transposes(t + 1)
                        pe.wait_ge(s_T_dve, KT + 2 * TT + 2 * t + 2)
                        if t == 0:
                            pe.wait_ge(s_wr, 2)
                        if t >= 2:
                            pe.wait_ge(s_lgs, t - 1)
                        for k in range(KT):
                            ins = three_passes(pe, bank(t % 2)[:, 0:E], h2T_hi[t % 2][:, k, :], h2T_lo[t % 2][:, k, :],
                                               wr_hi[:, k, :], wr_lo[:, k, :], k == 0, k == KT - 1)
                        ins.then_inc(s_lg, 1)
                    pe.wait_ge(s_mask, 2)
                    for t in range(TT):
                        dst = bank(2)[:, t * E:(t + 1) * E]
                        for j in range(t):
                            pe.matmul(dst, ones, mask[:, j, :], start=(j == 0), stop=False)
                        pe.matmul(dst, tri_strict, mask[:, t, :], start=(t == 0), stop=True)
                    for j in range(TT):
                        ins = pe.matmul(bank(3)[:, 0:E], ones, mask[:, j, :], start=(j == 0), stop=(j == TT - 1))
                    ins.then_inc(s_rk, 1)
                    pe.wait_ge(s_cols, 1)
                    for r, c, rhs in ((EXPERT, 0, ident), (FIRST, 1, ident), (KIND, 2, ident), (ANY_BEFORE, 3, tri_strict),
                                      (FULL_BEFORE, 4, tri_strict), (TAILS_BEFORE, 5, tri_strict)):
                        pe.matmul(bank(0)[0:1, r * NJ:(r + 1) * NJ], cols[:, c:c + 1], rhs[:, 0:NJ], start=True, stop=True)
                    pe.matmul(bank(0)[0:1, LAST_KIND * NJ:LAST_KIND * NJ + 1], cols[:, 2:3], tri_strict[:, 0:1],
                              start=True, stop=True)
                    pe.matmul(bank(0)[0:1, LAST_KIND * NJ + 1:(LAST_KIND + 1) * NJ], cols[:, 2:3], ident[:, 0:NJ - 1],
                              start=True, stop=True).then_inc(s_rows, 1)

        rest.close()
        A, B = 0, 1
        FULL = 2
        START = 1
        m_usedB = sem("m_usedB")
        m_free = [sem("m_freeA"), sem("m_freeB")]
        m_sig = [sem("m_sigA"), sem("m_sigB")]
        m_glu = [sem("m_gluA"), sem("m_gluB")]
        m_act = [sem("m_actA"), sem("m_actB")]
        m_scat_tail = sem("m_scat_tail")
        m_scat = [sem("m_scatA"), sem("m_scatB")]
        m_gat = [sem("m_gatA"), sem("m_gatB")]
        m_sel = [sem("m_selA"), sem("m_selB")]
        m_perm = [sem("m_permA"), sem("m_permB")]
        m_next = [sem("m_nextA"), sem("m_nextB")]
        m_cur = [sem("m_curA"), sem("m_curB")]
        m_tr = [sem("m_trA"), sem("m_trB")]
        m_tr_act = [sem("m_tr_actA"), sem("m_tr_actB")]
        m_tr_dve = [sem("m_tr_dveA"), sem("m_tr_dveB")]
        m_bias_raw = sem("m_bias_raw")
        m_bias_hi = sem("m_bias_hi")
        m_bias_lo = sem("m_bias_lo")
        m_warm = sem("m_warm")
        m_pick = sem("m_pick")
        m_const = sem("m_const")
        m_pass = sem("m_pass")

        ACT0, ACT1, TOKENS = 0, 1, 2

        def job(j, q):
            return 4 * j + (2 + q)

        def job_bank(b, q):
            return bank(7 if b else 4 + q % 2).rearrange("p (k n) -> p k n", k=4)

        with ExitStack() as st:
            slots = sb(st, "slots", [P, T])
            biases = sb(st, "biases", [2 * E, 2 * FF + D], f32r)
            pick = sb(st, "pick", [2 * E, P], f32r)
            warm = sb(st, "warm", [P, 2])
            tokens = [sb(st, f"tokens{b}", [P, D]) for b in (A, B)]
            xT_hi = [sb(st, f"xT_hi{b}", [P, KT, P], f32r) for b in (A, B)]
            xT_lo = [sb(st, f"xT_lo{b}", [P, KT, P], f32r) for b in (A, B)]
            hid = [sb(st, f"hid{b}", [P, FF]) for b in (A, B)]
            hidT_hi = [sb(st, f"hidT_hi{b}", [P, KT, P], f32r) for b in (A, B)]
            hidT_lo = [sb(st, f"hidT_lo{b}", [P, KT, P], f32r) for b in (A, B)]
            gate_part = [sb(st, f"gate_part{b}", [P, NC]) for b in (A, B)]
            sigm = [sb(st, f"sigm{b}", [P, NC]) for b in (A, B)]
            up_part = [sb(st, f"up_part{b}", [P, NC]) for b in (A, B)]
            y = [sb(st, f"y{b}", [P, D]) for b in (A, B)]
            onehot = [sb(st, f"onehot{b}", [P, TT, P]) for b in (A, B)]
            idx_next = [sb(st, f"idx_next{b}", [P, 1], i32) for b in (A, B)]
            pair_next = [sb(st, f"pair_next{b}", [P, 2]) for b in (A, B)]
            part_cur = sb(st, "part_cur", [P, 2], i32)
            xT_tail = sb(st, "xT_tail", [P, KT, TAIL])
            hidT_tail = sb(st, "hidT_tail", [P, KT, TAIL])
            idx_cur = [sb(st, f"idx_cur{b}", [P, 1], i32) for b in (A, B)]
            gate_cur = [sb(st, f"gate_cur{b}", [P, 1]) for b in (A, B)]

            def of_item(eng, row, j):
                most = {EXPERT: E - 1, FIRST: T - PAIR, KIND: FULL, LAST_KIND: FULL}.get(row, MAX_ITEMS)
                return eng.value_load(table[0:1, row, bass.ds(j, 1)], min_val=0, max_val=most)

            def kind_of(eng, j):
                return of_item(eng, KIND, j)

            def expert_of(eng, j):
                return of_item(eng, EXPERT, j)

            def n_items(eng):
                return eng.value_load(table[0:1, ITEMS, 0:1], min_val=E, max_val=MAX_ITEMS)

            def wait_from_zero(eng, s, value):
                eng.sem_inc(m_pass, 1)
                with eng.If(value > 0):
                    eng.wait_ge(s, value)
                    eng.sem_inc(m_pass, 1)

            def bias_cols(chunk):
                c = (chunk % 2) * FF + (chunk // 2) * NC if chunk < 4 else 2 * FF + (chunk - 4) * NC
                return slice(c, c + NC)

            bias_raw = [(hid[A], 0), (hid[B], FF), (y[A], 2 * FF)]

            def if_B(eng, kind, full, tail, counted):
                with eng.If(kind > 1):
                    full()
                with eng.Else():
                    with eng.If(kind > 0):
                        tail()
                    if counted:
                        with eng.Else():
                            for s, n, before in counted:
                                if not (isinstance(before, int) and before == 0):
                                    eng.wait_ge(s, before)
                                eng.sem_inc(s, n)

            def waits_scattered(eng, full, tails):
                wait_from_zero(eng, m_scat[B], 16 * full)
                wait_from_zero(eng, m_scat_tail, 2 * 16 * tails)

            with nc.Block() as block:
                @block.sync
                def _(sp):
                    sp.dma_start(slots[:, :], c_slots).then_inc(m_const, 16)
                    for rows in (slice(0, E), slice(E, 2 * E)):
                        for src, dst in ((bup[:, 0:FF], hid[A]), (bup[:, FF:2 * FF], hid[B]), (bdn, y[A])):
                            sp.dma_start(dst[rows, :], src).then_inc(m_bias_raw, 16)
                    n = n_items(sp)
                    with sp.Fori(0, n) as j:
                        kind, e, e1 = kind_of(sp, j), expert_of(sp, j), expert_of(sp, j + 1)
                        for m in range(RING, SUBS + RING):
                            with sp.If(kind > 0):
                                sp.wait_ge(m_usedB, SUBS * j + m + 1)
                                sp.sem_inc(m_pass, 1)
                            load_expert_sub(sp, N0 + SUBS * j + m, e if m < SUBS else e1, m % SUBS)
                    sp.wait_ge(s_raw[slot(LEAD)], raw_ready(LEAD, n))
                    sp.sem_inc(m_const, 1)

                @block.gpsimd
                def _(pool):
                    def gather(b, q):
                        pool.indirect_dma_start(
                            out=tokens[b][:, :], out_offset=None, in_=h2_d,
                            in_offset=bass.IndirectOffsetOnAxis(ap=idx_next[b][:, 0:1], axis=0)).then_inc(m_gat[b], 16)

                    def gather_tail():
                        pool.indirect_dma_start(
                            out=tokens[B][0:TAIL, :], out_offset=None, in_=h2_d,
                            in_offset=bass.IndirectOffsetOnAxis(ap=idx_next[B][0:TAIL, 0:1], axis=0)).then_inc(m_gat[B], 16)

                    def scatter_add_tail():
                        for h in range(2):
                            pool.indirect_dma_start(
                                out=out2.rearrange("t (k n) -> (t k) n", n=P),
                                out_offset=bass.IndirectOffsetOnAxis(ap=part_cur[:, h:h + 1], axis=0),
                                in_=y[B][:, h * P:(h + 1) * P], in_offset=None, compute_op=ALU.add).then_inc(m_scat_tail, 16)

                    def scatter_add(b):
                        pool.indirect_dma_start(
                            out=out2, out_offset=bass.IndirectOffsetOnAxis(ap=idx_cur[b][:, 0:1], axis=0),
                            in_=y[b][:, :], in_offset=None, compute_op=ALU.add).then_inc(m_scat[b], 16)

                    def first(item):
                        pool.wait_ge(m_cur[A], 2 * item + 2 + START)
                        pool.wait_ge(m_free[A], 6 * item + 6 + 2)
                        pool.sem_inc(m_pass, 1)
                        scatter_add(A)

                    def second(item, scatter):
                        pool.wait_ge(m_scat[A], 16 * item + 16)
                        pool.wait_ge(m_cur[B], 2 * item + 2 + START)
                        pool.wait_ge(m_free[B], 6 * item + 6 + 2)
                        pool.sem_inc(m_pass, 1)
                        scatter()

                    def seconds(kind, item):
                        if_B(pool, kind, lambda: second(item, lambda: scatter_add(B)),
                             lambda: second(item, scatter_add_tail), [])

                    n = n_items(pool)
                    kind0 = kind_of(pool, 0)
                    pool.wait_ge(m_next[A], 2)
                    gather(A, 0)

                    def gather_B(q, start):
                        pool.wait_ge(m_next[B], 2 * q + 2)
                        if not isinstance(q, int):
                            pool.wait_ge(m_tr[B], job(q - 1, ACT0))
                            pool.sem_inc(m_pass, 1)
                        start()

                    def gathers_B(kind, q):
                        if_B(pool, kind, lambda: gather_B(q, lambda: gather(B, q)), lambda: gather_B(q, gather_tail), [])

                    gathers_B(kind0, 0)
                    with pool.Fori(0, n) as j:
                        for s in range(SUBS):
                            m = s + LEAD
                            expert_lo_pool(pool, N0 + SUBS * j + m, m % SUBS)
                            if s == 6:
                                pool.wait_ge(m_next[A], 2 * j + 4)
                                pool.wait_ge(m_tr[A], job(j, ACT0))
                                pool.sem_inc(m_pass, 1)
                                gather(A, j + 1)
                                gathers_B(kind_of(pool, j + 1), j + 1)
                            if s == 0:
                                with pool.If(j > 0):
                                    first(j - 1)
                            if s == 1:
                                seconds(of_item(pool, LAST_KIND, j), j - 1)
                    first(n - 1)
                    seconds(of_item(pool, LAST_KIND, n), n - 1)
                    pool.wait_ge(m_scat[A], 16 * n)
                    waits_scattered(pool, of_item(pool, FULL_BEFORE, n), of_item(pool, TAILS_BEFORE, n))
                    pool.sem_inc(m_pass, 1)

                @block.scalar
                def _(act):
                    def take(j, b, q, dst, half):
                        act.wait_ge(m_tr[b], job(j, q) + 1)
                        act.activation(dst[b][:, half * 4:half * 4 + 4, :], job_bank(b, q), ACT.Copy).then_inc(m_tr_act[b], 1)

                    def take_tail(j, q, dst, half):
                        act.wait_ge(m_tr[B], job(j, q) + 1)
                        act.activation(dst[:, half * 4:half * 4 + 4, :],
                                       bank(7)[:, 0:P].rearrange("p (k n) -> p k n", n=TAIL), ACT.Copy).then_inc(m_tr_act[B], 1)

                    def takes_B(kind, j, q, hi, tail, half):
                        if_B(act, kind, lambda: take(j, B, q, hi, half), lambda: take_tail(j, q, tail, half),
                             [(m_tr_act[B], 1, job(j, q))])

                    def sigmoid(b, j, half, width=NC):
                        act.wait_ge(m_free[b], 6 * j + 2 * half + 1 + 2)
                        act.wait_ge(m_glu[b], 2 * j + half + START)
                        act.activation(sigm[b][:, 0:width], gate_part[b][:, 0:width], ACT.Sigmoid,
                                       scale=ALPHA).then_inc(m_sig[b], 1)

                    for i, (src, c) in enumerate(bias_raw):
                        if i == 0:
                            act.wait_ge(m_bias_raw, 16 * 2 * len(bias_raw))
                        act.activation(biases[:, c:c + FF], src[0:2 * E, :], ACT.Copy).then_inc(m_bias_hi, 1)
                    for b in (A, B):
                        act.sem_inc(m_sig[b], START)
                    act.activation(warm[:, 0:2], ident[:, 0:2], ACT.Copy).then_inc(m_warm, 1)
                    act.wait_ge(m_warm, 1)
                    act.activation(warm[:, 0:1], warm[:, 0:1], ACT.Sigmoid)
                    n = n_items(act)
                    for half in range(2):
                        take(-1, A, TOKENS + half, xT_hi, half)
                        takes_B(kind_of(act, 0), -1, TOKENS + half, xT_hi, xT_tail, half)
                    with act.Fori(0, n) as j:
                        act.activation(warm[:, 1:2], warm[:, 1:2], ACT.Sigmoid)
                        for s in range(SUBS):
                            m = s + LEAD
                            act.wait_ge(m_usedB, SUBS * j + m + 1)
                            expert_hi(act, N0 + SUBS * j + m, m % SUBS, j + m // SUBS)
                            if s == 1:
                                kind = kind_of(act, j)
                            if s == 9:
                                kind1 = kind_of(act, j + 1)
                            if s in (2, 6):
                                h = s // 4
                                sigmoid(A, j, h)
                                if_B(act, kind, lambda: sigmoid(B, j, h), lambda: sigmoid(B, j, h, P), [(m_sig[B], 1, 2 * j + h + START)])
                            if s == 6:
                                take(j, A, ACT0, hidT_hi, 0)
                                takes_B(kind, j, ACT0, hidT_hi, hidT_tail, 0)
                            if s == 8:
                                take(j, A, ACT1, hidT_hi, 1)
                                takes_B(kind, j, ACT1, hidT_hi, hidT_tail, 1)
                            if s in (10, 11):
                                h = s - 10
                                take(j, A, TOKENS + h, xT_hi, h)
                                takes_B(kind1, j, TOKENS + h, xT_hi, xT_tail, h)

                @block.vector
                def _(dve):
                    def take(j, b, q, hi, lo, half):
                        dve.wait_ge(m_tr_act[b], job(j, q) + 1)
                        dve.tensor_tensor(lo[b][:, half * 4:half * 4 + 4, :], job_bank(b, q),
                                          hi[b][:, half * 4:half * 4 + 4, :].bitcast(f32),
                                          ALU.subtract).then_inc(m_tr_dve[b], 1)

                    def taken_tail(j, q):
                        dve.wait_ge(m_tr_act[B], job(j, q) + 1)
                        dve.sem_inc(m_tr_dve[B], 1)

                    def takes_B(kind, j, q, hi, lo, half):
                        if_B(dve, kind, lambda: take(j, B, q, hi, lo, half), lambda: taken_tail(j, q),
                             [(m_tr_dve[B], 1, job(j, q))])

                    def one_hot(b, e, first):
                        dve.tensor_tensor(onehot[b][:, :, :],
                                          slot_of[:, bass.ds(e, 1), :].rearrange("p o t -> p (o t)").unsqueeze(2)
                                          .to_broadcast([P, TT, P]),
                                          slots[:, bass.ds(first + b * P, P)].unsqueeze(1).to_broadcast([P, TT, P]),
                                          ALU.is_equal).then_inc(m_sel[b], 1)

                    def one_hot_tail(e, first):
                        for g in range(GROUPS):
                            ins = dve.tensor_tensor(
                                onehot[B][:, :, g * TAIL:(g + 1) * TAIL],
                                slot_of[:, bass.ds(e, 1), :].rearrange("p o t -> p (o t)").unsqueeze(2)
                                .to_broadcast([P, TT, TAIL]),
                                slots[:, bass.ds(first + P, TAIL)].unsqueeze(1).to_broadcast([P, TT, TAIL]),
                                ALU.is_equal)
                        ins.then_inc(m_sel[B], 1)

                    def one_hots_B(kind, q, e, first):
                        if_B(dve, kind, lambda: one_hot(B, e, first), lambda: one_hot_tail(e, first), [(m_sel[B], 1, q)])

                    def from_psum(b):
                        pair = bank(6)[:, 2 * b:2 * b + 2]
                        dve.tensor_copy(idx_next[b][:, :], pair[:, 0:1]).then_inc(m_next[b], 1)
                        dve.tensor_copy(pair_next[b][:, :], pair).then_inc(m_next[b], 1)

                    def to_current(b):
                        dve.tensor_copy(idx_cur[b][:, :], idx_next[b][:, :]).then_inc(m_cur[b], 1)
                        dve.tensor_copy(gate_cur[b][:, :], pair_next[b][:, 1:2]).then_inc(m_cur[b], 1)

                    def to_current_tail():
                        dve.scalar_tensor_tensor(part_cur[:, :], pair_next[B][:, 0:1].to_broadcast([P, 2]), float(D // P),
                                                 part_of, ALU.mult, ALU.add).then_inc(m_cur[B], 1)
                        dve.tensor_copy(gate_cur[B][:, :], pair_next[B][:, 1:2]).then_inc(m_cur[B], 1)

                    def chunk_done(b, j, s):
                        if b == A:
                            dve.wait_ge(s_used, N0 + SUBS * j + s + 1)
                        else:
                            dve.wait_ge(m_usedB, SUBS * j + s + 1 + RING)

                    def clamp_gate(b, j, s, half, width=NC):
                        chunk_done(b, j, s)
                        dve.wait_ge(m_act[b], 2 * j + half + START)
                        dve.tensor_scalar(gate_part[b][:, 0:width], bank(2 * b)[:, 0:width], LIMIT, None,
                                          ALU.min).then_inc(m_free[b], 1)

                    def glu(b, j, half, width=NC):
                        dve.wait_ge(m_sig[b], 2 * j + half + 1 + START)
                        dve.tensor_tensor(gate_part[b][:, 0:width], gate_part[b][:, 0:width], sigm[b][:, 0:width],
                                          ALU.mult).then_inc(m_glu[b], 1)

                    def up(b, j, s, half, width=NC):
                        chunk_done(b, j, s)
                        dve.tensor_scalar(up_part[b][:, 0:width], bank(2 * b + 1)[:, 0:width], LIMIT, -LIMIT,
                                          ALU.min, ALU.max).then_inc(m_free[b], 1)
                        dve.wait_ge(m_free[b], 6 * j + 2 * half + 2 + 2)
                        dve.wait_ge(m_glu[b], 2 * j + half + 1 + START)
                        dve.scalar_tensor_tensor(hid[b][:, half * width:(half + 1) * width], up_part[b][:, 0:width], 1.0,
                                                 gate_part[b][:, 0:width], ALU.add, ALU.mult).then_inc(m_act[b], 1)

                    def down(b, j, s, half, width=NC):
                        chunk_done(b, j, s)
                        dve.tensor_scalar(y[b][:, half * width:(half + 1) * width], bank(2 * b + half)[:, 0:width],
                                          gate_cur[b][:, 0:1], None, ALU.mult).then_inc(m_free[b], 1)

                    def pick_biases(e):
                        for g in range(2):
                            r = slice(g * E, (g + 1) * E)
                            dve.tensor_copy(pick[r, :], ident[r, bass.ds(e + g * E, 1)].to_broadcast([E, P])).then_inc(m_pick, 1)

                    for sems in (m_glu, m_act, m_cur):
                        for b in (A, B):
                            dve.sem_inc(sems[b], START)
                    n = n_items(dve)
                    for b in (A, B):
                        dve.sem_inc(m_free[b], 2)
                    dve.wait_ge(m_const, 16)
                    kind0 = kind_of(dve, 0)
                    one_hot(A, 0, 0)
                    one_hots_B(kind0, 0, 0, 0)
                    dve.wait_ge(m_perm[A], 1)
                    dve.wait_ge(m_perm[B], 1)
                    from_psum(A)
                    if_B(dve, kind0, lambda: from_psum(B), lambda: from_psum(B), [(m_next[B], 2, 0)])
                    dve.wait_ge(m_bias_hi, len(bias_raw))
                    for src, c in bias_raw:
                        dve.tensor_tensor(biases[E:2 * E, c:c + FF], src[E:2 * E, :],
                                          biases[E:2 * E, c:c + FF].bitcast(f32), ALU.subtract).then_inc(m_bias_lo, 1)
                    dve.wait_ge(m_bias_lo, len(bias_raw))
                    pick_biases(0)
                    for half in range(2):
                        take(-1, A, TOKENS + half, xT_hi, xT_lo, half)
                        takes_B(kind0, -1, TOKENS + half, xT_hi, xT_lo, half)
                    with dve.Fori(0, n) as j:
                        for s in range(SUBS):
                            m = s + LEAD
                            expert_lo(dve, N0 + SUBS * j + m, m % SUBS)
                            if s == 0:
                                kind, kind1 = kind_of(dve, j), kind_of(dve, j + 1)
                                e1, first1 = expert_of(dve, j + 1), of_item(dve, FIRST, j + 1)
                                full, tails = of_item(dve, FULL_BEFORE, j), of_item(dve, TAILS_BEFORE, j)
                                any1 = of_item(dve, ANY_BEFORE, j + 1)
                                dve.wait_ge(m_perm[A], j + 1)
                                dve.wait_ge(m_perm[B], j + 1)
                                one_hot(A, e1, first1)
                                one_hots_B(kind1, j + 1, e1, first1)
                            if s in (1, 5):
                                h = s // 4
                                clamp_gate(A, j, s, h)
                                if_B(dve, kind, lambda: clamp_gate(B, j, s, h), lambda: clamp_gate(B, j, s, h, P), [(m_free[B], 1, 6 * j + 2 * h + 2)])
                            if s in (2, 6):
                                h = s // 4
                                glu(A, j, h)
                                if_B(dve, kind, lambda: glu(B, j, h), lambda: glu(B, j, h, P), [(m_glu[B], 1, 2 * j + h + START)])
                            if s in (3, 7):
                                h = s // 4
                                up(A, j, s, h)
                                if_B(dve, kind, lambda: up(B, j, s, h), lambda: up(B, j, s, h, P),
                                     [(m_free[B], 1, 6 * j + 2 * h + 3),
                                      (m_act[B], 1, 2 * j + h + START)])
                            if s == 3:
                                dve.wait_ge(m_next[A], 2 * j + 2)
                                dve.wait_ge(m_next[B], 2 * j + 2)
                                wait_from_zero(dve, m_scat[A], 16 * j)
                                waits_scattered(dve, full, tails)
                                to_current(A)
                                if_B(dve, kind, lambda: to_current(B), to_current_tail, [(m_cur[B], 2, 2 * j + START)])
                            if s == 5:
                                dve.wait_ge(m_perm[A], j + 2)
                                dve.wait_ge(m_perm[B], j + 2)
                                dve.wait_ge(m_cur[A], 2 * j + 2 + START)
                                dve.wait_ge(m_cur[B], 2 * j + 2 + START)
                                dve.wait_ge(m_gat[A], 16 * j + 16)
                                wait_from_zero(dve, m_gat[B], 16 * any1)
                                from_psum(A)
                                if_B(dve, kind1, lambda: from_psum(B), lambda: from_psum(B), [(m_next[B], 2, 2 * j + 2)])
                            if s == 6:
                                take(j, A, ACT0, hidT_hi, hidT_lo, 0)
                                takes_B(kind, j, ACT0, hidT_hi, hidT_lo, 0)
                            if s == 8:
                                take(j, A, ACT1, hidT_hi, hidT_lo, 1)
                                takes_B(kind, j, ACT1, hidT_hi, hidT_lo, 1)
                            if s in (10, 11):
                                h = s - 10
                                take(j, A, TOKENS + h, xT_hi, xT_lo, h)
                                takes_B(kind1, j, TOKENS + h, xT_hi, xT_lo, h)
                                down(A, j, s, h)
                                if_B(dve, kind, lambda: down(B, j, s, h), lambda: down(B, j, s, h, P),
                                     [(m_free[B], 1, 6 * j + 4 + h + 2)])
                                if s == 10:
                                    dve.wait_ge(s_used, N0 + SUBS * j + s + 1)
                                    pick_biases(e1)

                @block.tensor
                def _(pe):
                    def job_bank_free(j, b, q):
                        free = job(j, q) - (0 if b else 1)
                        if not (isinstance(free, int) and free <= 0):
                            pe.wait_ge(m_tr_act[b], free)
                            pe.wait_ge(m_tr_dve[b], free)

                    def transposes(j, b, q, src, half):
                        job_bank_free(j, b, q)
                        for i in range(4):
                            c = (half * 4 + i) * P
                            ins = pe.transpose(job_bank(b, q)[:, i, :], src[b][:, c:c + P], ident)
                        ins.then_inc(m_tr[b], 1)

                    def token_job(j, b, half, q16):
                        pe.wait_ge(m_gat[b], q16)
                        transposes(j, b, TOKENS + half, tokens, half)

                    def tail_token_job(j, half, q16):
                        pe.wait_ge(m_gat[B], q16)
                        job_bank_free(j, B, TOKENS + half)
                        pe.sem_inc(m_pass, 1)
                        for i in range(4):
                            c = (half * 4 + i) * P
                            ins = pe.transpose(bank(7)[:, i * TAIL:(i + 1) * TAIL], tokens[B][0:TAIL, c:c + P],
                                               ident[0:TAIL, 0:TAIL])
                        ins.then_inc(m_tr[B], 1)

                    def token_jobs_B(kind, j, half, q16):
                        if_B(pe, kind, lambda: token_job(j, B, half, q16), lambda: tail_token_job(j, half, q16),
                             [(m_tr[B], 1, job(j, TOKENS + half))])

                    def hidden_job(j, b, half):
                        pe.wait_ge(m_act[b], 2 * j + half + 1 + START)
                        transposes(j, b, ACT1 if half else ACT0, hid, half)

                    def tail_hidden_job(j, half):
                        q = ACT1 if half else ACT0
                        pe.wait_ge(m_act[B], 2 * j + half + 1 + START)
                        job_bank_free(j, B, q)
                        pe.transpose(bank(7)[:, 0:P], hid[B][:, half * P:(half + 1) * P], ident).then_inc(m_tr[B], 1)

                    def hidden_jobs_B(kind, j, half):
                        if_B(pe, kind, lambda: hidden_job(j, B, half), lambda: tail_hidden_job(j, half),
                             [(m_tr[B], 1, job(j, ACT1 if half else ACT0))])

                    def permutation(b, e, q2, half):
                        if half == 0:
                            pe.wait_ge(m_sel[b], q2)
                        for t in range(half * TT // 2, (half + 1) * TT // 2):
                            ins = pe.matmul(bank(6)[:, 2 * b:2 * b + 2], onehot[b][:, t, :],
                                            tok_gate[:, bass.ds(e, 1), t, :].rearrange("p o c -> p (o c)"),
                                            start=(t == 0), stop=(t == TT - 1))
                        if half == 1:
                            ins.then_inc(m_perm[b], 1)

                    def permutation_B(kind, e, q, half):
                        work = lambda: permutation(B, e, q + 1, half)
                        if_B(pe, kind, work, work, [(m_perm[B], 1, q)] if half == 1 else [])

                    def sub_tile_ready(b, j, s):
                        chunk, half = CHUNK_HALF[s]
                        if s == 0:
                            pe.wait_ge(m_tr_dve[b], 4 * j + 1)
                        if s == 1:
                            pe.wait_ge(m_tr_dve[b], 4 * j + 2)
                        if s == 8:
                            pe.wait_ge(m_tr_dve[b], job(j, ACT0) + 1)
                        if s == 10:
                            pe.wait_ge(m_tr_dve[b], job(j, ACT1) + 1)
                        if half == 0:
                            pe.wait_ge(m_free[b], 6 * j + chunk + 1)

                    def sub_tile(b, j, s):
                        sub_tile_ready(b, j, s)
                        chunk, half = CHUNK_HALF[s]
                        dst = bank(2 * b + chunk % 2)
                        x_hi, x_lo = (xT_hi, xT_lo) if chunk < 4 else (hidT_hi, hidT_lo)
                        if half == 0:
                            pe.matmul(dst, pick[:, :], biases[:, bias_cols(chunk)], start=True, stop=False)
                        for k in range(HK):
                            kk = half * HK + k
                            ins = three_passes(pe, dst, x_hi[b][:, kk, :], x_lo[b][:, kk, :],
                                               whi[slot(s)][:, k, :], wlo[slot(s)][:, k, :], False, kk == KT - 1)
                        ins.then_inc(s_used if b == A else m_usedB, 1)

                    def tail_sub_tile(j, s):
                        sub_tile_ready(B, j, s)
                        pe.sem_inc(m_pass, 1)
                        chunk, half = CHUNK_HALF[s]
                        src = xT_tail if chunk < 4 else hidT_tail
                        dst = [bank(2 * B + chunk % 2)[g * TAIL:(g + 1) * TAIL, 0:P] for g in range(GROUPS)]
                        if half == 0:
                            for g in range(GROUPS):
                                c = bias_cols(chunk).start + g * P
                                pe.matmul(dst[g], pick[:, 0:TAIL].bitcast(f32), biases[:, c:c + P].bitcast(f32),
                                          start=True, stop=False)
                        for k in range(HK):
                            kk = half * HK + k
                            for g in range(GROUPS):
                                ins = pe.matmul(dst[g], src[:, kk, :], raw[slot(s)][:, k, g * P:(g + 1) * P],
                                                start=False, stop=kk == KT - 1)
                        ins.then_inc(m_usedB, 1)

                    n = n_items(pe)
                    pe.sem_inc(m_usedB, RING)
                    kind0 = kind_of(pe, 0)
                    for half in range(2):
                        permutation(A, 0, 1, half)
                    for half in range(2):
                        permutation_B(kind0, 0, 0, half)
                    for half in range(2):
                        token_job(-1, A, half, 16)
                        token_jobs_B(kind0, -1, half, 16)
                    pe.wait_ge(m_bias_hi, len(bias_raw))
                    pe.wait_ge(m_bias_lo, len(bias_raw))
                    with pe.Fori(0, n) as j:
                        kind = kind_of(pe, j)
                        pe.wait_ge(m_pick, 2 * j + 2)
                        for s in range(SUBS):
                            pe.wait_ge(s_lo, N0 + SUBS * j + s + 1)
                            pe.wait_ge(s_lo_pool, N0 + SUBS * j + s + 1)
                            if_B(pe, kind, lambda: sub_tile(B, j, s), lambda: tail_sub_tile(j, s), [(m_usedB, 1, SUBS * j + s + RING)])
                            sub_tile(A, j, s)
                            if s == 2:
                                e1, kind1, any1 = expert_of(pe, j + 1), kind_of(pe, j + 1), of_item(pe, ANY_BEFORE, j + 1)
                                pe.wait_ge(m_next[A], 2 * j + 2)
                                pe.wait_ge(m_next[B], 2 * j + 2)
                            if s in (2, 3):
                                permutation(A, e1, j + 2, s - 2)
                            if s in (3, 4):
                                permutation_B(kind1, e1, j + 1, s - 3)
                            if s == 5:
                                hidden_job(j, A, 0)
                                hidden_jobs_B(kind, j, 0)
                            if s == 8:
                                hidden_job(j, A, 1)
                                hidden_jobs_B(kind, j, 1)
                            if s in (9, 10):
                                token_job(j, A, s - 9, 16 * j + 32)
                                token_jobs_B(kind1, j, s - 9, 16 * any1 + 16)


_INS = ["x", "meta_tokens", "norm1_gain", "w_in", "b_forget", "fox_q_gain", "fox_k_gain", "swa_q_gain",
        "swa_k_gain", "swa_sinks", "w_fox_out", "w_swa_out", "w_out", "norm2_gain", "w_router", "b_router",
        "w_up", "b_up", "w_down", "b_down"]
_OUT = (1, T, D)


def kernel(**inputs):
    import concourse.bacc as bacc
    from concourse.bass_utils import run_bass_kernel_spmd

    nc = bacc.Bacc("TRN2", target_bir_lowering=False, num_devices=1)
    arrays, args = {}, []
    named = [(name, np.ascontiguousarray(inputs[name])) for name in _INS]
    named += [(f"const{i}", c) for i, c in enumerate(constants())]
    for name, a in named:
        arrays[f"{name}_dram"] = a
        args.append(nc.dram_tensor(f"{name}_dram", a.shape, mybir.dt.from_np(a.dtype), kind="ExternalInput").ap())
    result = nc.dram_tensor("out_dram", _OUT, mybir.dt.float32, kind="ExternalOutput").ap()
    block_kernel(nc, *args, result)
    r = run_bass_kernel_spmd(nc, [arrays], core_ids=[0])
    return r.results[0]["out_dram"]
```
